# Optimizing a Trainium2 kernel written in Bass

```python
import jax, jax.numpy as jnp
from jax import lax
import numpy as np

D_MODEL = 1024
BATCH = 1
SEQ = 256
DEPTH = 1
DEC_BATCH = 1
DEC_SEQ = 1024
PAST_LEN = 256

GRID_W = 64
EPS = 1e-6
D_FOURIER = 256
N_FOURIER_GROUPS = 4
D_FOURIER_GROUP = D_FOURIER // N_FOURIER_GROUPS
D_CONV = 256
CONV_WIDTH = 31
D_MLSTM = 512
N_HEADS_M = 4
HEAD_DIM_M = D_MLSTM // N_HEADS_M
N_DIRS = 2
CHUNK = 128
N_GATES = 2 * N_DIRS * N_HEADS_M
D_MIX = D_FOURIER + D_CONV + D_MLSTM
D_IN_PROJ = D_FOURIER + 2 * D_CONV + 4 * D_MLSTM + N_GATES
N_EXPERTS = 16
N_EXPERT_GROUPS = 4
EXPERTS_PER_GROUP = N_EXPERTS // N_EXPERT_GROUPS
TOP_K = 2
D_EXPERT = 256
N_MOD = 6

kernel_name = 'hybrid_fnet_conformer_mlstm_moe_diffusion_step'

def rmsnorm(x, g):
    xf = x.astype(jnp.float32)
    y = xf * lax.rsqrt(jnp.mean(xf * xf, axis=-1, keepdims=True) + EPS)
    return (y * g.astype(jnp.float32)).astype(x.dtype)

def grid_pos_embed(n_tokens, dtype):
    rows = n_tokens // GRID_W
    r = jnp.repeat(jnp.arange(rows, dtype=jnp.float32), GRID_W)
    col = jnp.tile(jnp.arange(GRID_W, dtype=jnp.float32), rows)
    quarter = D_MODEL // 4
    omega = 1.0 / (10000.0 ** (jnp.arange(quarter, dtype=jnp.float32) / quarter))
    def enc(p):
        a = p[:, None] * omega[None, :]
        return jnp.concatenate([jnp.sin(a), jnp.cos(a)], axis=-1)
    return jnp.concatenate([enc(r), enc(col)], axis=-1).astype(dtype)

def fourier_mix(xa, w_fnet):
    B, T, _ = xa.shape
    xf = xa.astype(jnp.float32).reshape(B, T, N_FOURIER_GROUPS, D_FOURIER_GROUP)
    y = jnp.fft.fft2(xf, axes=(1, 3), norm='ortho').real.reshape(B, T, D_FOURIER)
    return y.astype(xa.dtype) @ w_fnet

def conv_mix(xb, w_dw, b_dw, ln_g, ln_b, w_pw):
    a, gt = jnp.split(xb, 2, axis=-1)
    u = a * jax.nn.sigmoid(gt)
    pad = CONV_WIDTH // 2
    u = lax.conv_general_dilated(u, w_dw[:, None, :], window_strides=(1,), padding=((pad, pad),),
                                 dimension_numbers=('NWC', 'WIO', 'NWC'),
                                 feature_group_count=D_CONV) + b_dw
    uf = u.astype(jnp.float32)
    mu = jnp.mean(uf, axis=-1, keepdims=True)
    var = jnp.mean(jnp.square(uf - mu), axis=-1, keepdims=True)
    uf = (uf - mu) * lax.rsqrt(var + EPS) * ln_g.astype(jnp.float32) + ln_b.astype(jnp.float32)
    return jax.nn.silu(uf).astype(xb.dtype) @ w_pw

def mlstm_chunk_scan(q, k, v, li, lf, C0, n0, m0):
    B, H, T, d = q.shape
    nc = T // CHUNK
    def to_chunks(z):
        z = z.reshape((B, H, nc, CHUNK) + z.shape[3:])
        return jnp.moveaxis(z, 2, 0)
    causal = jnp.tril(jnp.ones((CHUNK, CHUNK), dtype=bool))
    def body(carry, inp):
        C, n, m = carry
        qc, kc, vc, ic, fc = inp
        b = jnp.cumsum(fc, axis=-1)
        d_log = b[..., :, None] - b[..., None, :] + ic[..., None, :]
        d_log = jnp.where(causal, d_log, -jnp.inf)
        inter_log = b + m[..., None]
        m_t = jnp.maximum(inter_log, jnp.max(d_log, axis=-1))
        dmat = jnp.exp(d_log - m_t[..., None])
        inter = jnp.exp(inter_log - m_t)
        s = jnp.einsum('bhtd,bhsd->bhts', qc, kc) * dmat
        num = inter[..., None] * jnp.einsum('bhtd,bhde->bhte', qc, C) + jnp.einsum('bhts,bhse->bhte', s, vc)
        den = inter * jnp.einsum('bhtd,bhd->bht', qc, n) + jnp.sum(s, axis=-1)
        h = num / jnp.maximum(jnp.abs(den), jnp.exp(-m_t))[..., None]
        m_new = m_t[..., -1]
        w = jnp.exp(b[..., -1:] - b + ic - m_new[..., None])
        decay = jnp.exp(b[..., -1] + m - m_new)
        kw = kc * w[..., None]
        C_new = decay[..., None, None] * C + jnp.einsum('bhsd,bhse->bhde', kw, vc)
        n_new = decay[..., None] * n + jnp.sum(kw, axis=2)
        return (C_new, n_new, m_new), h
    (C, n, m), hs = lax.scan(body, (C0, n0, m0),
                             (to_chunks(q), to_chunks(k), to_chunks(v), to_chunks(li), to_chunks(lf)))
    h = jnp.moveaxis(hs, 0, 2).reshape(B, H, T, d)
    return h, C, n, m

def mlstm_mix(xc, b_gate, g_mh, C0, n0, m0):
    B, T, _ = xc.shape
    xf = xc.astype(jnp.float32)
    q, k, v, o, g = jnp.split(xf, [D_MLSTM, 2 * D_MLSTM, 3 * D_MLSTM, 4 * D_MLSTM], axis=-1)
    def heads(z):
        return z.reshape(B, T, N_HEADS_M, HEAD_DIM_M).transpose(0, 2, 1, 3)
    q, k, v = heads(q), heads(k) * (HEAD_DIM_M ** -0.5), heads(v)
    g = (g + b_gate.astype(jnp.float32)).reshape(B, T, N_DIRS, 2, N_HEADS_M).transpose(2, 3, 0, 4, 1)
    li = g[:, 0]
    lf = jax.nn.log_sigmoid(g[:, 1])
    h_f, Cf, nf, mf = mlstm_chunk_scan(q, k, v, li[0], lf[0], C0[:, 0], n0[:, 0], m0[:, 0])
    def flip(z):
        return jnp.flip(z, axis=2)
    h_b, Cb, nb, mb = mlstm_chunk_scan(flip(q), flip(k), flip(v), flip(li[1]), flip(lf[1]),
                                       C0[:, 1], n0[:, 1], m0[:, 1])
    h = h_f + flip(h_b)
    h = h * lax.rsqrt(jnp.mean(h * h, axis=-1, keepdims=True) + EPS) * g_mh.astype(jnp.float32).reshape(N_HEADS_M, 1, HEAD_DIM_M)
    h = h.transpose(0, 2, 1, 3).reshape(B, T, D_MLSTM) * jax.nn.sigmoid(o)
    C_out = jnp.stack([Cf, Cb], axis=1)
    n_out = jnp.stack([nf, nb], axis=1)
    m_out = jnp.stack([mf, mb], axis=1)
    return h.astype(xc.dtype), C_out, n_out, m_out

def moe(h, w_router, b_router, w_eg, w_eu, w_ed):
    B, T, _ = h.shape
    logits = jnp.einsum('btd,de->bte', h.astype(jnp.float32), w_router.astype(jnp.float32))
    scores = jax.nn.sigmoid(logits)
    sel = scores + b_router.astype(jnp.float32)
    grp = sel.reshape(B, T, N_EXPERT_GROUPS, EXPERTS_PER_GROUP)
    grp_score = jnp.sum(lax.top_k(grp, TOP_K)[0], axis=-1)
    best = jnp.argmax(grp_score, axis=-1)
    in_grp = best[..., None] == (jnp.arange(N_EXPERTS) // EXPERTS_PER_GROUP)
    masked = jnp.where(in_grp, sel, -jnp.inf)
    _, idx = lax.top_k(masked, TOP_K)
    w_sel = jnp.take_along_axis(scores, idx, axis=-1)
    w_sel = w_sel / jnp.sum(w_sel, axis=-1, keepdims=True)
    combine = jnp.sum(jax.nn.one_hot(idx, N_EXPERTS, dtype=jnp.float32) * w_sel[..., None], axis=-2)
    gate = jnp.einsum('btd,edf->btef', h, w_eg)
    up = jnp.einsum('btd,edf->btef', h, w_eu)
    a = jax.nn.silu(gate) * up * combine.astype(h.dtype)[..., None]
    return jnp.einsum('btef,efd->btd', a, w_ed)

def trunk_layer(x, cvec, C0, n0, m0, lp):
    (w_ada, b_ada, g1, g2, w_in, w_fnet, w_dw, b_dw, ln_g, ln_b, w_pw,
     b_gate, g_mh, w_out, w_router, b_router, w_eg, w_eu, w_ed) = lp
    mod = (jax.nn.silu(cvec) @ w_ada + b_ada)[..., None, :]
    sh1, sc1, ga1, sh2, sc2, ga2 = jnp.split(mod, N_MOD, axis=-1)
    h = rmsnorm(x, g1) * (1.0 + sc1) + sh1
    p = h @ w_in
    xa, xb, xc = jnp.split(p, [D_FOURIER, D_FOURIER + 2 * D_CONV], axis=-1)
    out_c, C_out, n_out, m_out = mlstm_mix(xc, b_gate, g_mh, C0, n0, m0)
    mix = jnp.concatenate([fourier_mix(xa, w_fnet), conv_mix(xb, w_dw, b_dw, ln_g, ln_b, w_pw), out_c], axis=-1)
    x = x + ga1 * (mix @ w_out)
    h = rmsnorm(x, g2) * (1.0 + sc2) + sh2
    x = x + ga2 * moe(h, w_router, b_router, w_eg, w_eu, w_ed)
    return x, C_out, n_out, m_out

def setup_inputs(seed: int = 0) -> dict:
    key = jax.random.key(seed)
    ks = jax.random.split(key, 32)
    f32 = jnp.float32
    def nrm(k, shape, scale):
        return jax.random.normal(k, shape, f32) * scale
    bi = nrm(ks[20], (DEPTH, N_DIRS, 1, N_HEADS_M), 0.1)
    bf = 3.0 + nrm(ks[21], (DEPTH, N_DIRS, 1, N_HEADS_M), 0.5)
    b_gate = jnp.concatenate([bi, bf], axis=2).reshape(DEPTH, N_GATES)
    return {
        'x_prompt': nrm(ks[0], (BATCH, SEQ, D_MODEL), 1.0),
        'x_sample': nrm(ks[1], (DEC_BATCH, DEC_SEQ, D_MODEL), 1.0),
        'state_C': nrm(ks[2], (DEC_BATCH, DEPTH, N_DIRS, N_HEADS_M, HEAD_DIM_M, HEAD_DIM_M), 0.1),
        'state_n': nrm(ks[3], (DEC_BATCH, DEPTH, N_DIRS, N_HEADS_M, HEAD_DIM_M), 0.5),
        'state_m': nrm(ks[4], (DEC_BATCH, DEPTH, N_DIRS, N_HEADS_M), 0.5),
        'c': nrm(ks[5], (DEC_BATCH, D_MODEL), 1.0),
        'c_ctx': nrm(ks[6], (D_MODEL,), 1.0),
        'w_ada': nrm(ks[7], (DEPTH, D_MODEL, N_MOD * D_MODEL), 0.5 * D_MODEL ** -0.5),
        'b_ada': nrm(ks[8], (DEPTH, N_MOD * D_MODEL), 0.02),
        'norm1_g': 1.0 + nrm(ks[9], (DEPTH, D_MODEL), 0.02),
        'norm2_g': 1.0 + nrm(ks[10], (DEPTH, D_MODEL), 0.02),
        'w_in': nrm(ks[11], (DEPTH, D_MODEL, D_IN_PROJ), D_MODEL ** -0.5),
        'w_fnet': nrm(ks[12], (DEPTH, D_FOURIER, D_FOURIER), D_FOURIER ** -0.5),
        'w_dw': nrm(ks[13], (DEPTH, CONV_WIDTH, D_CONV), CONV_WIDTH ** -0.5),
        'b_dw': nrm(ks[14], (DEPTH, D_CONV), 0.02),
        'conv_ln_g': 1.0 + nrm(ks[15], (DEPTH, D_CONV), 0.02),
        'conv_ln_b': nrm(ks[16], (DEPTH, D_CONV), 0.02),
        'w_pw': nrm(ks[17], (DEPTH, D_CONV, D_CONV), D_CONV ** -0.5),
        'b_gate': b_gate,
        'g_mh': 1.0 + nrm(ks[18], (DEPTH, D_MLSTM), 0.02),
        'w_out': nrm(ks[19], (DEPTH, D_MIX, D_MODEL), D_MIX ** -0.5),
        'w_router': nrm(ks[22], (D_MODEL, N_EXPERTS), D_MODEL ** -0.5),
        'b_router': nrm(ks[23], (N_EXPERTS,), 0.01),
        'w_exp_gate': nrm(ks[24], (DEPTH, N_EXPERTS, D_MODEL, D_EXPERT), D_MODEL ** -0.5),
        'w_exp_up': nrm(ks[25], (DEPTH, N_EXPERTS, D_MODEL, D_EXPERT), D_MODEL ** -0.5),
        'w_exp_down': nrm(ks[26], (DEPTH, N_EXPERTS, D_EXPERT, D_MODEL), D_EXPERT ** -0.5),
        'final_g': 1.0 + nrm(ks[27], (D_MODEL,), 0.02),
    }

def reference(x_prompt, x_sample, state_C, state_n, state_m, c, c_ctx, w_ada, b_ada, norm1_g, norm2_g,
              w_in, w_fnet, w_dw, b_dw, conv_ln_g, conv_ln_b, w_pw, b_gate, g_mh, w_out,
              w_router, b_router, w_exp_gate, w_exp_up, w_exp_down, final_g):
    f32 = jnp.float32
    def layer_params(l):
        return (w_ada[l], b_ada[l], norm1_g[l], norm2_g[l], w_in[l], w_fnet[l], w_dw[l], b_dw[l],
                conv_ln_g[l], conv_ln_b[l], w_pw[l], b_gate[l], g_mh[l], w_out[l],
                w_router, b_router, w_exp_gate[l], w_exp_up[l], w_exp_down[l])

    bp = x_prompt.shape[0]
    C0 = jnp.zeros((bp, N_DIRS, N_HEADS_M, HEAD_DIM_M, HEAD_DIM_M), f32)
    n0 = jnp.zeros((bp, N_DIRS, N_HEADS_M, HEAD_DIM_M), f32)
    m0 = jnp.zeros((bp, N_DIRS, N_HEADS_M), f32)
    xp = x_prompt
    Cs, ns, ms = [], [], []
    for l in range(DEPTH):
        xp, Cl, nl, ml = trunk_layer(xp, c_ctx, C0, n0, m0, layer_params(l))
        Cs.append(Cl)
        ns.append(nl)
        ms.append(ml)
    y_prompt = rmsnorm(xp, final_g)
    new_state_C = jnp.stack(Cs, axis=1).astype(x_prompt.dtype)
    new_state_n = jnp.stack(ns, axis=1).astype(x_prompt.dtype)
    new_state_m = jnp.stack(ms, axis=1).astype(x_prompt.dtype)

    n_tok = x_sample.shape[1]
    xs = x_sample + grid_pos_embed(n_tok, x_sample.dtype)[None]
    for l in range(DEPTH):
        xs, _, _, _ = trunk_layer(xs, c, state_C[:, l].astype(f32), state_n[:, l].astype(f32),
                                  state_m[:, l].astype(f32), layer_params(l))
    y_sample = rmsnorm(xs, final_g)
    return (y_prompt, y_sample, new_state_C, new_state_n, new_state_m)


_drawn_inputs = setup_inputs


def setup_inputs(seed=0):
    import zlib

    import numpy as np

    out = dict(_drawn_inputs(seed))
    spreads = {}
    factors = {'state_C': 8.0,
     'state_n': 8.0,
     'state_m': 8.0,
     'b_dw': 7.582,
     'conv_ln_g': 23.779,
     'conv_ln_b': 25.731,
     'g_mh': 20.326,
     'final_g': 9.73,
     'norm2_g': 3.868,
     'b_router': 2.975}
    for name, (base, spread) in spreads.items():
        noise = np.random.default_rng([zlib.crc32(name.encode()), seed]).standard_normal(out[name].shape)
        drawn = base * np.exp(spread * noise) if base else spread * noise
        out[name] = __import__('jax').numpy.asarray(drawn.astype(out[name].dtype))
    for name, factor in factors.items():
        out[name] = (out[name] * factor).astype(out[name].dtype)
    return out
```

```python
import numpy as np
import concourse.bass as bass
from concourse import mybir
from contextlib import ExitStack

F32 = mybir.dt.float32
F32R = mybir.dt.float32r
I32 = mybir.dt.int32
U32 = mybir.dt.uint32
ALU = mybir.AluOpType
ACT = mybir.ActivationFunctionType
AX = mybir.AxisListType

P = 128
D = 1024
KD = D // P
TP, TS = 256, 1024
T = TP + TS
NT = T // P
PT_TILES = TP // P
HT = T // 2
HTILES = NT // 2
GW = HT // 2
NH, HD = 4, 128
NE, NGRP, EPG = 16, 4, 4
FE = 256
TAPS, PAD = 31, 15
EPS = 1e-6
GRID_W = 64
NCH = 23
XA, CA, GT, QQ, KK, OO = 0, 2, 4, 6, 10, 14
NSLOT = 18
NADA = 48
ADA_FIRST = 16
ROWG = 36
NBLK = 36
NBMIN = 2 * T // P + 1
NEG = -1.0e30

C_CTX, C_C, C_G1, C_BDW, C_LNG, C_LNB, C_GMH, C_WDW = 0, 8, 16, 24, 26, 28, 30, 34
NROWS1 = C_WDW + 2 * TAPS


def program(nc, a, o, stop=99):
    ctx = ExitStack()

    def sbuf(name, shape, dt=F32):
        return ctx.enter_context(nc.sbuf_tensor(name, shape, dt))

    def sem(name):
        return ctx.enter_context(nc.semaphore(name))

    with nc.sbuf_tensor("input_parts", [P, 8 * T], F32R) as input_parts, nc.sbuf_tensor("weight_parts", [P, 4 * D], F32R) as weight_parts:
        hT = input_parts[:, :].rearrange("p (v k t) -> p v k t", v=2, k=KD)
        spl = weight_parts[:, :].rearrange("p (r v k n) -> p r v k n", r=2, v=2, k=KD)
    RA = sbuf("RA", [P, 8 * T])
    RS = sbuf("RS", [P, 4 * D])
    RB = sbuf("RB", [P, NSLOT * T])
    RC = sbuf("RC", [P, NT * NH * (HD + 1)])
    RW = sbuf("RW", [P, 4 * D])
    RE = sbuf("RE", [P, 3 * T])
    rows1 = sbuf("rows1", [NROWS1, P])
    rows2 = sbuf("rows2", [ADA_FIRST, P])
    ident = sbuf("ident", [P, P])
    colv = sbuf("colv", [P, NROWS1])
    bada = sbuf("bada", [P, ADA_FIRST])
    mod = sbuf("mod", [P, 2, ADA_FIRST])
    silc = sbuf("silc", [P, KD, 2])
    sc1 = sbuf("sc1", [P, 2, KD])
    gvec = sbuf("gvec", [ROWG, 3])
    ss = sbuf("ss", [P, 4, NT])
    mhalf = sbuf("mhalf", [P, NT])
    onesd = sbuf("onesd", [P, P])
    maskf = sbuf("maskf", [P, P])
    maskb = sbuf("maskb", [P, P])
    gcol = sbuf("gcol", [P, 4, NT, 2, NH])
    dec = sbuf("dec", [P, 2, NH, NT])
    small = sbuf("small", [ROWG, 4, NT])
    dens = sbuf("dens", [P, 4, NH])
    hss = sbuf("hss", [P, 3, NT, NH])
    uprompt = sbuf("uprompt", [P, 2, TP + 2 * PAD])

    PT = RB[:, :].rearrange("p (h s t) -> p h s t", h=2, s=NSLOT)
    vaug = RC[:, :].rearrange("p (t h e) -> p t h e", t=NT, h=NH)
    raw = RW[:, :].rearrange("p (r k n) -> p r k n", r=4, k=KD)
    LI = RE[0:ROWG, 0:T]
    LF = RE[0:ROWG, T:2 * T]
    fbuf = RE[:, 2 * T:3 * T].rearrange("p (b t) -> p b t", b=2)

    def xtile(t):
        h, i = divmod(t, HTILES)
        base = (h * NSLOT + (10 if h == 0 else 0)) * HT + i * D
        return RB[:, base:base + D]

    def xntile(t):
        h, i = divmod(t, HTILES)
        base = (h * NSLOT + (0 if h == 0 else 8)) * HT + i * D
        return RB[:, base:base + D]

    possel = RB[0:16, 8 * HT:8 * HT + D].rearrange("r (i p) -> r i p", p=P)
    posb = (NSLOT + 16) * HT
    postab = RB[0:16, posb:posb + 512]
    poscol = RB[:, posb + 512:posb + 1024]
    ub = (NSLOT + OO) * HT
    usample = RB[:, ub:ub + 2 * (TS + 2 * PAD)].rearrange("p (j t) -> p j t", j=2)

    psum = ctx.enter_context(nc.psum_tensor("psum", [P, 8, 512], F32))
    row1 = RE[0:2, 0:ADA_FIRST * P]
    MROWS = [(64, 0, 0, 14), (96, 0, 14, 28), (64, 14, 28, 32)]
    ROWS64, ROWS96 = 18 * P, 14 * P

    def modrow(b):
        part, place, c0, c1 = MROWS[b]
        return RE[part:part + 2, place * P:(place + c1 - c0) * P]


    AB = RA[:, 0:4 * T].rearrange("p (t v c) -> p t v c", t=NT, v=2)
    rowF = RA[0:ROWG, 4 * T:5 * T]
    rowG = RA[0:ROWG, 5 * T:6 * T]
    NK = TP + TS // 2 + 1
    YT = RA[:, 6 * T:6 * T + 2 * NK].rearrange("p (j k) -> p j k", j=2)
    rowC = RE[0:ROWG, 2 * T:3 * T]
    rowD = RB[0:ROWG, GT * HT:(GT + 2) * HT]
    rowE = RB[0:ROWG, (NSLOT + GT) * HT:(NSLOT + GT + 2) * HT]
    wf = RS[:, 0:1024].rearrange("p (v j c) -> p v j c", v=2, j=2)
    wpw = RS[:, 1024:1536].rearrange("p (j c) -> p j c", j=2)
    bdcs = RS[:, 1536:1792]
    ctp = RS[:, 1792:2816].rearrange("p (t v k) -> p t v k", t=2, v=2)
    sq = RS[:, 2816:2816 + 2 * HT].rearrange("p (j t) -> p j t", j=2)
    cts = RW[:, :].rearrange("p (r v k) -> p r v k", r=4, v=2)
    alt = sbuf("alt", [P, 1])
    ones1 = sbuf("ones1", [P, 1])
    Hd = RA[:, :].rearrange("p (d t e) -> p d t e", d=2, t=NT)
    nmb = RW[:, 0:1024].rearrange("p (b h t) -> p b h t", b=2, h=NH)
    Dm = RW[:, 1024:2048].rearrange("p (b h t) -> p b h t", b=2, h=NH)
    St = RW[:, 2048:3072].rearrange("p (b h t) -> p b h t", b=2, h=NH)
    kw = RW[:, 3072:4096].rearrange("p (b h t) -> p b h t", b=2, h=NH)
    E1 = HD + 1
    Cst = RE[:, 0:4 * NH * E1].rearrange("p (c h e) -> p c h e", c=4, h=NH)
    nb = 4 * NH * E1
    t1b = RE[:, nb:nb + 2 * NH * E1].rearrange("p (b h e) -> p b h e", b=2, h=NH)
    numb = RE[:, nb + 2 * NH * E1:nb + 3 * NH * E1].rearrange("p (h e) -> p h e", h=NH)
    SCALE = HD ** -0.5

    def wout(k):
        reg = RS if k < 4 else RC
        return reg[:, (k % 4) * D:(k % 4 + 1) * D]

    g2row = RC[:, 4 * D:5 * D]
    A2 = RW[:, 0:2 * D].rearrange("p (s c) -> p s c", s=2)
    B2 = RW[:, 2 * D:4 * D].rearrange("p (s c) -> p s c", s=2)
    rb = (NSLOT + 10) * HT
    ga1 = RB[:, rb:rb + 2 * D].rearrange("p (s c) -> p s c", s=2)
    ga2 = RB[:, rb + 2 * D:rb + 4 * D].rearrange("p (s c) -> p s c", s=2)
    fg = RB[:, rb + 4 * D:rb + 5 * D]
    NX = 5
    xr = RB[:, 10 * HT:10 * HT + NX * D].rearrange("p (b c) -> p b c", b=NX)
    x1 = RA[:, :].rearrange("p (t c) -> p t c", t=NT)
    h2 = RE[:, 0:2 * D].rearrange("p (b c) -> p b c", b=2)
    h2T = [RB[:, GT * HT:GT * HT + D].rearrange("p (k t) -> p k t", k=KD),
           RB[:, (NSLOT + GT) * HT:(NSLOT + GT) * HT + D].rearrange("p (k t) -> p k t", k=KD)]
    wr = sbuf("wr", [P, KD, NE])
    tabf = uprompt[:, :, :].rearrange("p a b -> p (a b)")
    upper = tabf[:, 0:P]
    NTAB = 37 + NE + NE + P
    CONSTB = tabf[:, P:P + NTAB]
    b128 = CONSTB[:, 0:37]
    mod3 = CONSTB[:, 37:37 + NE]
    brow = CONSTB[:, 37 + NE:37 + 2 * NE]
    iota = CONSTB[:, 37 + 2 * NE:NTAB]
    tokid = tabf[:, P + NTAB:P + NTAB + NT]
    ties = tabf[:, P + NTAB + NT:P + NTAB + NT + EPG * EPG].rearrange("p (i j) -> p i j", i=EPG)
    wtok = sbuf("wtok", [P, 2, NT])
    slotU = sbuf("slotU", [P, 2, NT], U32)
    idxU = sbuf("idxU", [P, NBLK + 1], U32)
    idxc = sbuf("idxc", [P, 2, 1], U32)
    eidI = sbuf("eidI", [P, NBLK], I32)
    offI = sbuf("offI", [P, NBLK], I32)
    endI = sbuf("endI", [P, NE], I32)
    trip = sbuf("trip", [P, 1], I32)
    WE = KD * 2 * FE + 2 * D
    WPART = 3
    wexp = RB[:, 0:3 * WE]
    xg = RW[:, 0:2 * D].rearrange("p (b c) -> p b c", b=2)
    xT = RW[:, 2 * D:4 * D].rearrange("p (b k t) -> p b k t", b=2, k=KD)
    mb = 3 * WE
    act_g = RB[:, mb:mb + 2 * FE].rearrange("p (b f) -> p b f", b=2)
    act_a = RB[:, mb + 2 * FE:mb + 4 * FE].rearrange("p (b f) -> p b f", b=2)
    aT = RB[:, mb + 4 * FE:mb + 6 * FE].rearrange("p (b j t) -> p b j t", b=2, j=2)
    assert mb + 6 * FE <= rb + 2 * D
    yb = RE[:, 0:2 * D].rearrange("p (b c) -> p b c", b=2)
    NY = 4
    y12 = RB[:, 0:8 * D].rearrange("p (b j c) -> p b j c", b=NY, j=2)
    x2 = RB[:, 8 * D:10 * D].rearrange("p (b c) -> p b c", b=2)
    sqb = RB[:, 10 * D:12 * D].rearrange("p (b c) -> p b c", b=2)
    outb = RB[:, 12 * D:15 * D].rearrange("p (b c) -> p b c", b=3)
    h2_dram = nc.dram_tensor("h2_scratch", (T, D), F32, kind="Internal").ap()
    y_dram = nc.dram_tensor("y_scratch", (NBLK * P, D), F32, kind="Internal").ap()
    modrow_dram = nc.dram_tensor("modrow_scratch", (2, 32 * P), F32, kind="Internal").ap()

    brow_in = sem("brow_in")
    mrow_ok = sem("mrow_ok")
    mrow_out = sem("mrow_out")
    tab_in = sem("tab_in")
    tab_ok = sem("tab_ok")
    wo_in = sem("wo_in")
    rows_b = sem("rows_b")
    rows_c = sem("rows_c")
    ab2_ok = sem("ab2_ok")
    o_ps = sem("o_ps")
    x1_ok = sem("x1_ok")
    sq2_ok = sem("sq2_ok")
    rs2_ok = sem("rs2_ok")
    h2_ok = sem("h2_ok")
    h2_out = [sem("h2_out0"), sem("h2_out1")]
    h2tr_ps = sem("h2tr_ps")
    h2T_ok = sem("h2T_ok")
    lg_ps = sem("lg_ps")
    sig_ok = sem("sig_ok")
    rstep = sem("rstep")
    pos_ps = sem("pos_ps")
    onehot = sem("onehot")
    tok_ps = sem("tok_ps")
    route_ok = sem("route_ok")
    w_full = sem("w_full")
    idx_ok = sem("idx_ok")
    xg_full = [sem("xg_full0"), sem("xg_full1")]
    xt_ps = sem("xt_ps")
    xt_ok = sem("xt_ok")
    gu_ps = sem("gu_ps")
    sg_ok = sem("sg_ok")
    a_ok = sem("a_ok")
    at_ps = sem("at_ps")
    at_ok = sem("at_ok")
    dn_ps = sem("dn_ps")
    yb_ok = sem("yb_ok")
    y_out = [sem("y_out0"), sem("y_out1")]
    y_in = [sem(f"y_in{b}") for b in range(NY)]
    t_ok = sem("t_ok")
    y_all = sem("y_all")
    fstep = sem("fstep")
    x2_ok = sem("x2_ok")
    sq3_ok = sem("sq3_ok")
    rs3_ok = sem("rs3_ok")
    o_ok = sem("o_ok")
    ob_out = [sem(f"ob_out{b}") for b in range(3)]

    rows_in = sem("rows_in")
    zero_out = sem("zero_out")
    pos_in = sem("pos_in")
    x_in = [sem(f"x_in{t}") for t in range(NT)]
    raw_full = [sem(f"raw_full{r}") for r in range(4)]
    ident_ok = sem("ident_ok")
    cols_ps = sem("cols_ps")
    cols_ok = sem("cols_ok")
    silc_ok = sem("silc_ok")
    ada_used = sem("ada_used")
    mod_ok = sem("mod_ok")
    ada_ev = sem("ada_ev")
    posr_ps = sem("posr_ps")
    x_pos = sem("x_pos")
    xs_out = sem("xs_out")
    ss_ok = sem("ss_ok")
    rstd_ok = sem("rstd_ok")
    xn_ok = sem("xn_ok")
    tr_ps = sem("tr_ps")
    f_ok = sem("f_ok")
    hT_ok = sem("hT_ok")
    wsplit = sem("wsplit")
    cm_ps = sem("cm_ps")
    cm_ev = sem("cm_ev")
    vtr_ps = sem("vtr_ps")
    v_ok = sem("v_ok")
    gates_ev = sem("gates_ev")
    gt_sig = sem("gt_sig")
    ones_ok = sem("ones_ok")
    upad_ok = sem("upad_ok")
    u_ok = sem("u_ok")
    conv = sem("conv")

    const_ok = sem("const_ok")
    misc_in = sem("misc_in")
    ct_full = [sem(f"ct_full{r}") for r in range(4)]
    ab_ps = sem("ab_ps")
    ab_ok = sem("ab_ok")
    yt_ps = sem("yt_ps")
    yt_ok = sem("yt_ok")
    fn_ps = sem("fn_ps")
    fn_ok = sem("fn_ok")
    ct_used = sem("ct_used")
    mean_ps = sem("mean_ps")
    cen_ok = sem("cen_ok")
    scl_ok = sem("scl_ok")
    sq_ok = sem("sq_ok")
    var_ps = sem("var_ps")
    var_ok = sem("var_ok")
    rst_ok = sem("rst_ok")
    z_ok = sem("z_ok")
    pw_ps = sem("pw_ps")
    pw_ok = sem("pw_ok")
    gstep = sem("gstep")
    gact = sem("gact")
    gout = sem("gout")
    gm_out = sem("gm_out")
    gtr_ps = sem("gtr_ps")
    gcol_ok = sem("gcol_ok")
    wcol_ok = sem("wcol_ok")
    dec_in = sem("dec_in")
    dec_ok = sem("dec_ok")
    st_in = sem("st_in")
    st_zero = sem("st_zero")
    nmb_in = [sem("nmb_in0"), sem("nmb_in1")]
    e_ok = sem("e_ok")
    exp_ok = sem("exp_ok")
    s_ps = sem("s_ps")
    kt_ps = sem("kt_ps")
    inter_ps = sem("inter_ps")
    intra_ps = sem("intra_ps")
    u_ps = sem("u_ps")
    st_ok = sem("st_ok")
    kw_ok = sem("kw_ok")
    t1_ok = sem("t1_ok")
    num_ok = sem("num_ok")
    den_ok = sem("den_ok")
    h_ok = sem("h_ok")
    c_ok = sem("c_ok")
    so_ok = sem("so_ok")
    hsum_ok = sem("hsum_ok")
    hsq_ok = sem("hsq_ok")
    hrs_ok = sem("hrs_ok")
    hn_ok = sem("hn_ok")
    htr_ps = sem("htr_ps")
    mix_ok = sem("mix_ok")
    out_done = sem("out_done")
    gm_dram = nc.dram_tensor("gm_scratch", (2, NH, T), F32, kind="Internal").ap()
    dec_dram = nc.dram_tensor("dec_scratch", (2, NH, NT), F32, kind="Internal").ap()

    UNITS = []
    for i in range(TS // P):
        UNITS += [(2, 0, PT_TILES + i), (3, 1, NT - 1 - i)]
        if i < PT_TILES:
            UNITS += [(0, 0, i), (1, 1, PT_TILES - 1 - i)]
    NU = len(UNITS)

    def before(n):
        return max((m for m in range(n) if UNITS[m][0] == UNITS[n][0]), default=None)

    def tile_cols(t):
        h, i = divmod(t, HTILES)
        return h, slice(i * P, (i + 1) * P)

    SPAN0 = HT - TP

    xs_dram = nc.dram_tensor("xs_scratch", (TS, D), F32, kind="Internal").ap()

    V0 = 1 + 14
    O0 = V0 + NH
    CONV_ALL = 2 * TAPS + 4 * TAPS

    FN = []
    for q, (n, dst) in enumerate((
            (TP, [(0, TP, 0, 0)]),
            (512, [(0, SPAN0, 0, TP), (SPAN0, 512, 1, 0)]),
            (1, [(0, 1, 1, 512 - SPAN0)]),
            (511, [(0, 511, 1, 513 - SPAN0)]))):
        for j in range(2):
            FN.append(((2 * q + j) % 4, n, dst))

    FN_ALL = len(FN)
    FN_DONE = [sum(len(f[2]) for f in FN[:q + 1]) for q in range(FN_ALL)]
    GOUT_ALL = 19

    place = [0, 0]

    def scratch(n, r=0):
        reg = (RS, RC)[r]
        place[r] += n
        return reg[:, place[r] - n:place[r]]

    NTE = NT * NE
    score, selv, rank, hot1, hot2, taken, tmp16 = (scratch(NTE) for _ in range(7))
    cmp_gt, cmp_eq = scratch(4 * NTE), scratch(4 * NTE)
    gsum, grank, gbest = (scratch(NT * NGRP) for _ in range(3))
    counts, nblk, ends = (scratch(NE) for _ in range(3))
    slotf, blkf = scratch(2 * NT), scratch(2 * NT)
    wsum, eidf = scratch(NT), scratch(NBLK)
    big = scratch(2 * NT * 37)
    offhot = scratch(2 * NT * P, 1).rearrange("p (n o) -> p n o", o=P)
    blkhot = scratch(2 * NT * NBLK, 1).rearrange("p (n b) -> p n b", b=NBLK)
    assert place[0] <= 4 * D and place[1] <= 5 * D
    ROUTE_A = 4 + 1 + 5 + 3 + 5 + 1 + 4 + 1

    block = ctx.enter_context(nc.Block())

    @block.sync
    def _(sp):
        for r in range(4):
            sp.dma_start(raw[:, r], a["w_ada"][r]).then_inc(raw_full[r], 16)
        with sp.Fori(1, ADA_FIRST // 4) as i:
            for r in range(4):
                sp.wait_ge(ada_used, i * 4 + (r - 3))
                sp.dma_start(raw[:, r], a["w_ada"][bass.ds(i * 4 + r, 1)].rearrange("a p k n -> (a p) k n"))\
                  .then_inc(raw_full[r], 16)

        for h in range(2):
            n0 = h * NCH

            def load_proj(n, r, c, free):
                sp.wait_ge(wsplit, free)
                src = a["w_in"][c] if isinstance(c, int) else a["w_in"][bass.ds(c, 1)].rearrange("a p k n -> (a p) k n")
                sp.dma_start(raw[:, r], src).then_inc(raw_full[r], 16)

            def load_ada(i, r, used):
                sp.wait_ge(ada_used, used)
                src = a["w_ada"][bass.ds(i, 1)].rearrange("a p k n -> (a p) k n")
                sp.dma_start(raw[:, r], src).then_inc(raw_full[r], 16)

            if h == 0:
                sp.wait_ge(ada_used, ADA_FIRST - 3)
                sp.dma_start(raw[:, 0], a["w_in"][0]).then_inc(raw_full[0], 16)
                sp.wait_ge(ada_used, ADA_FIRST)
                sp.dma_start(raw[:, 1], a["w_in"][1]).then_inc(raw_full[1], 16)
                sp.dma_start(raw[:, 2], a["w_ada"][ADA_FIRST]).then_inc(raw_full[2], 16)
                first = 2
            else:
                load_proj(n0, n0 % 2, 0, 2 * (n0 - 1))
                first = 1
            if h == 0:
                load_proj(2, 0, 2, 2)
                sp.dma_start(raw[:, 3], a["w_ada"][ADA_FIRST + 1]).then_inc(raw_full[3], 16)
                start = 1
            else:
                start = 0
            with sp.Fori(start, 7) as i:
                for j in range(2):
                    load_proj(None, (n0 + 1 + j) % 2, i * 2 + (1 + j), i * 4 + 2 * (n0 + j))
                    load_ada(i * 2 + (ADA_FIRST + 14 * h + j), 2 + j, i * 2 + (ADA_FIRST + 14 * h + j - 1))
            for c in range(V0, O0):
                load_proj(None, (n0 + c) % 2, c, 2 * (n0 + c - 1))
            with sp.Fori(0, 2) as i:
                for j in range(2):
                    load_proj(None, (n0 + O0 + j) % 2, i * 2 + (O0 + j), i * 4 + 2 * (n0 + O0 + j - 1))
                    if h == 1:
                        load_ada(i * 2 + (ADA_FIRST + 28 + j), 2 + j, i * 2 + (ADA_FIRST + 28 + j - 1))

        sp.wait_ge(cm_ps, 2 * NCH)
        sp.dma_start(bdcs, a["bdcs"]).then_inc(misc_in, 16)
        sp.dma_start(ctp, a["ctp"]).then_inc(misc_in, 16)
        sp.dma_start(alt[:, :], a["alt"]).then_inc(misc_in, 16)
        sp.dma_start(wf, a["wf"]).then_inc(misc_in, 16)
        sp.dma_start(wpw, a["wpw"]).then_inc(misc_in, 16)
        for q in range(2):
            for n, p0 in ((ROWS64, 64), (ROWS96, 96)):
                src = a["b_ada64"] if p0 == 64 else a["b_ada96"]
                sp.dma_start(RA[p0 + q:p0 + q + 1, 4 * T:4 * T + n], src.rearrange("(a n) -> a n", a=1)).then_inc(brow_in, 16)
        sp.wait_ge(wsplit, 4 * NCH)
        sp.wait_ge(ada_used, NADA)
        for i in range(TS // P):
            if i >= 4:
                sp.wait_ge(ct_used, i - 3)
            sp.dma_start(cts[:, i % 4], a["cts"][i]).then_inc(ct_full[i % 4], 16)
        sp.wait_ge(mrow_ok, 2)
        for b in range(3):
            sp.dma_start(modrow_dram[:, MROWS[b][2] * P:MROWS[b][3] * P], modrow(b)).then_inc(mrow_out, 16)
        sp.wait_ge(conv, 2 * TAPS)
        sp.dma_start(CONSTB, a["tables"].partition_broadcast(P)).then_inc(tab_in, 16)
        sp.dma_start(tokid, a["tokid"]).then_inc(tab_in, 16)
        sp.dma_start(wr[:, :, :], a["w_router"]).then_inc(tab_in, 16)
        sp.wait_ge(gout, GOUT_ALL)
        for d in range(2):
            sp.dma_start(gm_dram[d], rowG[32 * d:32 * d + NH, :]).then_inc(gm_out, 16)
            sp.dma_start(dec_dram[d], small[32 * d:32 * d + NH, 3, :]).then_inc(gm_out, 16)
            sp.dma_start(o[4][0, 0, d:d + 1, :].rearrange("a h -> h a"), small[32 * d:32 * d + NH, 2, 0:1],
                         allow_slow_non_contiguous=True).then_inc(out_done, 16)
        sp.wait_ge(gm_out, 64)
        sp.dma_start(dec[:, :, :, :].rearrange("p d h t -> p (d h t)"),
                     dec_dram.rearrange("d h t -> (d h t)").partition_broadcast(P)).then_inc(dec_in, 16)
        sp.wait_ge(gtr_ps, 4)
        for d in range(2):
            sp.dma_start(Cst[:, 2 + d, :, 0:HD], a["state_C"][d].rearrange("h d e -> d h e")).then_inc(st_in, 16)
            sp.dma_start(Cst[:, 2 + d, :, HD:E1], a["state_n"][d].rearrange("h (d a) -> d h a", a=1),
                         allow_slow_non_contiguous=True).then_inc(st_in, 16)
        sp.wait_ge(ct_used, TS // P)
        for n, (c, d, t) in enumerate(UNITS):
            if n >= 2:
                sp.wait_ge(e_ok, NH * (n - 1))
            sp.dma_start(nmb[:, n % 2], gm_dram[d][:, t * P:(t + 1) * P].partition_broadcast(P)).then_inc(nmb_in[n % 2], 16)
            if n == 0:
                sp.wait_ge(pw_ps, 2)
                for k in range(4):
                    sp.dma_start(wout(k), a["w_out"][k]).then_inc(wo_in, 16)
        for c in range(2):
            last = max(n for n in range(NU) if UNITS[n][0] == c)
            sp.wait_ge(c_ok, NH * (last + 1))
            sp.dma_start(o[2][0, 0, c].rearrange("h d e -> d h e"), Cst[:, c, :, 0:HD]).then_inc(out_done, 16)
            sp.dma_start(o[3][0, 0, c].rearrange("h (d a) -> d h a", a=1), Cst[:, c, :, HD:E1],
                         allow_slow_non_contiguous=True).then_inc(out_done, 16)
        sp.wait_ge(u_ps, NU)
        for k in range(4, KD):
            sp.dma_start(wout(k), a["w_out"][k]).then_inc(wo_in, 16)
        sp.dma_start(g2row, a["norm2_g"].partition_broadcast(P)).then_inc(rows_b, 16)
        sp.wait_ge(mrow_out, 48)
        for q in range(2):
            sp.dma_start(A2[:, q], modrow_dram[q, 2 * D:3 * D].partition_broadcast(P)).then_inc(rows_b, 16)
            sp.dma_start(B2[:, q], modrow_dram[q, D:2 * D].partition_broadcast(P)).then_inc(rows_b, 16)
        sp.wait_ge(mix_ok, NH * NT)
        for q in range(2):
            sp.dma_start(ga1[:, q], modrow_dram[q, 0:D].partition_broadcast(P)).then_inc(rows_b, 16)

        def load_x(t):
            src = a["x_prompt"][t * P:(t + 1) * P] if t < PT_TILES else xs_dram[(t - PT_TILES) * P:(t - PT_TILES + 1) * P]
            sp.dma_start(xr[:, t % NX], src).then_inc(x_in[t], 16)

        for t in range(NX):
            load_x(t)
        for q in range(2):
            sp.dma_start(ga2[:, q], modrow_dram[q, 3 * D:4 * D].partition_broadcast(P)).then_inc(rows_c, 16)
        sp.dma_start(fg, a["final_g"].partition_broadcast(P)).then_inc(rows_c, 16)
        for t in range(NT):
            if t + NX < NT:
                sp.wait_ge(x1_ok, 2 * (t + 1))
                load_x(t + NX)
            sp.wait_ge(h2_ok, 2 * (t + 1))
            sp.dma_start(h2_dram[t * P:(t + 1) * P], h2[:, t % 2]).then_inc(h2_out[t % 2], 16)
        WP = WE // WPART

        def load_expert(r, src, came):
            if came is not None:
                sp.wait_ge(w_full, came)
            for q in range(WPART):
                sp.dma_start(wexp[:, r * WE + q * WP:r * WE + (q + 1) * WP], src[:, q * WP:(q + 1) * WP]).then_inc(w_full, 16)

        sp.wait_ge(lg_ps, NT)
        for e in range(3):
            load_expert(e, a["w_exp"][e], 16 * WPART * e if e else None)
        sp.wait_ge(route_ok, 1)
        with sp.Fori(1, NE // 3) as i:
            for r in range(3):
                done = sp.value_load(endI[0:1, bass.ds(i * 3 + (r - 3), 1)], min_val=1, max_val=NBLK)
                sp.wait_ge(w_full, i * (48 * WPART) + 16 * WPART * r)
                sp.wait_ge(dn_ps, done)
                load_expert(r, a["w_exp"][bass.ds(i * 3 + r, 1)].rearrange("a p n -> (a p) n"), None)
        done = sp.value_load(endI[0:1, NE - 4:NE - 3], min_val=1, max_val=NBLK)
        sp.wait_ge(dn_ps, done)
        load_expert(0, a["w_exp"][NE - 1], 16 * WPART * (NE - 1))
        sp.wait_ge(out_done, 16 * 6)
        for t in range(NT):
            sp.wait_ge(o_ok, t + 1)
            dst = o[0][0, t * P:(t + 1) * P] if t < PT_TILES else o[1][0, (t - PT_TILES) * P:(t - PT_TILES + 1) * P]
            sp.dma_start(dst, outb[:, t % 3]).then_inc(ob_out[t % 3], 16)
        for b in range(3):
            sp.wait_ge(ob_out[b], 16 * len(range(b, NT, 3)))

    @block.gpsimd
    def _(gp):
        nc.gpsimd.memset(ident[:, :], 0.0).then_inc(ident_ok, 1)
        gp.wait_ge(ident_ok, 1)
        gp.affine_select(out=ident[:, :], in_=ident[:, :], compare_op=ALU.not_equal, fill=1.0, base=0,
                         pattern=[[-1, P]], channel_multiplier=1).then_inc(ident_ok, 1)
        nc.gpsimd.memset(mhalf[:, :], -0.5).then_inc(ident_ok, 1)
        nc.gpsimd.memset(ones1[:, :], 1.0).then_inc(ident_ok, 1)
        nc.gpsimd.memset(RC[:, 0:D], 0.0).then_inc(ident_ok, 1)
        nc.gpsimd.memset(uprompt[:, :, :], 0.0).then_inc(upad_ok, 1)
        nc.gpsimd.memset(onesd[:, :], 1.0 / 256).then_inc(const_ok, 1)
        nc.gpsimd.memset(maskf[:, :], 0.0).then_inc(const_ok, 1)
        nc.gpsimd.memset(maskb[:, :], 0.0).then_inc(const_ok, 1)
        gp.wait_ge(const_ok, 3)
        gp.affine_select(out=maskf[:, :], in_=maskf[:, :], compare_op=ALU.is_ge, fill=NEG, base=0,
                         pattern=[[1, P]], channel_multiplier=-1).then_inc(const_ok, 1)
        gp.affine_select(out=maskb[:, :], in_=maskb[:, :], compare_op=ALU.is_ge, fill=NEG, base=0,
                         pattern=[[-1, P]], channel_multiplier=1).then_inc(const_ok, 1)
        gp.wait_ge(ident_ok, 4)
        for t in range(NT):
            gp.wait_ge(ss_ok, t + 1)
            nc.gpsimd.tensor_scalar(ss[:, 1, t:t + 1], ss[:, 0, t:t + 1], 1.0 / D, EPS, ALU.mult, ALU.add)\
                .then_inc(rstd_ok, 1)
            gp.wait_ge(rstd_ok, 2 * t + 1)
            nc.gpsimd.tensor_tensor(ss[:, 2, t:t + 1], ss[:, 1, t:t + 1], mhalf[:, 0:1], ALU.pow)\
                .then_inc(rstd_ok, 1)

        def split(r, full, before, done):
            gp.wait_ge(raw_full[r], full)
            if before is not None:
                gp.wait_ge(cm_ps, before)
            nc.gpsimd.tensor_tensor(spl[:, r, 0], raw[:, r], ones1[:, :].unsqueeze(1).broadcast_to([P, KD, P]), ALU.mult).then_inc(wsplit, 1)
            gp.wait_ge(wsplit, done)
            nc.gpsimd.tensor_tensor(spl[:, r, 1], raw[:, r], spl[:, r, 0].bitcast(F32), ALU.subtract)\
                .then_inc(wsplit, 1)

        def head_rms(t):
            gp.wait_ge(hsq_ok, NH * (t + 1))
            nc.gpsimd.tensor_scalar(hss[:, 1, t], hss[:, 0, t], 1.0 / HD, EPS, ALU.mult, ALU.add).then_inc(hrs_ok, 1)
            gp.wait_ge(hrs_ok, 2 * t + 1)
            nc.gpsimd.tensor_tensor(hss[:, 2, t], hss[:, 1, t], mhalf[:, 0:NH], ALU.pow).then_inc(hrs_ok, 1)

        for n in (0, 1):
            split(n, 16 * 5, None, 2 * n + 1)
        with gp.Fori(1, NCH) as i:
            for r in range(2):
                split(r, (i + 5) * 16, i * 2 + (r - 1), i * 4 + (2 * r + 1))

        gp.wait_ge(ada_ev, 4 + NADA - ADA_FIRST)
        gp.wait_ge(brow_in, 64)
        for p0, n in ((64, ROWS64), (96, ROWS96)):
            rows = RE[p0:p0 + 2, 0:n]
            nc.gpsimd.tensor_tensor(rows, rows, RA[p0:p0 + 2, 4 * T:4 * T + n], ALU.add).then_inc(mrow_ok, 1)
        gp.wait_ge(mrow_ok, 2)
        gp.wait_ge(zero_out, 16 * (NBLK - NBMIN))
        nc.gpsimd.memset(vaug[:, :, :, HD], 1.0).then_inc(ones_ok, 1)
        gp.wait_ge(gtr_ps, 4)
        gp.wait_ge(mrow_out, 48)
        nc.gpsimd.memset(Cst[:, 0:2], 0.0).then_inc(st_zero, 1)
        for n, (c, d, t) in enumerate(UNITS):
            gp.wait_ge(den_ok, 3 * (n + 1))
            if n == 0:
                gp.wait_ge(fn_ps, FN_ALL)
            nc.gpsimd.tensor_tensor(Hd[:, d, t].rearrange("p (h e) -> p h e", h=NH), numb[:, :, 0:HD],
                                    dens[:, 2, :].unsqueeze(2).broadcast_to([P, NH, HD]), ALU.mult).then_inc(h_ok, 1)
        for t in range(NT):
            if t == 0:
                gp.wait_ge(h_ok, NU)
            nc.gpsimd.tensor_tensor(Hd[:, 0, t], Hd[:, 0, t], Hd[:, 1, t], ALU.add).then_inc(hsum_ok, 1)
            if t >= 1:
                head_rms(t - 1)
        head_rms(NT - 1)
        gp.wait_ge(var_ps, 2)
        nc.gpsimd.memset(onesd[:, :], 1.0).then_inc(const_ok, 1)
        gp.wait_ge(conv, 2 * TAPS)
        nc.gpsimd.memset(upper, 1.0).then_inc(tab_ok, 1)
        gp.wait_ge(tab_ok, 1)
        gp.affine_select(out=upper, in_=upper, compare_op=ALU.is_ge, fill=0.0, base=-1,
                         pattern=[[1, P]], channel_multiplier=-1).then_inc(tab_ok, 1)

        def root(src_ok, n, r, col, done):
            gp.wait_ge(src_ok, n)
            nc.gpsimd.tensor_scalar(ss[:, 1, col:col + 1], ss[:, r, col:col + 1], 1.0 / D, EPS, ALU.mult, ALU.add).then_inc(done, 1)
            gp.wait_ge(done, 2 * n - 1)
            nc.gpsimd.tensor_tensor(ss[:, 2, col:col + 1], ss[:, 1, col:col + 1], mhalf[:, 0:1], ALU.pow).then_inc(done, 1)

        for t in range(NT):
            root(sq2_ok, t + 1, 0, t, rs2_ok)

        def fetch(r):
            nc.gpsimd.indirect_dma_start(xg[:, r], None, h2_dram, bass.IndirectOffsetOnAxis(ap=idxc[:, r], axis=0))\
                .then_inc(xg_full[r], 16)

        gp.wait_ge(route_ok, 1)
        for b in range(2):
            gp.wait_ge(h2_out[b], 16 * (NT // 2))
        pairs = gp.value_load(trip[0:1, 0:1], min_val=1, max_val=NBLK // 2 - 1)
        for r in range(2):
            nc.gpsimd.tensor_copy(idxc[:, r], idxU[:, r:r + 1]).then_inc(idx_ok, 1)
        for r in range(2):
            gp.wait_ge(idx_ok, r + 1)
            fetch(r)
        gp.wait_ge(xg_full[0], 16)
        nc.gpsimd.tensor_copy(idxc[:, 0], idxU[:, 2:3]).then_inc(idx_ok, 1)
        with gp.Fori(0, pairs) as i:
            for j in range(2):
                gp.wait_ge(xt_ps, i * 2 + (j + 1))
                gp.wait_ge(idx_ok, i * 2 + (3 + j))
                gp.wait_ge(xg_full[1 - j], i * 16 + 16 * (j + 1))
                nc.gpsimd.tensor_copy(idxc[:, 1 - j], idxU[:, bass.ds(i * 2 + (3 + j), 1)]).then_inc(idx_ok, 1)
                fetch(j)
        gp.wait_ge(y_all, 1)
        def fetch_outputs(t):
            for j in range(2):
                nc.gpsimd.indirect_dma_start(y12[:, t % NY, j], None, y_dram,
                                             bass.IndirectOffsetOnAxis(ap=slotU[:, j, t:t + 1], axis=0)).then_inc(y_in[t % NY], 16)

        for t in range(NY):
            fetch_outputs(t)
        for t in range(NT):
            root(sq3_ok, t + 1, 0, t, rs3_ok)
            if t + NY < NT:
                gp.wait_ge(fstep, 2 * (t + 1))
                fetch_outputs(t + NY)


    @block.scalar
    def _(act):
        def h2_transposed(t):
            act.wait_ge(h2tr_ps, t + 1)
            nc.scalar.activation(h2T[t % 2][:, :, :].rearrange("p (b k) t -> p b (k t)", b=2), psum[:, 4:6, :], ACT.Copy)\
                .then_inc(h2T_ok, 1)

        def final_square(t):
            act.wait_ge(x2_ok, t + 1)
            nc.scalar.activation(sqb[:, t % 2], x2[:, t % 2], ACT.Square, accum_out=ss[:, 0, t:t + 1]).then_inc(sq3_ok, 1)

        act.dma_start(rows1[:, :], a["rows1"]).then_inc(rows_in, 16)
        act.dma_start(rows2[:, :], a["rows2"]).then_inc(rows_in, 16)
        for t in range(PT_TILES):
            act.dma_start(xtile(t), a["x_prompt"][t * P:(t + 1) * P, :]).then_inc(x_in[t], 16)
        act.dma_start(possel[:, :, :], a["possel"]).then_inc(pos_in, 16)
        act.dma_start(postab[:, :], a["postab"]).then_inc(pos_in, 16)
        act.dma_start(poscol[:, :], a["poscol"]).then_inc(pos_in, 16)
        act.dma_start(gvec[:, :], a["gvec"]).then_inc(pos_in, 16)
        for t in range(PT_TILES, NT):
            s = (t - PT_TILES) * P
            act.dma_start(xtile(t), a["x_sample"][s:s + P, :]).then_inc(x_in[t], 16)
        act.wait_ge(cols_ok, 1)
        nc.scalar.activation(silc[:, :, :], colv[:, C_CTX:C_G1].rearrange("p (s k) -> p k s", s=2), ACT.Silu)\
            .then_inc(silc_ok, 1)
        for t in range(NT):
            if t < PT_TILES:
                act.wait_ge(x_in[t], 16)
            else:
                act.wait_ge(x_pos, 2 * (t - PT_TILES + 1))
            nc.scalar.activation(xntile(t), xtile(t), ACT.Square, accum_out=ss[:, 0, t:t + 1]).then_inc(ss_ok, 1)
            if t >= PT_TILES:
                s = (t - PT_TILES) * P
                act.dma_start(xs_dram[s:s + P, :], xtile(t)).then_inc(xs_out, 16)

        for i in range(4):
            act.wait_ge(ada_used, 4 * (i + 1))
            nc.scalar.activation(row1[:, i * 512:(i + 1) * 512], psum[0:2, i, :], ACT.Copy).then_inc(ada_ev, 1)

        def ada_row(b, i, j, used):
            act.wait_ge(ada_used, used)
            nc.scalar.activation(modrow(b)[:, bass.ds(i, P)], psum[0:2, 6 + j, 0:P], ACT.Copy).then_inc(ada_ev, 1)

        def evac_half(h):
            if h == 0:
                act.wait_ge(mod_ok, 3)
            for k in range(KD):
                g = h * KD + k
                act.wait_ge(tr_ps, g + 1)
                if g >= 2:
                    act.wait_ge(hT_ok, 2 * (g - 1))
                for b, (c0, c1) in enumerate(((0, TP), (TP, HT))):
                    s = 0 if (h == 0 and b == 0) else 1
                    nc.scalar.activation(fbuf[:, k % 2, c0:c1], psum[:, 2 * (k % 2) + b, 0:c1 - c0], ACT.Identity,
                                         scale=sc1[:, s, k:k + 1], bias=mod[:, s, k:k + 1]).then_inc(f_ok, 1)

        def evac_chunk(n1, bank, dst):
            act.wait_ge(cm_ps, n1)
            nc.scalar.activation(dst, psum[:, bank:bank + 2, 0:GW], ACT.Copy).then_inc(cm_ev, 1)

        def slot_ap(h, s):
            if isinstance(s, int):
                return PT[:, h, s].rearrange("p (g t) -> p g t", g=2)
            return PT[:, h, bass.ds(s, 1)].rearrange("p a (g t) -> p (a g) t", g=2)

        for h in range(2):
            n0 = h * NCH
            evac_half(h)
            if h == 0:
                act.wait_ge(ident_ok, 5)
                for b in range(NBMIN, NBLK):
                    act.dma_start(y_dram[b * P:(b + 1) * P], RC[:, 0:D]).then_inc(zero_out, 16)
            act.wait_ge(cm_ps, n0 + 1)
            if h == 0:
                act.wait_ge(pos_in, 64)
            bank = 2 * (n0 % 2)
            cols = slice(h * HT, (h + 1) * HT)
            nc.scalar.activation(LI[:, cols].rearrange("p (g t) -> p g t", g=2), psum[0:ROWG, bank:bank + 2, 0:GW],
                                 ACT.Identity, bias=gvec[:, 0:1]).then_inc(gates_ev, 1)
            nc.scalar.activation(LF[:, cols].rearrange("p (g t) -> p g t", g=2),
                                 psum[64:64 + ROWG, bank:bank + 2, 0:GW], ACT.Copy).then_inc(cm_ev, 1)
            if h == 0:
                act.wait_ge(xs_out, 16 * (NT - PT_TILES))
            with act.Fori(0, 3) as i:
                for j in range(2):
                    evac_chunk(i * 2 + (n0 + 2 + j), 2 * ((n0 + 1 + j) % 2), slot_ap(h, i * 2 + j))
                    ada_row(h, i * (2 * P) + j * P, j, i * 2 + (ADA_FIRST + 14 * h + j + 1))
            act.wait_ge(cm_ev, n0 + 7)
            nc.scalar.activation(PT[:, h, GT:GT + 2], PT[:, h, GT:GT + 2], ACT.Sigmoid).then_inc(gt_sig, 1)
            with act.Fori(3, 7) as i:
                for j in range(2):
                    evac_chunk(i * 2 + (n0 + 2 + j), 2 * ((n0 + 1 + j) % 2), slot_ap(h, i * 2 + j))
                    ada_row(h, i * (2 * P) + j * P, j, i * 2 + (ADA_FIRST + 14 * h + j + 1))

            def v_tokens(j):
                act.wait_ge(vtr_ps, h * NH + j + 1)
                if h == 0 and j == 0:
                    act.wait_ge(zero_out, 16 * (NBLK - NBMIN))
                nc.scalar.activation(vaug[:, 5 * h:5 * h + 2, j, 0:HD],
                                     psum[:, 4, 0:2 * P].rearrange("p (t e) -> p t e", e=HD), ACT.Copy).then_inc(v_ok, 1)
                nc.scalar.activation(vaug[:, 5 * h + 2:5 * h + 5, j, 0:HD],
                                     psum[:, 5, 0:3 * P].rearrange("p (t e) -> p t e", e=HD), ACT.Copy).then_inc(v_ok, 1)

            for j in range(NH):
                n = n0 + V0 + j
                act.wait_ge(cm_ps, n + 1)
                if j == 0:
                    act.wait_ge(hT_ok, 2 * KD * (h + 1))
                if j >= 2:
                    act.wait_ge(vtr_ps, h * NH + j - 1)
                nc.scalar.activation(fbuf[:, j % 2].rearrange("p (g t) -> p g t", g=2),
                                     psum[:, 2 * (n % 2):2 * (n % 2) + 2, 0:GW], ACT.Copy).then_inc(cm_ev, 1)
                if j >= 1:
                    v_tokens(j - 1)
            v_tokens(NH - 1)
            if h == 1:
                act.wait_ge(conv, CONV_ALL)
            with act.Fori(0, 2) as i:
                for j in range(2):
                    evac_chunk(i * 2 + (n0 + O0 + 1 + j), 2 * ((n0 + O0 + j) % 2), slot_ap(h, i * 2 + (OO + j)))
                    if h == 1:
                        ada_row(2, i * (2 * P) + j * P, j, i * 2 + (ADA_FIRST + 28 + j + 1))

        act.wait_ge(cm_ev, 2 * NCH)
        for h in range(2):
            nc.scalar.activation(PT[:, h, OO:OO + 4], PT[:, h, OO:OO + 4], ACT.Sigmoid).then_inc(so_ok, 1)
        for t in range(NT):
            act.wait_ge(ab_ps, t + 1)
            nc.scalar.activation(AB[:, t].rearrange("p v (j c) -> p j v c", j=2),
                                 psum[:, t % 4, :].rearrange("p (j v c) -> p j v c", j=2, v=2), ACT.Copy).then_inc(ab_ok, 1)
        act.wait_ge(gstep, 10)
        nc.scalar.activation(rowC, rowC, ACT.Exp, scale=-1.0).then_inc(gact, 1)
        act.wait_ge(gact, 1)
        nc.scalar.activation(rowC, rowC, ACT.Ln, bias=1.0).then_inc(gact, 1)
        def squares(h):
            act.wait_ge(cen_ok, 2 * (h + 1))
            if h == 1:
                act.wait_ge(scl_ok, 1)
            for j in range(2):
                nc.scalar.activation(sq[:, j], PT[:, h, CA + j], ACT.Square).then_inc(sq_ok, 1)

        def conv_silu(h):
            act.wait_ge(var_ok, h + 1)
            nc.scalar.activation(sq[:, 0], sq[:, 0], ACT.Ln).then_inc(rst_ok, 1)
            act.wait_ge(rst_ok, 2 * h + 1)
            nc.scalar.activation(sq[:, 1], sq[:, 0], ACT.Exp, scale=-0.5).then_inc(rst_ok, 1)
            act.wait_ge(scl_ok, h + 1)
            for j in range(2):
                nc.scalar.activation(PT[:, h, CA + j], PT[:, h, CA + j], ACT.Silu, scale=colv[:, C_LNG + j:C_LNG + j + 1],
                                     bias=colv[:, C_LNB + j:C_LNB + j + 1]).then_inc(z_ok, 1)

        squares(0)
        conv_silu(0)
        act.wait_ge(yt_ps, 1)
        nc.scalar.activation(YT[:, :, 0:TP], psum[:, 4:6, 0:TP], ACT.Copy).then_inc(yt_ok, 1)
        squares(1)
        act.wait_ge(ct_used, TS // P)
        nc.scalar.activation(YT[:, :, TP:TP + 512], psum[:, 6:8, :], ACT.Copy).then_inc(yt_ok, 1)
        act.wait_ge(yt_ps, 2)
        nc.scalar.activation(YT[:, :, TP + 512:NK], psum[:, 4, 0:2].unsqueeze(2), ACT.Copy).then_inc(yt_ok, 1)
        conv_silu(1)
        for q, (bank, n, dst) in enumerate(FN):
            act.wait_ge(fn_ps, q + 1)
            for (c0, c1, h, col) in dst:
                nc.scalar.activation(PT[:, h, XA + q % 2, col:col + c1 - c0], psum[:, bank, c0:c1], ACT.Copy).then_inc(fn_ok, 1)
        for h in range(2):
            act.wait_ge(pw_ps, h + 1)
            for j in range(2):
                nc.scalar.activation(PT[:, h, CA + j].rearrange("p (g t) -> p g t", g=2), psum[:, 2 * j:2 * j + 2, 0:GW], ACT.Copy)\
                    .then_inc(pw_ok, 1)
        for q in range(4):
            act.wait_ge(gtr_ps, q + 1)
            src = psum[:, 4 + q, 0:NT * ROWG].rearrange("p (t r) -> p t r", r=ROWG)
            for d in range(2):
                nc.scalar.activation(gcol[:, q, :, d, :], src[:, :, 32 * d:32 * d + NH], ACT.Copy if q == 0 else ACT.Exp)\
                    .then_inc(gcol_ok, 1)
        act.wait_ge(dec_in, 16)
        nc.scalar.activation(dec[:, :, :, :], dec[:, :, :, :], ACT.Exp).then_inc(dec_ok, 1)
        act.wait_ge(wcol_ok, 1)
        def decays(n):
            act.wait_ge(e_ok, NH * (n + 1))
            nc.scalar.activation(Dm[:, n % 2], Dm[:, n % 2], ACT.Exp).then_inc(exp_ok, 1)

        decays(0)
        decays(1)
        for n, (c, d, t) in enumerate(UNITS):
            act.wait_ge(kt_ps, n + 1)
            if n >= 2:
                act.wait_ge(u_ps, n - 1)
            for hd in range(NH):
                nc.scalar.activation(kw[:, n % 2, hd], psum[:, 1, hd * P:(hd + 1) * P], ACT.Copy,
                                     scale=gcol[:, 2, t, d, hd:hd + 1]).then_inc(kw_ok, 1)
            act.wait_ge(inter_ps, n + 1)
            if n >= 2:
                act.wait_ge(num_ok, n - 1)
            for hd in range(NH):
                nc.scalar.activation(t1b[:, n % 2, hd], psum[:, 4 + hd // 2, (hd % 2) * E1:(hd % 2 + 1) * E1], ACT.Copy,
                                     scale=gcol[:, 1, t, d, hd:hd + 1]).then_inc(t1_ok, 1)
            if n + 2 < NU:
                decays(n + 2)
        for t in range(NT):
            act.wait_ge(hsum_ok, t + 1)
            for hd in range(NH):
                nc.scalar.activation(Hd[:, 1, t, hd * HD:(hd + 1) * HD], Hd[:, 0, t, hd * HD:(hd + 1) * HD], ACT.Square,
                                     accum_out=hss[:, 0, t, hd:hd + 1]).then_inc(hsq_ok, 1)
        for t in range(NT):
            act.wait_ge(x1_ok, 2 * (t + 1))
            if t >= 2:
                act.wait_ge(h2_out[t % 2], 16 * (t // 2))
            nc.scalar.activation(h2[:, t % 2], x1[:, t], ACT.Square, accum_out=ss[:, 0, t:t + 1]).then_inc(sq2_ok, 1)
            h2_transposed(t)
        act.wait_ge(lg_ps, NT)
        nc.scalar.activation(score, psum[:, 6, 0:NT * NE], ACT.Sigmoid).then_inc(sig_ok, 1)

        act.wait_ge(route_ok, 1)
        pairs = act.value_load(trip[0:1, 0:1], min_val=1, max_val=NBLK // 2 - 1)

        def x_chan(r, n):
            act.wait_ge(xt_ps, n)
            nc.scalar.activation(xT[:, r].rearrange("p (b k) t -> p b (k t)", b=2), psum[:, 4:6, :], ACT.Copy).then_inc(xt_ok, 1)

        def gate_silu(r, n):
            act.wait_ge(gu_ps, n)
            nc.scalar.activation(act_g[:, r], psum[:, r, 0:FE], ACT.Silu).then_inc(sg_ok, 1)

        def out_rows(r, n, free, row):
            act.wait_ge(dn_ps, n + 1)
            act.wait_ge(y_out[r], free)
            nc.scalar.activation(yb[:, r].rearrange("p (b c) -> p b c", b=2), psum[:, 2:4, :], ACT.Copy).then_inc(yb_ok, 1)
            act.wait_ge(yb_ok, n + 1)
            act.dma_start(row, yb[:, r]).then_inc(y_out[r], 16)

        x_chan(0, 1)
        x_chan(1, 2)
        gate_silu(0, 1)
        with act.Fori(0, pairs) as i:
            for j in range(2):
                r = 1 - j
                x_chan(j, i * 2 + (3 + j))
                gate_silu(r, i * 2 + (2 + j))
                out_rows(j, i * 2 + (1 + j), i * 16 + 16, y_dram[bass.ds(i * 256 + j * P, P)])
        out_rows(0, pairs * 2 + 1, pairs * 16 + 16, y_dram[bass.ds(pairs * 256, P)])

        for t in range(NT):
            act.wait_ge(y_in[t % NY], 32 * (t // NY + 1))
            nc.scalar.activation(y12[:, t % NY, 0], y12[:, t % NY, 0], ACT.Copy, scale=wtok[:, 0, t:t + 1]).then_inc(t_ok, 1)
            if t >= 1:
                final_square(t - 1)
        final_square(NT - 1)

    @block.tensor
    def _(pe):
        pe.wait_ge(ident_ok, 2)
        pe.wait_ge(rows_in, 32)
        nc.tensor.transpose(psum[:, 7, 0:NROWS1], rows1[:, :], ident[0:NROWS1, 0:NROWS1])
        nc.tensor.transpose(psum[:, 7, NROWS1:NROWS1 + ADA_FIRST], rows2[:, :], ident[0:ADA_FIRST, 0:ADA_FIRST]).then_inc(cols_ps, 1)

        def ada(out, r):
            for k in range(KD):
                last = nc.tensor.matmul(out, silc[:, k, :], raw[:, r, k], start=(k == 0), stop=(k == KD - 1))
            last.then_inc(ada_used, 1)

        pe.wait_ge(pos_in, 64)
        for s in range(NT - PT_TILES):
            if s >= 2:
                pe.wait_ge(x_pos, 2 * (s - 1))
            nc.tensor.matmul(psum[:, 4 + s % 2], possel[:, s, :], postab[:, :], start=True, stop=True)\
                .then_inc(posr_ps, 1)
        pe.wait_ge(silc_ok, 1)
        with pe.Fori(0, ADA_FIRST // 4) as i:
            for r in range(4):
                pe.wait_ge(raw_full[r], (i + 1) * 16)
                ada(psum[0:2, bass.ds(i, 1), r * P:(r + 1) * P].rearrange("p a n -> p (a n)"), r)
        pe.wait_ge(ada_ev, 4)
        for m in range(ADA_FIRST):
            last = nc.tensor.transpose(psum[:, 7, 2 * m:2 * m + 2], row1[:, m * P:(m + 1) * P], ident[0:2, 0:2])
        last.then_inc(cols_ps, 1)

        for h in range(2):
            n0 = h * NCH
            for k in range(KD):
                g = h * KD + k
                if k == 0:
                    pe.wait_ge(xn_ok, HTILES * (h + 1))
                if h == 1 and k == 0:
                    pe.wait_ge(cm_ev, NCH)
                if k >= 2:
                    pe.wait_ge(f_ok, 2 * (g - 1))
                for i in range(HTILES):
                    bank, col = (0, i) if i < 2 else (1, i - 2)
                    last = nc.tensor.transpose(psum[:, 2 * (k % 2) + bank, col * P:(col + 1) * P],
                                               xntile(h * HTILES + i)[:, k * P:(k + 1) * P], ident[:, :])
                last.then_inc(tr_ps, 1)

            def chunk(r, full_split, ev):
                pe.wait_ge(wsplit, full_split)
                if ev is not None:
                    pe.wait_ge(cm_ev, ev)
                for k in range(KD):
                    for wv, xv in ((0, 0), (0, 1), (1, 0)):
                        for g in range(2):
                            last = nc.tensor.matmul(psum[:, 2 * r + g, 0:GW], spl[:, r, wv, k],
                                                    hT[:, xv, k, g * GW:(g + 1) * GW],
                                                    start=(k == 0 and wv == 0 and xv == 0),
                                                    stop=(k == KD - 1 and wv == 1))
                last.then_inc(cm_ps, 1)

            pe.wait_ge(hT_ok, 2 * KD * (h + 1))
            chunk(n0 % 2, 2 * (n0 + 1), None)
            with pe.Fori(0, 7) as i:
                for j in range(2):
                    n = n0 + 1 + j
                    chunk(n % 2, i * 4 + 2 * (n + 1), i * 2 + (n - 1) if n > 1 else i * 2)
                    pe.wait_ge(raw_full[2 + j], i * 16 + 16 * (4 + 7 * h + 1))
                    pe.wait_ge(ada_ev, i * 2 + (14 * h + j + 3))
                    ada(psum[0:2, 6 + j, 0:P], 2 + j)

            def v_transposes(j):
                pe.wait_ge(cm_ev, n0 + V0 + j + 1)
                g = h * NH + j
                if g >= 1:
                    pe.wait_ge(v_ok, 2 * g)
                for i in range(HTILES):
                    bank, col = (4, i) if i < 2 else (5, i - 2)
                    last = nc.tensor.transpose(psum[:, bank, col * P:(col + 1) * P],
                                               fbuf[:, j % 2, i * P:(i + 1) * P], ident[:, :])
                last.then_inc(vtr_ps, 1)

            for j in range(NH):
                n = n0 + V0 + j
                chunk(n % 2, 2 * (n + 1), n - 1)
                if j >= 1:
                    v_transposes(j - 1)
            v_transposes(NH - 1)
            with pe.Fori(0, 2) as i:
                for j in range(2):
                    n = n0 + O0 + j
                    chunk(n % 2, i * 4 + 2 * (n + 1), i * 2 + (n - 1))
                    if h == 1:
                        pe.wait_ge(raw_full[2 + j], i * 16 + 16 * (4 + 14 + 1))
                        pe.wait_ge(ada_ev, i * 2 + (28 + j + 3))
                        ada(psum[0:2, 6 + j, 0:P], 2 + j)

        def mm(out, lhsT, rhs, start=True, stop=True, **kw_):
            return nc.tensor.matmul(out, lhsT, rhs, start=start, stop=stop, **kw_)

        pe.wait_ge(v_ok, 4 * NH)
        pe.wait_ge(ada_ev, 4 + NADA - ADA_FIRST)
        pe.wait_ge(const_ok, 1)
        for h in range(2):
            for g in range(2):
                for j in range(2):
                    last = mm(psum[:, 4 + 2 * h + g, 0:GW], onesd[:, :], PT[:, h, CA + j, g * GW:(g + 1) * GW], j == 0, j == 1)
            last.then_inc(mean_ps, 1)
        pe.wait_ge(misc_in, 80)
        pe.wait_ge(cm_ev, 2 * NCH)
        for t in range(NT):
            if t >= 4:
                pe.wait_ge(ab_ok, t - 3)
            h, cols = tile_cols(t)
            for j in range(2):
                last = mm(psum[:, t % 4, j * 256:(j + 1) * 256], PT[:, h, XA + j, cols], bdcs)
            last.then_inc(ab_ps, 1)
        pe.wait_ge(ab_ok, NT)

        def variance(h):
            pe.wait_ge(sq_ok, 2 * (h + 1))
            for g in range(2):
                for j in range(2):
                    last = mm(psum[:, 2 * h + g, 0:GW], onesd[:, :], sq[:, j, g * GW:(g + 1) * GW], j == 0, j == 1)
            last.then_inc(var_ps, 1)

        variance(0)
        pe.wait_ge(cen_ok, 4)
        for j in range(2):
            for t in range(PT_TILES):
                for v in range(2):
                    last = mm(psum[:, 4 + j, 0:TP], AB[:, t, v, j * P:(j + 1) * P], ctp[:, t, v, :], t + v == 0, t + v == 2)
        last.then_inc(yt_ps, 1)
        for i in range(TS // P):
            pe.wait_ge(ct_full[i % 4], 16 * (i // 4 + 1))
            for j in range(2):
                for v in range(2):
                    last = mm(psum[:, 6 + j, :], AB[:, PT_TILES + i, v, j * P:(j + 1) * P], cts[:, i % 4, v, :],
                              i + v == 0, i + v == TS // P)
            last.then_inc(ct_used, 1)
        pe.wait_ge(yt_ok, 1)
        for j in range(2):
            for i in range(TS // P):
                last = mm(psum[:, 4, j:j + 1], AB[:, PT_TILES + i, 0, j * P:(j + 1) * P], alt[:, :], i == 0, i == TS // P - 1)
        last.then_inc(yt_ps, 1)
        variance(1)

        def pointwise(h):
            pe.wait_ge(z_ok, 2 * (h + 1))
            if h == 1:
                pe.wait_ge(pw_ok, 2)
            for jo in range(2):
                for g in range(2):
                    for j in range(2):
                        last = mm(psum[:, 2 * jo + g, 0:GW], wpw[:, j, jo * P:(jo + 1) * P], PT[:, h, CA + j, g * GW:(g + 1) * GW],
                                  j == 0, j == 1)
            last.then_inc(pw_ps, 1)

        pe.wait_ge(yt_ok, 3)
        pe.wait_ge(var_ok, 2)
        for q, (bank, n, dst) in enumerate(FN):
            jo = q % 2
            kind = q // 2
            if q >= 4:
                pe.wait_ge(fn_ok, FN_DONE[q - 4])
            for j in range(2):
                rhs = (YT[:, j, 0:TP], YT[:, j, TP:TP + 512], YT[:, j, TP + 512:NK], YT[:, j, TP + 1:TP + 512][:, ::-1])[kind]
                last = mm(psum[:, bank, 0:n], wf[:, 1 if kind == 3 else 0, j, jo * P:(jo + 1) * P], rhs, j == 0, j == 1)
            last.then_inc(fn_ps, 1)
        pe.wait_ge(fn_ok, FN_DONE[-1])
        pointwise(0)
        pointwise(1)
        pe.wait_ge(gout, GOUT_ALL)
        for q, row in enumerate((LF, rowC, rowD, LI)):
            for t in range(NT):
                last = nc.tensor.transpose(psum[:, 4 + q, t * ROWG:(t + 1) * ROWG], row[:, t * P:(t + 1) * P],
                                           ident[0:ROWG, 0:ROWG])
            last.then_inc(gtr_ps, 1)

        pe.wait_ge(pw_ok, 4)
        pe.wait_ge(gcol_ok, 8)
        pe.wait_ge(ones_ok, 1)

        def scores(n):
            c, d, t = UNITS[n]
            h, cols = tile_cols(t)
            if n >= 1:
                pe.wait_ge(st_ok, n)
            for hd in range(NH):
                last = mm(psum[:, 0, hd * P:(hd + 1) * P], PT[:, h, KK + hd, cols], PT[:, h, QQ + hd, cols])
            last.then_inc(s_ps, 1)
            if n >= 1:
                pe.wait_ge(kw_ok, NH * n)
            for hd in range(NH):
                last = nc.tensor.transpose(psum[:, 1, hd * P:(hd + 1) * P], PT[:, h, KK + hd, cols], ident[:, :])
            last.then_inc(kt_ps, 1)

        scores(0)
        for n, (c, d, t) in enumerate(UNITS):
            h, cols = tile_cols(t)
            m = before(n)
            if m is None:
                pe.wait_ge(st_in, 64)
                pe.wait_ge(st_zero, 1)
            else:
                pe.wait_ge(c_ok, NH * (m + 1))
            if n >= 1:
                pe.wait_ge(t1_ok, NH * n)
            for hd in range(NH):
                last = mm(psum[:, 4 + hd // 2, (hd % 2) * E1:(hd % 2 + 1) * E1], PT[:, h, QQ + hd, cols], Cst[:, c, hd])
            last.then_inc(inter_ps, 1)
            if n + 1 < NU:
                scores(n + 1)
            pe.wait_ge(st_ok, n + 1)
            if n >= 1:
                pe.wait_ge(num_ok, n)
            for hd in range(NH):
                last = mm(psum[:, 2 + hd // 2, (hd % 2) * E1:(hd % 2 + 1) * E1], St[:, n % 2, hd], vaug[:, t, hd])
            last.then_inc(intra_ps, 1)
            pe.wait_ge(kw_ok, NH * (n + 1))
            if n >= 1:
                pe.wait_ge(c_ok, NH * n)
            for hd in range(NH):
                last = mm(psum[:, 6 + hd // 2, (hd % 2) * E1:(hd % 2 + 1) * E1], kw[:, n % 2, hd], vaug[:, t, hd])
            last.then_inc(u_ps, 1)
        for t in range(NT):
            pe.wait_ge(hn_ok, t + 1)
            if t == 0:
                pe.wait_ge(st_ok, NU)
                pe.wait_ge(kw_ok, NH * NU)
            if t >= 2:
                pe.wait_ge(mix_ok, NH * (t - 1))
            for hd in range(NH):
                last = nc.tensor.transpose(psum[:, t % 2, hd * P:(hd + 1) * P], Hd[:, 0, t, hd * HD:(hd + 1) * HD], ident[:, :])
            last.then_inc(htr_ps, 1)

        def route(t):
            pe.wait_ge(h2_ok, 2 * (t + 1))
            if t >= 1:
                pe.wait_ge(h2T_ok, t)
            for k in range(KD):
                last = nc.tensor.transpose(psum[:, 4 + k // 4, (k % 4) * P:(k % 4 + 1) * P], h2[:, t % 2, k * P:(k + 1) * P],
                                           ident[:, :])
            last.then_inc(h2tr_ps, 1)

        def logits(t):
            pe.wait_ge(h2T_ok, t + 1)
            for k in range(KD):
                last = mm(psum[:, 6, t * NE:(t + 1) * NE], h2T[t % 2][:, k], wr[:, k], k == 0, k == KD - 1)
            last.then_inc(lg_ps, 1)

        MIX = (0, 1, 2, 3, QQ, QQ + 1, QQ + 2, QQ + 3)
        pe.wait_ge(mix_ok, NH * NT)
        pe.wait_ge(wo_in, 16 * KD)
        pe.wait_ge(tab_in, 48)
        for t in range(NT):
            h, cols = tile_cols(t)
            if t >= 2:
                pe.wait_ge(x1_ok, 2 * t - 3)
            for g in range(2):
                for k in range(KD):
                    last = mm(psum[:, 2 * (t % 2) + g, :], PT[:, h, MIX[k], cols], wout(k)[:, g * 512:(g + 1) * 512],
                              k == 0, k == KD - 1)
            last.then_inc(o_ps, 1)
            if t >= 1:
                route(t - 1)
            if t >= 2:
                logits(t - 2)
        route(NT - 1)
        logits(NT - 2)
        logits(NT - 1)

        pe.wait_ge(rstep, ROUTE_A)
        pe.wait_ge(const_ok, 6)
        pe.wait_ge(tab_ok, 2)
        mm(psum[:, 0, 0:NT * NE], upper, taken, True, False)
        for q in range(1, NT):
            mm(psum[:, 0, q * NE:NT * NE], onesd[:, :], taken[:, 0:(NT - q) * NE], False, q == NT - 1)
        for q in range(NT):
            last = mm(psum[:, 1, 0:NE], onesd[:, :], taken[:, q * NE:(q + 1) * NE], q == 0, q == NT - 1)
        last.then_inc(pos_ps, 1)
        pe.wait_ge(onehot, 2)
        for q in range(2 * NT):
            last = mm(psum[:, 2, 0:NBLK], offhot[:, q], blkhot[:, q], q == 0, q == 2 * NT - 1)
        last.then_inc(tok_ps, 1)

        pe.wait_ge(route_ok, 1)
        pairs = pe.value_load(trip[0:1, 0:1], min_val=1, max_val=NBLK // 2 - 1)

        def x_trans(r, full, read):
            pe.wait_ge(xg_full[r], full)
            if read is not None:
                pe.wait_ge(xt_ok, read)
            for k in range(KD):
                last = nc.tensor.transpose(psum[:, 4 + k // 4, (k % 4) * P:(k % 4 + 1) * P], xg[:, r, k * P:(k + 1) * P], ident[:, :])
            last.then_inc(xt_ps, 1)

        def gate_up(r, blk, have):
            need = pe.value_load(eidI[0:1, blk], min_val=16 * WPART, max_val=16 * WPART * NE)
            off = pe.value_load(offI[0:1, blk], min_val=0, max_val=2 * WE)
            pe.wait_ge(w_full, need)
            pe.wait_ge(xt_ok, have)
            for k in range(KD):
                last = mm(psum[:, r, :], xT[:, r, k], wexp[:, bass.ds(off + k * 2 * FE, 2 * FE)], k == 0, k == KD - 1)
            last.then_inc(gu_ps, 1)
            return off

        def a_trans(r, n):
            pe.wait_ge(a_ok, n)
            for j in range(2):
                last = nc.tensor.transpose(psum[:, 6, j * P:(j + 1) * P], act_a[:, r, j * P:(j + 1) * P], ident[:, :])
            last.then_inc(at_ps, 1)

        def down(r, n, off):
            pe.wait_ge(at_ok, n)
            pe.wait_ge(yb_ok, n)
            for g in range(2):
                for j in range(2):
                    last = mm(psum[:, 2 + g, :], aT[:, r, j], wexp[:, bass.ds(off + (KD * 2 * FE + j * D + g * 512), 512)],
                              j == 0, j == 1)
            last.then_inc(dn_ps, 1)

        x_trans(0, 16, None)
        x_trans(1, 16, 1)
        gate_up(0, slice(0, 1), 1)
        with pe.Fori(0, pairs) as i:
            for j in range(2):
                prev = bass.ds(i * 2 + j, 1)
                a_trans(j, i * 2 + (1 + j))
                x_trans(j, i * 16 + 32, i * 2 + (2 + j))
                gate_up(1 - j, bass.ds(i * 2 + (1 + j), 1), i * 2 + (2 + j))
                off = pe.value_load(offI[0:1, prev], min_val=0, max_val=2 * WE)
                down(j, i * 2 + (1 + j), off)
        a_trans(0, pairs * 2 + 1)
        off = pe.value_load(offI[0:1, bass.ds(pairs * 2, 1)], min_val=0, max_val=2 * WE)
        down(0, pairs * 2 + 1, off)

    @block.vector
    def _(dve):
        dve.wait_ge(cols_ps, 1)
        nc.vector.tensor_copy(colv[:, :], psum[:, 7, 0:NROWS1]).then_inc(cols_ok, 1)
        nc.vector.tensor_copy(bada[:, :], psum[:, 7, NROWS1:NROWS1 + ADA_FIRST]).then_inc(cols_ok, 1)
        dve.wait_ge(pos_in, 64)

        def add_pos(t):
            s = t - PT_TILES
            dve.wait_ge(x_in[t], 16)
            dve.wait_ge(posr_ps, s + 1)
            x = xtile(t)
            nc.vector.tensor_tensor(x[:, 0:512], x[:, 0:512], psum[:, 4 + s % 2], ALU.add).then_inc(x_pos, 1)
            nc.vector.tensor_tensor(x[:, 512:D], x[:, 512:D], poscol[:, :], ALU.add).then_inc(x_pos, 1)

        def norm(t):
            dve.wait_ge(rstd_ok, 2 * (t + 1))
            nc.vector.tensor_scalar(xntile(t), xtile(t), ss[:, 2, t:t + 1], None, ALU.mult).then_inc(xn_ok, 1)

        for t in range(PT_TILES, HTILES):
            add_pos(t)
        for t in range(HTILES):
            norm(t)
        for t in range(HTILES, NT):
            add_pos(t)
        for t in range(HTILES, NT):
            norm(t)
        dve.wait_ge(cols_ps, 2)
        dve.wait_ge(cols_ok, 2)
        bb = bada[:, :].unsqueeze(1).broadcast_to([P, 2, ADA_FIRST])
        nc.vector.tensor_tensor(mod[:, :, :], psum[:, 7, 0:2 * ADA_FIRST].rearrange("p (m s) -> p s m", s=2), bb, ALU.add).then_inc(mod_ok, 1)
        dve.wait_ge(mod_ok, 1)
        g1 = colv[:, C_G1:C_G1 + KD].unsqueeze(1).broadcast_to([P, 2, KD])
        nc.vector.tensor_scalar(sc1[:, :, :], mod[:, :, KD:2 * KD], 1.0, None, ALU.add).then_inc(mod_ok, 1)
        dve.wait_ge(mod_ok, 2)
        nc.vector.tensor_tensor(sc1[:, :, :], sc1[:, :, :], g1, ALU.mult).then_inc(mod_ok, 1)

        def split_input(h):
            for k in range(KD):
                g = h * KD + k
                dve.wait_ge(f_ok, 2 * (g + 1))
                if h == 1 and k == 0:
                    dve.wait_ge(cm_ps, NCH)
                nc.vector.tensor_copy(hT[:, 0, k], fbuf[:, k % 2]).then_inc(hT_ok, 1)
                dve.wait_ge(hT_ok, 2 * g + 1)
                nc.vector.tensor_tensor(hT[:, 1, k], fbuf[:, k % 2], hT[:, 0, k].bitcast(F32), ALU.subtract)\
                    .then_inc(hT_ok, 1)

        def taps(wcol, pieces, base):
            m = len(pieces)
            for q, (j, u, out, n) in enumerate(pieces):
                nc.vector.tensor_scalar(out, u[:, 0:n], colv[:, C_WDW + j:C_WDW + j + 1], colv[:, C_BDW + j:C_BDW + j + 1],
                                        ALU.mult, ALU.add).then_inc(conv, 1)
            with dve.Fori(1, TAPS) as i:
                for q, (j, u, out, n) in enumerate(pieces):
                    dve.wait_ge(conv, i * m + (base + q + 1 - m))
                    nc.vector.scalar_tensor_tensor(out, u[:, bass.ds(i, n)], colv[:, bass.ds(i * 2 + (C_WDW + j), 1)], out,
                                                   ALU.mult, ALU.add).then_inc(conv, 1)

        def mix_tile(t):
            h, cols = tile_cols(t)
            dve.wait_ge(htr_ps, t + 1)
            for hd in range(NH):
                nc.vector.scalar_tensor_tensor(PT[:, h, QQ + hd, cols], psum[:, t % 2, hd * P:(hd + 1) * P],
                                               colv[:, C_GMH + hd:C_GMH + hd + 1], PT[:, h, OO + hd, cols],
                                               ALU.mult, ALU.mult).then_inc(mix_ok, 1)

        split_input(0)
        dve.wait_ge(gt_sig, 1)
        dve.wait_ge(upad_ok, 1)
        nc.vector.tensor_tensor(uprompt[:, :, PAD:PAD + TP], PT[:, 0, CA:CA + 2, 0:TP], PT[:, 0, GT:GT + 2, 0:TP],
                                ALU.mult).then_inc(u_ok, 1)
        dve.wait_ge(u_ok, 1)
        taps(0, [(j, uprompt[:, j], PT[:, 0, CA + j, 0:TP], TP) for j in range(2)], 0)
        split_input(1)
        dve.wait_ge(gt_sig, 2)
        n1 = HT - TP
        nc.vector.memset(usample[:, :, 0:PAD], 0.0).then_inc(u_ok, 1)
        nc.vector.memset(usample[:, :, PAD + TS:], 0.0).then_inc(u_ok, 1)
        nc.vector.tensor_tensor(usample[:, :, PAD:PAD + n1], PT[:, 0, CA:CA + 2, TP:HT], PT[:, 0, GT:GT + 2, TP:HT],
                                ALU.mult).then_inc(u_ok, 1)
        nc.vector.tensor_tensor(usample[:, :, PAD + n1:PAD + TS], PT[:, 1, CA:CA + 2], PT[:, 1, GT:GT + 2],
                                ALU.mult).then_inc(u_ok, 1)
        dve.wait_ge(u_ok, 5)
        taps(0, [p for j in range(2) for p in ((j, usample[:, j], PT[:, 0, CA + j, TP:HT], n1),
                                               (j, usample[:, j, n1:], PT[:, 1, CA + j], HT))], 2 * TAPS)

        for h in range(2):
            dve.wait_ge(mean_ps, h + 1)
            if h == 0:
                dve.wait_ge(conv, CONV_ALL)
            for j in range(2):
                x = PT[:, h, CA + j].rearrange("p (g t) -> p g t", g=2)
                nc.vector.tensor_tensor(x, x, psum[:, 4 + 2 * h:6 + 2 * h, 0:GW], ALU.subtract).then_inc(cen_ok, 1)

        steps = [0]

        def link(ins):
            steps[0] += 1
            ins.then_inc(gstep, 1)
            dve.wait_ge(gstep, steps[0])

        SEQ = ((0, TP), (TP, T))

        dve.wait_ge(cm_ev, NCH + 1)
        dve.wait_ge(gates_ev, 2)
        dve.wait_ge(conv, CONV_ALL)
        link(nc.vector.memset(rowD, 0.0))
        link(nc.vector.memset(rowE, 0.0))
        link(nc.vector.tensor_copy(rowE[0:NH, :], LI[0:NH, :]))
        link(nc.vector.tensor_scalar(rowD[0:NH, :], LF[0:NH, :], gvec[0:NH, 1:2], None, ALU.add))
        bk = slice(32, 32 + NH)
        for c0, c1 in SEQ:
            link(nc.vector.tensor_copy(rowE[bk, c0:c1][:, ::-1], LI[bk, c0:c1]))
            link(nc.vector.tensor_scalar(rowD[bk, c0:c1][:, ::-1], LF[bk, c0:c1], gvec[bk, 1:2], None, ALU.add))
        dve.wait_ge(vtr_ps, 2 * NH)
        link(nc.vector.memset(rowC, 0.0))
        link(nc.vector.scalar_tensor_tensor(rowC, rowD, -1.0, rowD, ALU.mult, ALU.max))
        dve.wait_ge(cm_ps, 2 * NCH)
        link(nc.vector.memset(rowF, 1.0))
        link(nc.vector.memset(rowF[:, 0:T:P], 0.0))
        dve.wait_ge(gact, 2)
        link(nc.vector.scalar_tensor_tensor(rowD, rowD, 0.0, rowC, ALU.min, ALU.subtract))
        link(nc.vector.tensor_tensor_scan(rowC, rowF, rowD, 0.0, ALU.mult, ALU.add))
        link(nc.vector.tensor_tensor_scan(rowG[:, 0:TP], rowD[:, 0:TP], rowE[:, 0:TP], 0.0, ALU.add, ALU.max))
        link(nc.vector.tensor_tensor_scan(rowG[:, TP:T], rowD[:, TP:T], rowE[:, TP:T], gvec[:, 2:3], ALU.add, ALU.max))
        link(nc.vector.tensor_tensor(rowF, rowG, rowC, ALU.subtract))
        link(nc.vector.tensor_tensor(rowE, rowE, rowC, ALU.subtract))
        mprev, mlast, decs, deco = (small[:, i, :] for i in range(4))
        link(nc.vector.memset(mprev[:, 0:1], 0.0))
        link(nc.vector.tensor_copy(mprev[:, 1:2], rowG[:, P - 1:P]))
        link(nc.vector.tensor_copy(mprev[:, PT_TILES:PT_TILES + 1], gvec[:, 2:3]))
        link(nc.vector.tensor_copy(mprev[:, PT_TILES + 1:NT], rowG[:, TP + P - 1:T - 1:P]))
        link(nc.vector.tensor_copy(mlast, rowF[:, P - 1:T:P]))
        link(nc.vector.tensor_tensor(decs, mprev, mlast, ALU.subtract))
        fw = slice(0, NH)
        nc.vector.tensor_scalar(LI[fw, :], rowG[fw, :], -1.0, None, ALU.mult).then_inc(gout, 1)
        nc.vector.tensor_copy(LF[fw, :], rowE[fw, :]).then_inc(gout, 1)
        ch = lambda ap: ap.rearrange("p (c t) -> p c t", t=P)
        per = lambda ap, r, c0, c1: ap[r, c0 // P:c1 // P].unsqueeze(2).broadcast_to([NH, (c1 - c0) // P, P])
        nc.vector.tensor_tensor(ch(rowC[fw, :]), per(mprev, fw, 0, T), ch(rowF[fw, :]), ALU.subtract).then_inc(gout, 1)
        nc.vector.tensor_tensor(ch(rowD[fw, :]), ch(rowE[fw, :]), per(mlast, fw, 0, T), ALU.subtract).then_inc(gout, 1)
        for c0, c1 in SEQ:
            rev = lambda ap: ap[bk, c0:c1][:, ::-1]
            nc.vector.tensor_scalar(rev(LI), rowG[bk, c0:c1], -1.0, None, ALU.mult).then_inc(gout, 1)
            nc.vector.tensor_copy(rev(LF), rowE[bk, c0:c1]).then_inc(gout, 1)
            nc.vector.tensor_tensor(ch(rev(rowC)), per(mprev, bk, c0, c1), ch(rowF[bk, c0:c1]), ALU.subtract).then_inc(gout, 1)
            nc.vector.tensor_tensor(ch(rev(rowD)), ch(rowE[bk, c0:c1]), per(mlast, bk, c0, c1), ALU.subtract).then_inc(gout, 1)
        nc.vector.tensor_copy(deco[fw, :], decs[fw, :]).then_inc(gout, 1)
        nc.vector.tensor_copy(deco[bk, 0:PT_TILES][:, ::-1], decs[bk, 0:PT_TILES]).then_inc(gout, 1)
        nc.vector.tensor_copy(deco[bk, PT_TILES:][:, ::-1], decs[bk, PT_TILES:]).then_inc(gout, 1)
        dve.wait_ge(gout, 15)
        nc.vector.tensor_copy(decs[:, 0:1], rowG[:, TP - 1:TP]).then_inc(gout, 1)
        dve.wait_ge(gout, 16)
        nc.vector.tensor_scalar(rowG[fw, :], rowF[fw, :], -1.0, None, ALU.mult).then_inc(gout, 1)
        for c0, c1 in SEQ:
            nc.vector.tensor_scalar(rowG[bk, c0:c1][:, ::-1], rowF[bk, c0:c1], -1.0, None, ALU.mult).then_inc(gout, 1)

        for h in range(2):
            dve.wait_ge(var_ps, h + 1)
            nc.vector.tensor_scalar(sq[:, 0].rearrange("p (g t) -> p g t", g=2), psum[:, 2 * h:2 * h + 2, 0:GW], EPS, None,
                                    ALU.add).then_inc(var_ok, 1)
            dve.wait_ge(rst_ok, 2 * (h + 1))
            x = PT[:, h, CA:CA + 2]
            nc.vector.tensor_tensor(x, x, sq[:, 1].unsqueeze(1).broadcast_to([P, 2, HT]), ALU.mult).then_inc(scl_ok, 1)

        dve.wait_ge(gcol_ok, 8)
        nc.vector.tensor_scalar(gcol[:, 2], gcol[:, 2], SCALE, None, ALU.mult).then_inc(wcol_ok, 1)

        def decay_logs(n):
            c, d, t = UNITS[n]
            dve.wait_ge(nmb_in[n % 2], 16 * (n // 2 + 1))
            if n >= 2:
                dve.wait_ge(st_ok, n - 1)
            for hd in range(NH):
                nc.vector.scalar_tensor_tensor(Dm[:, n % 2, hd], nmb[:, n % 2, hd], gcol[:, 0, t, d, hd:hd + 1],
                                               (maskf if d == 0 else maskb)[:, :], ALU.add, ALU.min).then_inc(e_ok, 1)

        dve.wait_ge(const_ok, 5)
        dve.wait_ge(ada_used, NADA)
        dve.wait_ge(ct_used, TS // P)
        def decayed_scores(n):
            dve.wait_ge(exp_ok, n + 1)
            dve.wait_ge(s_ps, n + 1)
            if n >= 2:
                dve.wait_ge(intra_ps, n - 1)
            nc.vector.scalar_tensor_tensor(St[:, n % 2], psum[:, 0, :].rearrange("p (h t) -> p h t", h=NH), SCALE, Dm[:, n % 2],
                                           ALU.mult, ALU.mult).then_inc(st_ok, 1)

        decay_logs(0)
        decay_logs(1)
        decayed_scores(0)
        for n, (c, d, t) in enumerate(UNITS):
            if n + 1 < NU:
                decayed_scores(n + 1)
            if n + 2 < NU:
                decay_logs(n + 2)
            dve.wait_ge(u_ps, n + 1)
            if n == 0:
                dve.wait_ge(dec_ok, 1)
            for hd in range(NH):
                nc.vector.scalar_tensor_tensor(Cst[:, c, hd], Cst[:, c, hd], dec[:, d, hd, t:t + 1],
                                               psum[:, 6 + hd // 2, (hd % 2) * E1:(hd % 2 + 1) * E1],
                                               ALU.mult, ALU.add).then_inc(c_ok, 1)
            dve.wait_ge(intra_ps, n + 1)
            dve.wait_ge(t1_ok, NH * (n + 1))
            if n >= 1:
                dve.wait_ge(h_ok, n)
            nc.vector.tensor_tensor(numb[:, :, :].rearrange("p (b h) e -> p b h e", b=2),
                                    t1b[:, n % 2].rearrange("p (b h) e -> p b h e", b=2),
                                    psum[:, 2:4, 0:2 * E1].rearrange("p b (h e) -> p b h e", h=2), ALU.add).then_inc(num_ok, 1)
            dve.wait_ge(num_ok, n + 1)
            den = numb[:, :, HD]
            nc.vector.scalar_tensor_tensor(dens[:, 0], den, -1.0, den, ALU.mult, ALU.max).then_inc(den_ok, 1)
            dve.wait_ge(den_ok, 3 * n + 1)
            nc.vector.tensor_tensor(dens[:, 1], dens[:, 0], gcol[:, 3, t, d], ALU.max).then_inc(den_ok, 1)
            dve.wait_ge(den_ok, 3 * n + 2)
            nc.vector.reciprocal(dens[:, 2], dens[:, 1]).then_inc(den_ok, 1)
        dve.wait_ge(so_ok, 2)
        for t in range(NT):
            h, cols = tile_cols(t)
            dve.wait_ge(hrs_ok, 2 * (t + 1))
            x = Hd[:, 0, t].rearrange("p (h e) -> p h e", h=NH)
            nc.vector.tensor_tensor(x, x, hss[:, 2, t].unsqueeze(2).broadcast_to([P, NH, HD]), ALU.mult).then_inc(hn_ok, 1)
            if t >= 1:
                mix_tile(t - 1)
        mix_tile(NT - 1)

        dve.wait_ge(rows_b, 16 * 7)
        for q in range(2):
            nc.vector.scalar_tensor_tensor(A2[:, q], A2[:, q], 1.0, g2row, ALU.add, ALU.mult).then_inc(ab2_ok, 1)

        def normed(t):
            q = 0 if t < PT_TILES else 1
            dve.wait_ge(rs2_ok, 2 * (t + 1))
            if t == 0:
                dve.wait_ge(ab2_ok, 2)
            if t >= 2:
                dve.wait_ge(h2tr_ps, t - 1)
            nc.vector.scalar_tensor_tensor(h2[:, t % 2], x1[:, t], ss[:, 2, t:t + 1], A2[:, q], ALU.mult, ALU.mult).then_inc(h2_ok, 1)
            dve.wait_ge(h2_ok, 2 * t + 1)
            nc.vector.tensor_tensor(h2[:, t % 2], h2[:, t % 2], B2[:, q], ALU.add).then_inc(h2_ok, 1)

        for t in range(NT):
            q = 0 if t < PT_TILES else 1
            dve.wait_ge(o_ps, t + 1)
            if t == 0:
                dve.wait_ge(htr_ps, NT)
            nc.vector.tensor_tensor(x1[:, t].rearrange("p (b c) -> p b c", b=2), psum[:, 2 * (t % 2):2 * (t % 2) + 2, :],
                                    ga1[:, q].rearrange("p (b c) -> p b c", b=2), ALU.mult).then_inc(x1_ok, 1)
            dve.wait_ge(x1_ok, 2 * t + 1)
            dve.wait_ge(x_in[t], 32)
            nc.vector.tensor_tensor(x1[:, t], x1[:, t], xr[:, t % NX], ALU.add).then_inc(x1_ok, 1)
            normed(t)

        rsteps = [0]

        def then(ins):
            rsteps[0] += 1
            ins.then_inc(rstep, 1)
            dve.wait_ge(rstep, rsteps[0])

        NG = NT * NGRP
        for i in range(1, EPG):
            if i == 1:
                dve.wait_ge(conv, 2 * TAPS)
                then(nc.vector.memset(ties, 0.0))
            then(nc.vector.memset(ties[:, i, 0:i], 1.0))
        dve.wait_ge(sig_ok, 1)
        dve.wait_ge(tab_in, 48)

        def ranks(dst, vals, n):
            other = vals.rearrange("p (n j) -> p n j", j=EPG).unsqueeze(2).broadcast_to([P, n, EPG, EPG])
            self_ = vals.rearrange("p (n i) -> p n i", i=EPG).unsqueeze(3).broadcast_to([P, n, EPG, EPG])
            four = lambda w: w[:, 0:n * EPG * EPG].rearrange("p (n i j) -> p n i j", i=EPG, j=EPG)
            then(nc.vector.tensor_tensor(four(cmp_gt), other, self_, ALU.is_gt))
            then(nc.vector.tensor_tensor(four(cmp_eq), other, self_, ALU.is_equal))
            then(nc.vector.tensor_tensor(four(cmp_eq), four(cmp_eq), ties.unsqueeze(1).broadcast_to([P, n, EPG, EPG]), ALU.mult))
            then(nc.vector.tensor_tensor(four(cmp_gt), four(cmp_gt), four(cmp_eq), ALU.add))
            then(nc.vector.tensor_reduce(dst, cmp_gt[:, 0:n * EPG * EPG].rearrange("p (n j) -> p n j", j=EPG), AX.X, ALU.add))

        te = lambda ap: ap.rearrange("p (t e) -> p t e", e=NE)
        then(nc.vector.tensor_tensor(te(selv), te(score), brow.unsqueeze(1).broadcast_to([P, NT, NE]), ALU.add))
        ranks(rank, selv, NG)
        then(nc.vector.tensor_scalar(hot1, rank, 2.0, None, ALU.is_lt))
        then(nc.vector.tensor_tensor(hot2, hot1, selv, ALU.mult))
        then(nc.vector.tensor_reduce(gsum, hot2.rearrange("p (n j) -> p n j", j=EPG), AX.X, ALU.add))
        ranks(grank, gsum, NT)
        then(nc.vector.tensor_scalar(gbest, grank, 0.0, None, ALU.is_equal))
        gb4 = gbest.unsqueeze(2).broadcast_to([P, NG, EPG])
        ge = lambda ap: ap.rearrange("p (n j) -> p n j", j=EPG)
        for hot, r in ((hot1, 0.0), (hot2, 1.0)):
            then(nc.vector.tensor_scalar(hot, rank, r, None, ALU.is_equal))
            then(nc.vector.tensor_tensor(ge(hot), ge(hot), gb4, ALU.mult))
        then(nc.vector.tensor_tensor(taken, hot1, hot2, ALU.add))
        assert rsteps[0] == ROUTE_A
        for j, hot in enumerate((hot1, hot2)):
            then(nc.vector.tensor_tensor(tmp16, hot, score, ALU.mult))
            then(nc.vector.tensor_reduce(wtok[:, j], te(tmp16), AX.X, ALU.add))
        then(nc.vector.tensor_tensor(wsum, wtok[:, 0], wtok[:, 1], ALU.add))
        then(nc.vector.reciprocal(wsum, wsum))
        then(nc.vector.tensor_tensor(wtok[:, :, :], wtok[:, :, :], wsum.unsqueeze(1).broadcast_to([P, 2, NT]), ALU.mult))
        dve.wait_ge(pos_ps, 1)
        then(nc.vector.tensor_copy(counts, psum[:, 1, 0:NE]))
        eb = big[:, 0:NE * NT].rearrange("p (e b) -> p e b", b=NT)
        then(nc.vector.tensor_tensor(eb, counts.unsqueeze(2).broadcast_to([P, NE, NT]),
                                     b128[:, 0:NT].unsqueeze(1).broadcast_to([P, NE, NT]), ALU.is_gt))
        then(nc.vector.tensor_reduce(nblk, eb, AX.X, ALU.add))
        then(nc.vector.memset(counts, 1.0))
        then(nc.vector.tensor_tensor_scan(ends, counts, nblk, 0.0, ALU.mult, ALU.add))
        then(nc.vector.tensor_tensor(counts, ends, nblk, ALU.subtract))
        then(nc.vector.tensor_scalar(counts, counts, float(P), None, ALU.mult))
        then(nc.vector.tensor_tensor(te(tmp16), te(psum[:, 0, 0:NT * NE]), counts.unsqueeze(1).broadcast_to([P, NT, NE]), ALU.add))
        for j, hot in enumerate((hot1, hot2)):
            then(nc.vector.tensor_tensor(hot, hot, tmp16, ALU.mult))
            then(nc.vector.tensor_reduce(slotf[:, j * NT:(j + 1) * NT], te(hot), AX.X, ALU.add))
        then(nc.vector.tensor_copy(slotU[:, :, :].rearrange("p j t -> p (j t)"), slotf))
        N2 = 2 * NT
        ge37 = big[:, 0:N2 * 37].rearrange("p (n b) -> p n b", b=37)
        then(nc.vector.tensor_tensor(ge37, slotf.unsqueeze(2).broadcast_to([P, N2, 37]), b128.unsqueeze(1).broadcast_to([P, N2, 37]),
                                     ALU.is_ge))
        then(nc.vector.tensor_reduce(blkf, ge37, AX.X, ALU.add))
        then(nc.vector.tensor_tensor(blkhot, ge37[:, :, 0:36], ge37[:, :, 1:37], ALU.subtract))
        for j in range(2):
            sl = blkhot[:, j * NT:(j + 1) * NT]
            then(nc.vector.tensor_tensor(sl, sl, tokid.unsqueeze(2).broadcast_to([P, NT, NBLK]), ALU.mult))
        nc.vector.tensor_scalar(blkf, blkf, -float(P), float(P), ALU.mult, ALU.add).then_inc(onehot, 1)
        dve.wait_ge(onehot, 1)
        then(nc.vector.tensor_tensor(slotf, slotf, blkf, ALU.add))
        nc.vector.tensor_tensor(offhot, slotf.unsqueeze(2).broadcast_to([P, N2, P]), iota.unsqueeze(1).broadcast_to([P, N2, P]),
                                ALU.is_equal).then_inc(onehot, 1)
        dve.wait_ge(onehot, 2)
        ee = big[:, 0:NBLK * 15].rearrange("p (b e) -> p b e", e=15)
        then(nc.vector.tensor_tensor(ee, ends[:, 0:15].unsqueeze(1).broadcast_to([P, NBLK, 15]),
                                     iota[:, 0:NBLK].unsqueeze(2).broadcast_to([P, NBLK, 15]), ALU.is_le))
        then(nc.vector.tensor_reduce(eidf, ee, AX.X, ALU.add))
        then(nc.vector.tensor_scalar(eidI[:, :], eidf, 16.0 * WPART, 16.0 * WPART, ALU.mult, ALU.add))
        then(nc.vector.tensor_tensor(ee, ee, mod3[:, 0:15].unsqueeze(1).broadcast_to([P, NBLK, 15]), ALU.mult))
        then(nc.vector.tensor_reduce(eidf, ee, AX.X, ALU.add))
        then(nc.vector.tensor_scalar(offI[:, :], eidf, float(WE), None, ALU.mult))
        then(nc.vector.tensor_scalar(endI[:, :], ends, 1.0, None, ALU.add))
        then(nc.vector.tensor_scalar(eidf[:, 0:17], iota[:, 1:35:2], ends[:, 15:16], None, ALU.is_lt))
        then(nc.vector.tensor_reduce(gsum[:, 0:1], eidf[:, 0:17], AX.X, ALU.add))
        then(nc.vector.tensor_copy(trip[:, :], gsum[:, 0:1]))
        nc.vector.memset(idxU[:, NBLK:NBLK + 1], 0).then_inc(dn_ps, 1)
        nc.vector.memset(wsum, 0.0).then_inc(yb_ok, 1)
        nc.vector.memset(counts, 0.0).then_inc(y_out[0], 16)
        nc.vector.memset(nblk, 0.0).then_inc(y_out[1], 16)
        dve.wait_ge(tok_ps, 1)
        then(nc.vector.tensor_copy(idxU[:, 0:NBLK], psum[:, 2, 0:NBLK]))
        nc.vector.nop().then_inc(route_ok, 1)

        pairs = dve.value_load(trip[0:1, 0:1], min_val=1, max_val=NBLK // 2 - 1)

        def product(r, n):
            dve.wait_ge(sg_ok, n)
            nc.vector.tensor_tensor(act_a[:, r], act_g[:, r], psum[:, r, FE:2 * FE], ALU.mult).then_inc(a_ok, 1)

        def a_chan(r, n):
            dve.wait_ge(at_ps, n)
            nc.vector.tensor_copy(aT[:, r].rearrange("p j t -> p (j t)"), psum[:, 6, 0:2 * P]).then_inc(at_ok, 1)

        product(0, 1)
        with dve.Fori(0, pairs) as i:
            for j in range(2):
                a_chan(j, i * 2 + (1 + j))
                product(1 - j, i * 2 + (2 + j))
        a_chan(0, pairs * 2 + 1)

        dve.wait_ge(y_out[0], pairs * 16 + 32)
        dve.wait_ge(y_out[1], pairs * 16 + 16)
        nc.vector.memset(wsum, 0.0).then_inc(y_all, 1)
        dve.wait_ge(rows_c, 48)

        def out_norm(t):
            dve.wait_ge(rs3_ok, 2 * (t + 1))
            if t >= 3:
                dve.wait_ge(ob_out[t % 3], 16 * (t // 3))
            nc.vector.scalar_tensor_tensor(outb[:, t % 3], x2[:, t % 2], ss[:, 2, t:t + 1], fg, ALU.mult, ALU.mult).then_inc(o_ok, 1)

        for t in range(NT):
            q = 0 if t < PT_TILES else 1
            dve.wait_ge(t_ok, t + 1)
            y = y12[:, t % NY]
            nc.vector.scalar_tensor_tensor(y[:, 1], y[:, 1], wtok[:, 1, t:t + 1], y[:, 0], ALU.mult, ALU.add).then_inc(fstep, 1)
            dve.wait_ge(fstep, 2 * t + 1)
            if t >= 2:
                dve.wait_ge(o_ok, t - 1)
                dve.wait_ge(sq3_ok, t - 1)
            nc.vector.tensor_tensor(x2[:, t % 2], y[:, 1], ga2[:, q], ALU.mult).then_inc(fstep, 1)
            dve.wait_ge(fstep, 2 * t + 2)
            nc.vector.tensor_tensor(x2[:, t % 2], x2[:, t % 2], x1[:, t], ALU.add).then_inc(x2_ok, 1)
            if t >= 1:
                out_norm(t - 1)
        out_norm(NT - 1)

    ctx.close()


def host_arrays(x):
    f = np.float32
    cut = np.ascontiguousarray
    w_in = np.asarray(x["w_in"])[0]
    w_ada = np.asarray(x["w_ada"])[0]

    def chunked(w):
        return cut(w.reshape(KD, P, -1, P).transpose(2, 1, 0, 3))

    gates = np.zeros((D, P), f)
    gb = np.zeros((ROWG, 3), f)
    b_gate = np.asarray(x["b_gate"])[0]
    for d in range(2):
        for kind in range(2):
            src = 2816 + d * 8 + kind * 4
            gates[:, 64 * kind + 32 * d:64 * kind + 32 * d + 4] = w_in[:, src:src + 4]
            gb[32 * d:32 * d + 4, kind] = b_gate[d * 8 + kind * 4:d * 8 + kind * 4 + 4]
        gb[32 * d:32 * d + 4, 2] = np.asarray(x["state_m"])[0, 0, d]
    arrays = {
        "w_ada": chunked(w_ada),
        "w_in": chunked(np.concatenate([gates, w_in[:, :2816]], axis=1)),
        "gvec": gb,
        "rows1": cut(np.concatenate([
            np.asarray(x[n]).reshape(-1, P) for n in
            ("c_ctx", "c", "norm1_g", "b_dw", "conv_ln_g", "conv_ln_b", "g_mh", "w_dw")])),
        "rows2": cut(np.asarray(x["b_ada"]).reshape(-1, P)[:ADA_FIRST]),
        "x_prompt": np.asarray(x["x_prompt"])[0],
        "x_sample": np.asarray(x["x_sample"])[0],
    }
    rest = np.asarray(x["b_ada"]).reshape(-1, P)[ADA_FIRST:]
    arrays["b_ada64"] = cut(np.concatenate([rest[0:14], rest[28:32]]).reshape(-1))
    arrays["b_ada96"] = cut(rest[14:28].reshape(-1))
    quarter = D // 4
    omega = (1.0 / (f(10000.0) ** (np.arange(quarter, dtype=f) / f(quarter)))).astype(f)

    def enc(n):
        ang = (np.arange(n, dtype=f)[:, None] * omega[None, :]).astype(f)
        return np.concatenate([np.sin(ang), np.cos(ang)], axis=-1).astype(f)

    arrays["postab"] = enc(TS // GRID_W)
    arrays["poscol"] = cut(np.tile(enc(GRID_W), (P // GRID_W, 1)))
    def angles(n, rows, cols):
        return 2 * np.pi * ((rows[:, None] * cols[None, :]) % n) / n

    ch = angles(64, np.arange(64), np.arange(64))
    bd = np.zeros((P, 2, P), f)
    for i in range(2):
        bd[64 * i:64 * i + 64, 0, 64 * i:64 * i + 64] = np.cos(ch) / 8
        bd[64 * i:64 * i + 64, 1, 64 * i:64 * i + 64] = np.sin(ch) / 8
    arrays["bdcs"] = bd.reshape(P, 2 * P)
    an = angles(TP, np.arange(TP), np.arange(TP))
    arrays["ctp"] = cut(np.stack([np.cos(an), -np.sin(an)], 1).astype(f).reshape(2, P, 2, TP).transpose(1, 0, 2, 3) / f(16))
    an = angles(TS, np.arange(TS), np.arange(TS // 2))
    arrays["cts"] = cut(np.stack([np.cos(an), -np.sin(an)], 1).astype(f).reshape(TS // P, P, 2, TS // 2) / f(32))
    arrays["alt"] = (((-1.0) ** np.arange(P)) / 32).astype(f)[:, None]
    wfn = np.asarray(x["w_fnet"])[0]
    neg = np.array([(c // 64) * 64 + (-c) % 64 for c in range(256)])
    arrays["wf"] = cut(np.stack([wfn, wfn[neg]]).reshape(2, 2, P, 256).transpose(2, 0, 1, 3))
    arrays["wpw"] = cut(np.asarray(x["w_pw"])[0].reshape(2, P, 256).transpose(1, 0, 2))
    arrays["state_C"] = np.asarray(x["state_C"])[0, 0]
    arrays["state_n"] = np.asarray(x["state_n"])[0, 0]
    sel = np.zeros((16, TS // P, P), f)
    for i in range(TS // P):
        for p in range(P):
            sel[i * 2 + p // GRID_W, i, p] = 1.0
    arrays["possel"] = sel
    arrays["w_out"] = np.asarray(x["w_out"])[0].reshape(KD, P, D)
    arrays["norm2_g"] = np.asarray(x["norm2_g"])[0]
    arrays["final_g"] = np.asarray(x["final_g"])
    arrays["w_router"] = cut(np.asarray(x["w_router"]).reshape(KD, P, NE).transpose(1, 0, 2))
    arrays["tables"] = np.concatenate([np.arange(37) * 128.0, np.where(np.arange(NE) % 3 == 2, -2.0, 1.0), np.asarray(x["b_router"]),
                                       np.arange(P)]).astype(f)
    arrays["tokid"] = cut(np.arange(T, dtype=f).reshape(NT, P).T)
    wg, wu, wd = (np.asarray(x[n])[0] for n in ("w_exp_gate", "w_exp_up", "w_exp_down"))
    gu = np.concatenate([wg, wu], axis=2).reshape(NE, KD, P, 2 * FE).transpose(0, 2, 1, 3).reshape(NE, P, -1)
    arrays["w_exp"] = cut(np.concatenate([gu, wd.reshape(NE, 2, P, D).transpose(0, 2, 1, 3).reshape(NE, P, -1)], axis=2))
    return {f"in_{n}": v for n, v in arrays.items()}


OUTS = [((1, TP, D), "float32"), ((1, TS, D), "float32"), ((1, 1, 2, NH, HD, HD), "float32"),
        ((1, 1, 2, NH, HD), "float32"), ((1, 1, 2, NH), "float32")]


def kernel(**inputs):
    from concourse import bacc
    from concourse.bass_utils import run_bass_kernel_spmd

    nc = bacc.Bacc("TRN2", target_bir_lowering=False, num_devices=1)
    arrays = host_arrays(inputs)
    a = {n[3:]: nc.dram_tensor(n, v.shape, mybir.dt.from_np(v.dtype), kind="ExternalInput").ap() for n, v in arrays.items()}
    o = [nc.dram_tensor(f"out_{i}", s, mybir.dt.from_np(np.dtype(d)), kind="ExternalOutput").ap()
         for i, (s, d) in enumerate(OUTS)]
    program(nc, a, o)
    r = run_bass_kernel_spmd(nc, [arrays], core_ids=[0])
    return tuple(r.results[0][f"out_{i}"] for i in range(len(OUTS)))
```

```python
import numpy as np
import concourse.bass as bass
from concourse import mybir
from contextlib import ExitStack

F32 = mybir.dt.float32
F32R = mybir.dt.float32r
I32 = mybir.dt.int32
BF16 = mybir.dt.bfloat16
U32 = mybir.dt.uint32
ALU = mybir.AluOpType
ACT = mybir.ActivationFunctionType
AX = mybir.AxisListType

P = 128
D = 1024
KD = D // P
TP, TS = 256, 1024
T = TP + TS
NT = T // P
PT_TILES = TP // P
HT = T // 2
HTILES = NT // 2
GW = HT // 2
NH, HD = 4, 128
NE, NGRP, EPG = 16, 4, 4
FE = 256
TAPS, PAD = 31, 15
EPS = 1e-6
GRID_W = 64
NCH = 23
XA, CA, GT, QQ, KK, OO = 0, 2, 4, 6, 10, 14
NSLOT = 18
NADA = 48
ADA_FIRST = 16
ROWG = 36
NBLK = 36
NBMIN = 2 * T // P + 1
NEG = -1.0e30

C_CTX, C_C, C_G1, C_BDW, C_LNG, C_LNB, C_GMH, C_WDW = 0, 8, 16, 24, 26, 28, 30, 34
NROWS1 = C_WDW + 2 * TAPS


def program(nc, a, o):
    ctx = ExitStack()

    def sbuf(name, shape, dt=F32):
        return ctx.enter_context(nc.sbuf_tensor(name, shape, dt))

    def sem(name):
        return ctx.enter_context(nc.semaphore(name))

    with nc.sbuf_tensor("input_parts", [P, 8 * T], F32R) as input_parts, nc.sbuf_tensor("weight_parts", [P, 4 * D], F32R) as weight_parts:
        hT = input_parts[:, :].rearrange("p (v k t) -> p v k t", v=2, k=KD)
        spl = weight_parts[:, :].rearrange("p (r v k n) -> p r v k n", r=2, v=2, k=KD)
    RA = sbuf("RA", [P, 8 * T])
    RS = sbuf("RS", [P, 4 * D])
    RB = sbuf("RB", [P, NSLOT * T])
    RC = sbuf("RC", [P, NT * NH * (HD + 1)])
    RW = sbuf("RW", [P, 4 * D])
    RE = sbuf("RE", [P, 3 * T])
    rows1 = sbuf("rows1", [NROWS1, P])
    rows2 = sbuf("rows2", [ADA_FIRST, P])
    ident = sbuf("ident", [P, P])
    colv = sbuf("colv", [P, NROWS1])
    bada = sbuf("bada", [P, ADA_FIRST])
    mod = sbuf("mod", [P, 2, ADA_FIRST])
    silc = sbuf("silc", [P, KD, 2])
    sc1 = sbuf("sc1", [P, 2, KD])
    gvec = sbuf("gvec", [ROWG, 3])
    ss = sbuf("ss", [P, 4, NT])
    mhalf = sbuf("mhalf", [P, NT])
    onesd = sbuf("onesd", [P, P])
    maskf = sbuf("maskf", [P, P])
    maskb = sbuf("maskb", [P, P])
    gcol = sbuf("gcol", [P, 4, NT, 2, NH])
    dec = sbuf("dec", [P, 2, NH, NT])
    small = sbuf("small", [ROWG, 4, NT])
    dens = sbuf("dens", [P, 4, NH])
    hss = sbuf("hss", [P, 3, NT, NH])
    uprompt = sbuf("uprompt", [P, 2, TP + 2 * PAD])

    PT = RB[:, :].rearrange("p (h s t) -> p h s t", h=2, s=NSLOT)
    vaug = RC[:, :].rearrange("p (t h e) -> p t h e", t=NT, h=NH)
    raw = RW[:, :].rearrange("p (r k n) -> p r k n", r=4, k=KD)
    LI = RE[0:ROWG, 0:T]
    LF = RE[0:ROWG, T:2 * T]
    fbuf = RE[:, 2 * T:3 * T].rearrange("p (b t) -> p b t", b=2)

    def xtile(t):
        h, i = divmod(t, HTILES)
        base = (h * NSLOT + (10 if h == 0 else 0)) * HT + i * D
        return RB[:, base:base + D]

    def xntile(t):
        h, i = divmod(t, HTILES)
        base = (h * NSLOT + (0 if h == 0 else 8)) * HT + i * D
        return RB[:, base:base + D]

    possel = RB[0:16, 8 * HT:8 * HT + D].rearrange("r (i p) -> r i p", p=P)
    posb = (NSLOT + 16) * HT
    postab = RB[0:16, posb:posb + 512]
    poscol = RB[:, posb + 512:posb + 1024]
    ub = (NSLOT + OO) * HT
    usample = RB[:, ub:ub + 2 * (TS + 2 * PAD)].rearrange("p (j t) -> p j t", j=2)

    psum = ctx.enter_context(nc.psum_tensor("psum", [P, 8, 512], F32))
    row1 = RE[0:2, 0:ADA_FIRST * P]
    MROWS = [(64, 0, 0, 14), (96, 0, 14, 28), (64, 14, 28, 32)]
    ROWS64, ROWS96 = 18 * P, 14 * P

    def modrow(b):
        part, place, c0, c1 = MROWS[b]
        return RE[part:part + 2, place * P:(place + c1 - c0) * P]


    AB = RA[:, 0:4 * T].rearrange("p (t v c) -> p t v c", t=NT, v=2)
    rowF = RA[0:ROWG, 4 * T:5 * T]
    rowG = RA[0:ROWG, 5 * T:6 * T]
    NK = TP + TS // 2 + 1
    YT = RA[:, 6 * T:6 * T + 2 * NK].rearrange("p (j k) -> p j k", j=2)
    rowC = RE[0:ROWG, 2 * T:3 * T]
    rowD = RB[0:ROWG, GT * HT:(GT + 2) * HT]
    rowE = RB[0:ROWG, (NSLOT + GT) * HT:(NSLOT + GT + 2) * HT]
    wf = RS[:, 0:1024].rearrange("p (v j c) -> p v j c", v=2, j=2)
    wpw = RS[:, 1024:1536].rearrange("p (j c) -> p j c", j=2)
    bdcs = RS[:, 1536:1792]
    ctp = RS[:, 1792:2816].rearrange("p (t v k) -> p t v k", t=2, v=2)
    sq = RS[:, 2816:2816 + 2 * HT].rearrange("p (j t) -> p j t", j=2)
    cts = RW[:, :].rearrange("p (r v k) -> p r v k", r=4, v=2)
    alt = sbuf("alt", [P, 1])
    ones1 = sbuf("ones1", [P, 1])
    Hd = RA[:, :].rearrange("p (d t e) -> p d t e", d=2, t=NT)
    nmb = RW[:, 0:1024].rearrange("p (b h t) -> p b h t", b=2, h=NH)
    Dm = RW[:, 1024:2048].rearrange("p (b h t) -> p b h t", b=2, h=NH)
    St = RW[:, 2048:3072].rearrange("p (b h t) -> p b h t", b=2, h=NH)
    kw = RW[:, 3072:4096].rearrange("p (b h t) -> p b h t", b=2, h=NH)
    E1 = HD + 1
    Cst = RE[:, 0:4 * NH * E1].rearrange("p (c h e) -> p c h e", c=4, h=NH)
    nb = 4 * NH * E1
    t1b = RE[:, nb:nb + 2 * NH * E1].rearrange("p (b h e) -> p b h e", b=2, h=NH)
    numb = RE[:, nb + 2 * NH * E1:nb + 3 * NH * E1].rearrange("p (h e) -> p h e", h=NH)
    SCALE = HD ** -0.5

    def wout(k):
        reg = RS if k < 4 else RC
        return reg[:, (k % 4) * D:(k % 4 + 1) * D]

    g2row = RC[:, 4 * D:5 * D]
    A2 = RW[:, 0:2 * D].rearrange("p (s c) -> p s c", s=2)
    B2 = RW[:, 2 * D:4 * D].rearrange("p (s c) -> p s c", s=2)
    rb = (NSLOT + 10) * HT
    ga1 = RB[:, rb:rb + 2 * D].rearrange("p (s c) -> p s c", s=2)
    ga2 = RB[:, rb + 2 * D:rb + 4 * D].rearrange("p (s c) -> p s c", s=2)
    fg = RB[:, rb + 4 * D:rb + 5 * D]
    NX = 2
    xr = RB[:, 10 * HT:10 * HT + NX * D].rearrange("p (b c) -> p b c", b=NX)
    x1 = RA[:, :].rearrange("p (t c) -> p t c", t=NT)
    h2 = RE[:, 0:2 * D].rearrange("p (b c) -> p b c", b=2)
    h2T = [RB[:, GT * HT:GT * HT + D].rearrange("p (k t) -> p k t", k=KD),
           RB[:, (NSLOT + GT) * HT:(NSLOT + GT) * HT + D].rearrange("p (k t) -> p k t", k=KD)]
    wr = sbuf("wr", [P, KD, NE])
    tabf = uprompt[:, :, :].rearrange("p a b -> p (a b)")
    upper = tabf[:, 0:P]
    NTAB = 37 + NE + NE + P
    CONSTB = tabf[:, P:P + NTAB]
    b128 = CONSTB[:, 0:37]
    mod3 = CONSTB[:, 37:37 + NE]
    brow = CONSTB[:, 37 + NE:37 + 2 * NE]
    iota = CONSTB[:, 37 + 2 * NE:NTAB]
    tokid = tabf[:, P + NTAB:P + NTAB + NT]
    ties = tabf[:, P + NTAB + NT:P + NTAB + NT + EPG * EPG].rearrange("p (i j) -> p i j", i=EPG)
    wtok = sbuf("wtok", [P, 2, NT])
    slotU = sbuf("slotU", [P, 2, NT], U32)
    idxU = sbuf("idxU", [P, NBLK + 1], U32)
    idxc = sbuf("idxc", [P, 2, 1], U32)
    eidI = sbuf("eidI", [P, NBLK], I32)
    offI = sbuf("offI", [P, NBLK], I32)
    endI = sbuf("endI", [P, NE], I32)
    trip = sbuf("trip", [P, 1], I32)
    WE = KD * 2 * FE + 2 * D
    WPART = 3
    wexp = RB[:, 0:3 * WE]
    xg = RW[:, 0:2 * D].rearrange("p (b c) -> p b c", b=2)
    xT = RW[:, 2 * D:4 * D].rearrange("p (b k t) -> p b k t", b=2, k=KD)
    mb = 3 * WE
    act_g = RB[:, mb:mb + 2 * FE].rearrange("p (b f) -> p b f", b=2)
    act_a = RB[:, mb + 2 * FE:mb + 4 * FE].rearrange("p (b f) -> p b f", b=2)
    aT = RB[:, mb + 4 * FE:mb + 6 * FE].rearrange("p (b j t) -> p b j t", b=2, j=2)
    assert mb + 6 * FE <= rb + 2 * D
    yb = RE[:, 0:2 * D].rearrange("p (b c) -> p b c", b=2)
    NY = 4
    diag = RC[:, 2 * D:2 * D + 2 * NT * P].rearrange("p (j t q) -> p j t q", j=2, t=NT)
    y12 = RB[:, 0:8 * D].rearrange("p (b j c) -> p b j c", b=NY, j=2)
    x2 = RB[:, 8 * D:10 * D].rearrange("p (b c) -> p b c", b=2)
    sqb = RB[:, 10 * D:12 * D].rearrange("p (b c) -> p b c", b=2)
    outb = RB[:, 12 * D:15 * D].rearrange("p (b c) -> p b c", b=3)
    h2_dram = nc.dram_tensor("h2_scratch", (T, D), F32, kind="Internal").ap()
    y_dram = nc.dram_tensor("y_scratch", (NBLK * P, D), F32, kind="Internal").ap()
    modrow_dram = nc.dram_tensor("modrow_scratch", (2, 32 * P), F32, kind="Internal").ap()

    brow_in = sem("brow_in")
    mrow_ok = sem("mrow_ok")
    mrow_out = sem("mrow_out")
    tab_in = sem("tab_in")
    tab_ok = sem("tab_ok")
    wo_in = sem("wo_in")
    rows_b = sem("rows_b")
    rows_c = sem("rows_c")
    ab2_ok = sem("ab2_ok")
    o_ps = sem("o_ps")
    x1_ok = sem("x1_ok")
    sq2_ok = sem("sq2_ok")
    rs2_ok = sem("rs2_ok")
    h2_ok = sem("h2_ok")
    h2_out = [sem("h2_out0"), sem("h2_out1")]
    h2tr_ps = sem("h2tr_ps")
    h2T_ok = sem("h2T_ok")
    lg_ps = sem("lg_ps")
    sig_ok = sem("sig_ok")
    rstep = sem("rstep")
    pos_ps = sem("pos_ps")
    onehot = sem("onehot")
    tok_ps = sem("tok_ps")
    route_ok = sem("route_ok")
    w_full = sem("w_full")
    idx_ok = sem("idx_ok")
    xg_full = [sem("xg_full0"), sem("xg_full1")]
    xt_ps = sem("xt_ps")
    xt_ok = sem("xt_ok")
    gu_ps = sem("gu_ps")
    sg_ok = sem("sg_ok")
    a_ok = sem("a_ok")
    at_ps = sem("at_ps")
    at_ok = sem("at_ok")
    dn_ps = sem("dn_ps")
    yb_ok = sem("yb_ok")
    y_out = [sem("y_out0"), sem("y_out1")]
    y_in = [sem(f"y_in{b}") for b in range(NY)]
    diag_ok = sem("diag_ok")
    comb_ps = sem("comb_ps")
    y_all = sem("y_all")
    fstep = sem("fstep")
    x2_ok = sem("x2_ok")
    sq3_ok = sem("sq3_ok")
    rs3_ok = sem("rs3_ok")
    o_ok = sem("o_ok")
    ob_out = [sem(f"ob_out{b}") for b in range(3)]

    rows_in = sem("rows_in")
    zero_out = sem("zero_out")
    pos_in = sem("pos_in")
    x_in = [sem(f"x_in{t}") for t in range(NT)]
    raw_full = [sem(f"raw_full{r}") for r in range(4)]
    ident_ok = sem("ident_ok")
    cols_ps = sem("cols_ps")
    cols_ok = sem("cols_ok")
    silc_ok = sem("silc_ok")
    ada_used = sem("ada_used")
    mod_ok = sem("mod_ok")
    ada_ev = sem("ada_ev")
    posr_ps = sem("posr_ps")
    x_pos = sem("x_pos")
    xs_out = sem("xs_out")
    ss_ok = sem("ss_ok")
    rstd_ok = sem("rstd_ok")
    xn_ok = sem("xn_ok")
    tr_ps = sem("tr_ps")
    f_ok = sem("f_ok")
    hT_ok = sem("hT_ok")
    wsplit = sem("wsplit")
    cm_ps = sem("cm_ps")
    cm_ev = sem("cm_ev")
    vtr_ps = sem("vtr_ps")
    v_ok = sem("v_ok")
    gates_ev = sem("gates_ev")
    gt_sig = sem("gt_sig")
    ones_ok = sem("ones_ok")
    upad_ok = sem("upad_ok")
    u_ok = sem("u_ok")
    conv = sem("conv")

    const_ok = sem("const_ok")
    misc_in = sem("misc_in")
    ct_full = [sem(f"ct_full{r}") for r in range(4)]
    ab_ps = sem("ab_ps")
    ab_ok = sem("ab_ok")
    yt_ps = sem("yt_ps")
    yt_ok = sem("yt_ok")
    fn_ps = sem("fn_ps")
    fn_ok = sem("fn_ok")
    ct_used = sem("ct_used")
    mean_ps = sem("mean_ps")
    cen_ok = sem("cen_ok")
    scl_ok = sem("scl_ok")
    sq_ok = sem("sq_ok")
    var_ps = sem("var_ps")
    var_ok = sem("var_ok")
    rst_ok = sem("rst_ok")
    z_ok = sem("z_ok")
    pw_ps = sem("pw_ps")
    pw_ok = sem("pw_ok")
    gstep = sem("gstep")
    gact = sem("gact")
    gout = sem("gout")
    gm_out = sem("gm_out")
    gtr_ps = sem("gtr_ps")
    gcol_ok = sem("gcol_ok")
    wcol_ok = sem("wcol_ok")
    dec_in = sem("dec_in")
    dec_ok = sem("dec_ok")
    st_in = sem("st_in")
    st_zero = sem("st_zero")
    nmb_in = [sem("nmb_in0"), sem("nmb_in1")]
    e_ok = sem("e_ok")
    exp_ok = sem("exp_ok")
    s_ps = sem("s_ps")
    kt_ps = sem("kt_ps")
    inter_ps = sem("inter_ps")
    intra_ps = sem("intra_ps")
    u_ps = sem("u_ps")
    st_ok = sem("st_ok")
    kw_ok = sem("kw_ok")
    t1_ok = sem("t1_ok")
    num_ok = sem("num_ok")
    den_ok = sem("den_ok")
    h_ok = sem("h_ok")
    c_ok = sem("c_ok")
    so_ok = sem("so_ok")
    hsum_ok = sem("hsum_ok")
    hsq_ok = sem("hsq_ok")
    hrs_ok = sem("hrs_ok")
    hn_ok = sem("hn_ok")
    htr_ps = sem("htr_ps")
    mix_ok = sem("mix_ok")
    out_done = sem("out_done")
    gm_dram = nc.dram_tensor("gm_scratch", (2, NH, T), F32, kind="Internal").ap()
    dec_dram = nc.dram_tensor("dec_scratch", (2, NH, NT), F32, kind="Internal").ap()

    UNITS = []
    for i in range(TS // P):
        UNITS += [(2, 0, PT_TILES + i), (3, 1, NT - 1 - i)]
        if i < PT_TILES:
            UNITS += [(0, 0, i), (1, 1, PT_TILES - 1 - i)]
    NU = len(UNITS)

    def before(n):
        return max((m for m in range(n) if UNITS[m][0] == UNITS[n][0]), default=None)

    DONE = sorted((max(n for n in range(NU) if UNITS[n][2] == t), t) for t in range(NT))
    TILE_Q = {t: q for q, (_, t) in enumerate(DONE)}

    def due(n, lag):
        last = n == NU - 1
        return [q for q, (m, _) in enumerate(DONE) if m + lag == n or (last and m + lag > n)]

    def tile_cols(t):
        h, i = divmod(t, HTILES)
        return h, slice(i * P, (i + 1) * P)

    SPAN0 = HT - TP

    xs_dram = nc.dram_tensor("xs_scratch", (TS, D), F32, kind="Internal").ap()

    V0 = 1 + 14
    O0 = V0 + NH
    CONV_ALL = 2 * TAPS + 4 * TAPS

    FN = []
    for q, (n, dst) in enumerate((
            (TP, [(0, TP, 0, 0)]),
            (512, [(0, SPAN0, 0, TP), (SPAN0, 512, 1, 0)]),
            (1, [(0, 1, 1, 512 - SPAN0)]),
            (511, [(0, 511, 1, 513 - SPAN0)]))):
        for j in range(2):
            FN.append(((2 * q + j) % 4, n, dst))

    GBANK = (0, 1, 4, 5)
    FN_ALL = len(FN)
    FN_DONE = [sum(len(f[2]) for f in FN[:q + 1]) for q in range(FN_ALL)]
    GOUT_ALL = 19

    place = [2 * D, 0, 0]

    def scratch(n, r=0):
        reg = (RE, RS, RC)[r]
        place[r] += n
        return reg[:, place[r] - n:place[r]]

    NTE = NT * NE
    score, selv, rank, hot1, hot2, taken, tmp16, cum = (scratch(NTE) for _ in range(8))
    gsum, grank, gbest = (scratch(NT * NGRP) for _ in range(3))
    counts, nblk, ends, total = (scratch(NE) for _ in range(4))
    slotf, blkf = scratch(2 * NT), scratch(2 * NT)
    wsum, eidf = scratch(NT), scratch(NBLK)
    BATCH = NT - 3
    free0 = 10 * HT + NX * D
    pairs_a = [RB[:, free0 + i * 4 * NE * BATCH:free0 + (i + 1) * 4 * NE * BATCH] for i in range(2)]
    pairs_b = [scratch(4 * NE * (NT - BATCH), 1) for _ in range(2)]
    big = scratch(2 * NT * 37, 1)
    diff = scratch(2 * NT * NBLK, 1).rearrange("p (n b) -> p n b", b=NBLK)
    offhot = scratch(NT * P, 2).bitcast(BF16).rearrange("p (n o) -> p n o", o=P)
    blkhot = scratch(2 * NT * NBLK, 2).bitcast(BF16).rearrange("p (n v b) -> p n v b", v=2, b=NBLK)
    assert place[0] <= 3 * T and place[1] <= 4 * D and place[2] <= 5 * D

    block = ctx.enter_context(nc.Block())

    @block.sync
    def _(sp):
        for r in range(4):
            sp.dma_start(raw[:, r], a["w_ada"][r]).then_inc(raw_full[r], 16)
        with sp.Fori(1, ADA_FIRST // 4) as i:
            for r in range(4):
                sp.wait_ge(ada_used, i * 4 + (r - 3))
                sp.dma_start(raw[:, r], a["w_ada"][bass.ds(i * 4 + r, 1)].rearrange("a p k n -> (a p) k n"))\
                  .then_inc(raw_full[r], 16)

        for h in range(2):
            n0 = h * NCH

            def load_proj(n, r, c, free):
                sp.wait_ge(wsplit, free)
                src = a["w_in"][c] if isinstance(c, int) else a["w_in"][bass.ds(c, 1)].rearrange("a p k n -> (a p) k n")
                sp.dma_start(raw[:, r], src).then_inc(raw_full[r], 16)

            def load_ada(i, r, used):
                sp.wait_ge(ada_used, used)
                src = a["w_ada"][bass.ds(i, 1)].rearrange("a p k n -> (a p) k n")
                sp.dma_start(raw[:, r], src).then_inc(raw_full[r], 16)

            if h == 0:
                sp.wait_ge(ada_used, ADA_FIRST - 3)
                sp.dma_start(raw[:, 0], a["w_in"][0]).then_inc(raw_full[0], 16)
                sp.wait_ge(ada_used, ADA_FIRST)
                sp.dma_start(raw[:, 1], a["w_in"][1]).then_inc(raw_full[1], 16)
                sp.dma_start(raw[:, 2], a["w_ada"][ADA_FIRST]).then_inc(raw_full[2], 16)
                first = 2
            else:
                load_proj(n0, n0 % 2, 0, 2 * (n0 - 1))
                first = 1
            if h == 0:
                load_proj(2, 0, 2, 2)
                sp.dma_start(raw[:, 3], a["w_ada"][ADA_FIRST + 1]).then_inc(raw_full[3], 16)
                start = 1
            else:
                start = 0
            with sp.Fori(start, 7) as i:
                for j in range(2):
                    load_proj(None, (n0 + 1 + j) % 2, i * 2 + (1 + j), i * 4 + 2 * (n0 + j))
                    load_ada(i * 2 + (ADA_FIRST + 14 * h + j), 2 + j, i * 2 + (ADA_FIRST + 14 * h + j - 1))
            for c in range(V0, O0):
                load_proj(None, (n0 + c) % 2, c, 2 * (n0 + c - 1))
            with sp.Fori(0, 2) as i:
                for j in range(2):
                    load_proj(None, (n0 + O0 + j) % 2, i * 2 + (O0 + j), i * 4 + 2 * (n0 + O0 + j - 1))
                    if h == 1:
                        load_ada(i * 2 + (ADA_FIRST + 28 + j), 2 + j, i * 2 + (ADA_FIRST + 28 + j - 1))

        sp.wait_ge(cm_ps, 2 * NCH)
        sp.dma_start(bdcs, a["bdcs"]).then_inc(misc_in, 16)
        sp.dma_start(ctp, a["ctp"]).then_inc(misc_in, 16)
        sp.dma_start(alt[:, :], a["alt"]).then_inc(misc_in, 16)
        sp.dma_start(wf, a["wf"]).then_inc(misc_in, 16)
        sp.dma_start(wpw, a["wpw"]).then_inc(misc_in, 16)
        for q in range(2):
            for n, p0 in ((ROWS64, 64), (ROWS96, 96)):
                src = a["b_ada64"] if p0 == 64 else a["b_ada96"]
                sp.dma_start(RA[p0 + q:p0 + q + 1, 4 * T:4 * T + n], src.rearrange("(a n) -> a n", a=1)).then_inc(brow_in, 16)
        sp.wait_ge(wsplit, 4 * NCH)
        sp.wait_ge(ada_used, NADA)
        for i in range(TS // P):
            if i >= 4:
                sp.wait_ge(ct_used, i - 3)
            sp.dma_start(cts[:, i % 4], a["cts"][i]).then_inc(ct_full[i % 4], 16)
        sp.wait_ge(mrow_ok, 2)
        for b in range(3):
            sp.dma_start(modrow_dram[:, MROWS[b][2] * P:MROWS[b][3] * P], modrow(b)).then_inc(mrow_out, 16)
        sp.wait_ge(conv, 2 * TAPS)
        sp.dma_start(CONSTB, a["tables"].partition_broadcast(P)).then_inc(tab_in, 16)
        sp.dma_start(tokid, a["tokid"]).then_inc(tab_in, 16)
        sp.dma_start(wr[:, :, :], a["w_router"]).then_inc(tab_in, 16)
        sp.wait_ge(gout, GOUT_ALL)
        for d in range(2):
            sp.dma_start(gm_dram[d], rowG[32 * d:32 * d + NH, :]).then_inc(gm_out, 16)
            sp.dma_start(dec_dram[d], small[32 * d:32 * d + NH, 3, :]).then_inc(gm_out, 16)
            sp.dma_start(o[4][0, 0, d:d + 1, :].rearrange("a h -> h a"), small[32 * d:32 * d + NH, 2, 0:1],
                         allow_slow_non_contiguous=True).then_inc(out_done, 16)
        sp.wait_ge(gm_out, 64)
        sp.dma_start(dec[:, :, :, :].rearrange("p d h t -> p (d h t)"),
                     dec_dram.rearrange("d h t -> (d h t)").partition_broadcast(P)).then_inc(dec_in, 16)
        sp.wait_ge(gtr_ps, 4)
        for d in range(2):
            sp.dma_start(Cst[:, 2 + d, :, 0:HD], a["state_C"][d].rearrange("h d e -> d h e")).then_inc(st_in, 16)
            sp.dma_start(Cst[:, 2 + d, :, HD:E1], a["state_n"][d].rearrange("h (d a) -> d h a", a=1),
                         allow_slow_non_contiguous=True).then_inc(st_in, 16)
        sp.wait_ge(ct_used, TS // P)
        for n, (c, d, t) in enumerate(UNITS):
            if n >= 2:
                sp.wait_ge(e_ok, NH * (n - 1))
            sp.dma_start(nmb[:, n % 2], gm_dram[d][:, t * P:(t + 1) * P].partition_broadcast(P)).then_inc(nmb_in[n % 2], 16)
            if n == 2:
                sp.wait_ge(pw_ps, 2)
                sp.wait_ge(fn_ps, FN_ALL)
                for k in range(4):
                    sp.dma_start(wout(k), a["w_out"][k]).then_inc(wo_in, 16)
        for c in range(2):
            last = max(n for n in range(NU) if UNITS[n][0] == c)
            sp.wait_ge(c_ok, NH * (last + 1))
            sp.dma_start(o[2][0, 0, c].rearrange("h d e -> d h e"), Cst[:, c, :, 0:HD]).then_inc(out_done, 16)
            sp.dma_start(o[3][0, 0, c].rearrange("h (d a) -> d h a", a=1), Cst[:, c, :, HD:E1],
                         allow_slow_non_contiguous=True).then_inc(out_done, 16)
        sp.wait_ge(u_ps, NU)
        for k in range(4, KD):
            sp.dma_start(wout(k), a["w_out"][k]).then_inc(wo_in, 16)
        sp.dma_start(g2row, a["norm2_g"].partition_broadcast(P)).then_inc(rows_b, 16)
        sp.wait_ge(mrow_out, 48)
        for q in range(2):
            sp.dma_start(A2[:, q], modrow_dram[q, 2 * D:3 * D].partition_broadcast(P)).then_inc(rows_b, 16)
            sp.dma_start(B2[:, q], modrow_dram[q, D:2 * D].partition_broadcast(P)).then_inc(rows_b, 16)
        for q in range(2):
            sp.dma_start(ga1[:, q], modrow_dram[q, 0:D].partition_broadcast(P)).then_inc(rows_b, 16)

        def load_x(t):
            src = a["x_prompt"][t * P:(t + 1) * P] if t < PT_TILES else xs_dram[(t - PT_TILES) * P:(t - PT_TILES + 1) * P]
            sp.dma_start(xr[:, t % NX], src).then_inc(x_in[t], 16)

        def store_h2(t):
            sp.wait_ge(h2_ok, 2 * (t + 1))
            sp.dma_start(h2_dram[t * P:(t + 1) * P], h2[:, t % 2]).then_inc(h2_out[t % 2], 16)

        for t in range(NX):
            load_x(t)
        for t in range(NT):
            if t + NX < NT:
                sp.wait_ge(x1_ok, 2 * (t + 1))
                load_x(t + NX)
            store_h2(t)
        sp.wait_ge(mix_ok, NH * NT)
        for q in range(2):
            sp.dma_start(ga2[:, q], modrow_dram[q, 3 * D:4 * D].partition_broadcast(P)).then_inc(rows_c, 16)
        sp.dma_start(fg, a["final_g"].partition_broadcast(P)).then_inc(rows_c, 16)
        WP = WE // WPART

        def load_expert(r, src, came):
            if came is not None:
                sp.wait_ge(w_full, came)
            for q in range(WPART):
                sp.dma_start(wexp[:, r * WE + q * WP:r * WE + (q + 1) * WP], src[:, q * WP:(q + 1) * WP]).then_inc(w_full, 16)

        sp.wait_ge(lg_ps, NT)
        for e in range(2):
            load_expert(e, a["w_exp"][e], 16 * WPART * e if e else None)
        sp.wait_ge(route_ok, 3)
        sp.wait_ge(xg_full[0], 16)
        sp.wait_ge(xg_full[1], 16)
        load_expert(2, a["w_exp"][2], 16 * WPART * 2)
        with sp.Fori(1, NE // 3) as i:
            for r in range(3):
                done = sp.value_load(endI[0:1, bass.ds(i * 3 + (r - 3), 1)], min_val=1, max_val=NBLK)
                sp.wait_ge(w_full, i * (48 * WPART) + 16 * WPART * r)
                sp.wait_ge(dn_ps, done)
                load_expert(r, a["w_exp"][bass.ds(i * 3 + r, 1)].rearrange("a p n -> (a p) n"), None)
        done = sp.value_load(endI[0:1, NE - 4:NE - 3], min_val=1, max_val=NBLK)
        sp.wait_ge(dn_ps, done)
        load_expert(0, a["w_exp"][NE - 1], 16 * WPART * (NE - 1))
        sp.wait_ge(out_done, 16 * 6)
        for t in range(NT):
            sp.wait_ge(o_ok, t + 1)
            dst = o[0][0, t * P:(t + 1) * P] if t < PT_TILES else o[1][0, (t - PT_TILES) * P:(t - PT_TILES + 1) * P]
            sp.dma_start(dst, outb[:, t % 3]).then_inc(ob_out[t % 3], 16)
        for b in range(3):
            sp.wait_ge(ob_out[b], 16 * len(range(b, NT, 3)))

    @block.gpsimd
    def _(gp):
        nc.gpsimd.memset(ident[:, :], 0.0).then_inc(ident_ok, 1)
        gp.wait_ge(ident_ok, 1)
        gp.affine_select(out=ident[:, :], in_=ident[:, :], compare_op=ALU.not_equal, fill=1.0, base=0,
                         pattern=[[-1, P]], channel_multiplier=1).then_inc(ident_ok, 1)
        nc.gpsimd.memset(mhalf[:, :], -0.5).then_inc(ident_ok, 1)
        nc.gpsimd.memset(ones1[:, :], 1.0).then_inc(ident_ok, 1)
        nc.gpsimd.memset(RC[:, 0:D], 0.0).then_inc(ident_ok, 1)
        nc.gpsimd.memset(uprompt[:, :, :], 0.0).then_inc(upad_ok, 1)
        nc.gpsimd.memset(onesd[:, :], 1.0 / 256).then_inc(const_ok, 1)
        nc.gpsimd.memset(maskf[:, :], 0.0).then_inc(const_ok, 1)
        nc.gpsimd.memset(maskb[:, :], 0.0).then_inc(const_ok, 1)
        gp.wait_ge(const_ok, 3)
        gp.affine_select(out=maskf[:, :], in_=maskf[:, :], compare_op=ALU.is_ge, fill=NEG, base=0,
                         pattern=[[1, P]], channel_multiplier=-1).then_inc(const_ok, 1)
        gp.affine_select(out=maskb[:, :], in_=maskb[:, :], compare_op=ALU.is_ge, fill=NEG, base=0,
                         pattern=[[-1, P]], channel_multiplier=1).then_inc(const_ok, 1)
        gp.wait_ge(ident_ok, 4)
        for t in range(NT):
            gp.wait_ge(ss_ok, t + 1)
            nc.gpsimd.tensor_scalar(ss[:, 1, t:t + 1], ss[:, 0, t:t + 1], 1.0 / D, EPS, ALU.mult, ALU.add)\
                .then_inc(rstd_ok, 1)
            gp.wait_ge(rstd_ok, 2 * t + 1)
            nc.gpsimd.tensor_tensor(ss[:, 2, t:t + 1], ss[:, 1, t:t + 1], mhalf[:, 0:1], ALU.pow)\
                .then_inc(rstd_ok, 1)

        def split(r, full, before, done):
            gp.wait_ge(raw_full[r], full)
            if before is not None:
                gp.wait_ge(cm_ps, before)
            nc.gpsimd.tensor_tensor(spl[:, r, 0], raw[:, r], ones1[:, :].unsqueeze(1).broadcast_to([P, KD, P]), ALU.mult).then_inc(wsplit, 1)
            gp.wait_ge(wsplit, done)
            nc.gpsimd.tensor_tensor(spl[:, r, 1], raw[:, r], spl[:, r, 0].bitcast(F32), ALU.subtract)\
                .then_inc(wsplit, 1)

        def head_sum(q):
            t = DONE[q][1]
            nc.gpsimd.tensor_tensor(Hd[:, 0, t], Hd[:, 0, t], Hd[:, 1, t], ALU.add).then_inc(hsum_ok, 1)

        def head_rms(q):
            t = DONE[q][1]
            gp.wait_ge(hsq_ok, NH * (q + 1))
            nc.gpsimd.tensor_scalar(hss[:, 1, t], hss[:, 0, t], 1.0 / HD, EPS, ALU.mult, ALU.add).then_inc(hrs_ok, 1)
            gp.wait_ge(hrs_ok, 2 * q + 1)
            nc.gpsimd.tensor_tensor(hss[:, 2, t], hss[:, 1, t], mhalf[:, 0:NH], ALU.pow).then_inc(hrs_ok, 1)

        for n in (0, 1):
            split(n, 16 * 5, None, 2 * n + 1)
        with gp.Fori(1, NCH) as i:
            for r in range(2):
                split(r, (i + 5) * 16, i * 2 + (r - 1), i * 4 + (2 * r + 1))

        gp.wait_ge(ada_ev, 4 + NADA - ADA_FIRST)
        gp.wait_ge(brow_in, 64)
        for p0, n in ((64, ROWS64), (96, ROWS96)):
            rows = RE[p0:p0 + 2, 0:n]
            nc.gpsimd.tensor_tensor(rows, rows, RA[p0:p0 + 2, 4 * T:4 * T + n], ALU.add).then_inc(mrow_ok, 1)
        gp.wait_ge(mrow_ok, 2)
        gp.wait_ge(zero_out, 16 * (NBLK - NBMIN))
        nc.gpsimd.memset(vaug[:, :, :, HD], 1.0).then_inc(ones_ok, 1)
        gp.wait_ge(gtr_ps, 4)
        gp.wait_ge(mrow_out, 48)
        nc.gpsimd.memset(Cst[:, 0:2], 0.0).then_inc(st_zero, 1)
        for n, (c, d, t) in enumerate(UNITS):
            gp.wait_ge(den_ok, 3 * (n + 1))
            if n == 0:
                gp.wait_ge(fn_ps, FN_ALL)
            nc.gpsimd.tensor_tensor(Hd[:, d, t].rearrange("p (h e) -> p h e", h=NH), numb[:, :, 0:HD],
                                    dens[:, 2, :].unsqueeze(2).broadcast_to([P, NH, HD]), ALU.mult).then_inc(h_ok, 1)
            for q in due(n, 0):
                gp.wait_ge(h_ok, n + 1)
                head_sum(q)
            for q in due(n, 2):
                head_rms(q)
        gp.wait_ge(var_ps, 2)
        nc.gpsimd.memset(onesd[:, :], 1.0).then_inc(const_ok, 1)
        gp.wait_ge(conv, 2 * TAPS)
        nc.gpsimd.memset(upper, 1.0).then_inc(tab_ok, 1)
        gp.wait_ge(tab_ok, 1)
        gp.affine_select(out=upper, in_=upper, compare_op=ALU.is_ge, fill=0.0, base=-1,
                         pattern=[[1, P]], channel_multiplier=-1).then_inc(tab_ok, 1)

        def root(src_ok, n, col, done):
            gp.wait_ge(src_ok, n)
            nc.gpsimd.tensor_scalar(ss[:, 1, col:col + 1], ss[:, 0, col:col + 1], 1.0 / D, EPS, ALU.mult, ALU.add).then_inc(done, 1)
            gp.wait_ge(done, 2 * n - 1)
            nc.gpsimd.tensor_tensor(ss[:, 2, col:col + 1], ss[:, 1, col:col + 1], mhalf[:, 0:1], ALU.pow).then_inc(done, 1)

        for t in range(NT):
            root(sq2_ok, t + 1, t, rs2_ok)

        def fetch(r):
            nc.gpsimd.indirect_dma_start(xg[:, r], None, h2_dram, bass.IndirectOffsetOnAxis(ap=idxc[:, r], axis=0))\
                .then_inc(xg_full[r], 16)

        gp.wait_ge(route_ok, 2)
        for b in range(2):
            gp.wait_ge(h2_out[b], 16 * (NT // 2))
        for r in range(2):
            nc.gpsimd.tensor_copy(idxc[:, r], idxU[:, r:r + 1]).then_inc(idx_ok, 1)
        for r in range(2):
            gp.wait_ge(idx_ok, r + 1)
            fetch(r)
        gp.wait_ge(xg_full[0], 16)
        nc.gpsimd.tensor_copy(idxc[:, 0], idxU[:, 2:3]).then_inc(idx_ok, 1)
        gp.wait_ge(route_ok, 3)
        pairs = gp.value_load(trip[0:1, 0:1], min_val=1, max_val=NBLK // 2 - 1)
        with gp.Fori(0, pairs) as i:
            for j in range(2):
                gp.wait_ge(xt_ps, i * 2 + (j + 1))
                gp.wait_ge(idx_ok, i * 2 + (3 + j))
                gp.wait_ge(xg_full[1 - j], i * 16 + 16 * (j + 1))
                nc.gpsimd.tensor_copy(idxc[:, 1 - j], idxU[:, bass.ds(i * 2 + (3 + j), 1)]).then_inc(idx_ok, 1)
                fetch(j)
        gp.wait_ge(y_all, 1)
        def fetch_outputs(t):
            for j in range(2):
                nc.gpsimd.indirect_dma_start(y12[:, t % NY, j], None, y_dram,
                                             bass.IndirectOffsetOnAxis(ap=slotU[:, j, t:t + 1], axis=0)).then_inc(y_in[t % NY], 16)

        for t in range(NY):
            fetch_outputs(t)
        for t in range(NT):
            if t + NY < NT:
                gp.wait_ge(comb_ps, t + 1)
                fetch_outputs(t + NY)
            root(sq3_ok, t + 1, t, rs3_ok)
    @block.scalar
    def _(act):
        def h2_transposed(t):
            act.wait_ge(h2tr_ps, t + 1)
            nc.scalar.activation(h2T[t % 2][:, :, :].rearrange("p (b k) t -> p b (k t)", b=2), psum[:, 4:6, :], ACT.Copy)\
                .then_inc(h2T_ok, 1)

        def final_square(t):
            act.wait_ge(x2_ok, t + 1)
            nc.scalar.activation(sqb[:, t % 2], x2[:, t % 2], ACT.Square, accum_out=ss[:, 0, t:t + 1]).then_inc(sq3_ok, 1)

        act.dma_start(rows1[:, :], a["rows1"]).then_inc(rows_in, 16)
        act.dma_start(rows2[:, :], a["rows2"]).then_inc(rows_in, 16)
        for t in range(PT_TILES):
            act.dma_start(xtile(t), a["x_prompt"][t * P:(t + 1) * P, :]).then_inc(x_in[t], 16)
        act.dma_start(possel[:, :, :], a["possel"]).then_inc(pos_in, 16)
        act.dma_start(postab[:, :], a["postab"]).then_inc(pos_in, 16)
        act.dma_start(poscol[:, :], a["poscol"]).then_inc(pos_in, 16)
        act.dma_start(gvec[:, :], a["gvec"]).then_inc(pos_in, 16)
        act.wait_ge(cols_ok, 1)
        nc.scalar.activation(silc[:, :, :], colv[:, C_CTX:C_G1].rearrange("p (s k) -> p k s", s=2), ACT.Silu)\
            .then_inc(silc_ok, 1)

        def load_sample(t0, t1):
            for t in range(t0, t1):
                act.dma_start(xtile(t), a["x_sample"][(t - PT_TILES) * P:(t - PT_TILES + 1) * P, :]).then_inc(x_in[t], 16)

        def store_sample(t):
            p0 = (t - PT_TILES) * P
            act.dma_start(xs_dram[p0:p0 + P, :], xtile(t)).then_inc(xs_out, 16)

        load_sample(PT_TILES, HTILES)
        def squares_of_input(t):
            if t < PT_TILES:
                act.wait_ge(x_in[t], 16)
            else:
                act.wait_ge(x_pos, 2 * (t - PT_TILES + 1))
            nc.scalar.activation(xntile(t), xtile(t), ACT.Square, accum_out=ss[:, 0, t:t + 1]).then_inc(ss_ok, 1)

        def first_rows(i):
            act.wait_ge(ada_used, 4 * (i + 1))
            nc.scalar.activation(row1[:, i * 512:(i + 1) * 512], psum[0:2, i, :], ACT.Copy).then_inc(ada_ev, 1)

        for t in range(HTILES):
            squares_of_input(t)
        first_rows(0)
        load_sample(HTILES, NT)
        first_rows(1)
        for t in range(HTILES, NT):
            squares_of_input(t)
        first_rows(2)
        first_rows(3)

        def ada_row(b, i, j, used):
            act.wait_ge(ada_used, used)
            nc.scalar.activation(modrow(b)[:, bass.ds(i, P)], psum[0:2, 6 + j, 0:P], ACT.Copy).then_inc(ada_ev, 1)

        def evac_half(h):
            if h == 0:
                act.wait_ge(mod_ok, 3)
            for k in range(KD):
                g = h * KD + k
                act.wait_ge(tr_ps, g + 1)
                if g >= 2:
                    act.wait_ge(hT_ok, 2 * (g - 1))
                for b, (c0, c1) in enumerate(((0, TP), (TP, HT))):
                    s = 0 if (h == 0 and b == 0) else 1
                    nc.scalar.activation(fbuf[:, k % 2, c0:c1], psum[:, 4 + 2 * (k % 2) + b, 0:c1 - c0], ACT.Identity,
                                         scale=sc1[:, s, k:k + 1], bias=mod[:, s, k:k + 1]).then_inc(f_ok, 1)

        def evac_chunk(n1, bank, dst):
            act.wait_ge(cm_ps, n1)
            nc.scalar.activation(dst, psum[:, bank:bank + 2, 0:GW], ACT.Copy).then_inc(cm_ev, 1)

        def slot_ap(h, s):
            if isinstance(s, int):
                return PT[:, h, s].rearrange("p (g t) -> p g t", g=2)
            return PT[:, h, bass.ds(s, 1)].rearrange("p a (g t) -> p (a g) t", g=2)

        for h in range(2):
            n0 = h * NCH
            evac_half(h)
            if h == 0:
                for t in range(PT_TILES, HTILES):
                    store_sample(t)
                act.wait_ge(ident_ok, 5)
                act.dma_start(y_dram[(NBLK - 1) * P:], RC[:, 0:D]).then_inc(zero_out, 16)
                assert NBLK - 1 - NBMIN == 14
            else:
                act.wait_ge(xs_out, 16 * (NT - PT_TILES))
            act.wait_ge(cm_ps, n0 + 1)
            if h == 0:
                act.wait_ge(pos_in, 64)
            bank = 2 * (n0 % 2)
            cols = slice(h * HT, (h + 1) * HT)
            nc.scalar.activation(LI[:, cols].rearrange("p (g t) -> p g t", g=2), psum[0:ROWG, bank:bank + 2, 0:GW],
                                 ACT.Identity, bias=gvec[:, 0:1]).then_inc(gates_ev, 1)
            nc.scalar.activation(LF[:, cols].rearrange("p (g t) -> p g t", g=2),
                                 psum[64:64 + ROWG, bank:bank + 2, 0:GW], ACT.Copy).then_inc(cm_ev, 1)
            with act.Fori(0, 3) as i:
                for j in range(2):
                    evac_chunk(i * 2 + (n0 + 2 + j), 2 * ((n0 + 1 + j) % 2), slot_ap(h, i * 2 + j))
                    ada_row(h, i * (2 * P) + j * P, j, i * 2 + (ADA_FIRST + 14 * h + j + 1))
                    if h == 0:
                        act.dma_start(y_dram[bass.ds(i * (2 * P) + (NBMIN + j) * P, P)], RC[:, 0:D]).then_inc(zero_out, 16)
            act.wait_ge(cm_ev, n0 + 7)
            nc.scalar.activation(PT[:, h, GT:GT + 2], PT[:, h, GT:GT + 2], ACT.Sigmoid).then_inc(gt_sig, 1)
            if h == 0:
                act.wait_ge(xs_out, 16 * (HTILES - PT_TILES))
            with act.Fori(3, 7) as i:
                for j in range(2):
                    evac_chunk(i * 2 + (n0 + 2 + j), 2 * ((n0 + 1 + j) % 2), slot_ap(h, i * 2 + j))
                    ada_row(h, i * (2 * P) + j * P, j, i * 2 + (ADA_FIRST + 14 * h + j + 1))
                    if h == 0:
                        act.dma_start(y_dram[bass.ds(i * (2 * P) + (NBMIN + j) * P, P)], RC[:, 0:D]).then_inc(zero_out, 16)

            def v_tokens(j):
                act.wait_ge(vtr_ps, h * NH + j + 1)
                if h == 0 and j == 0:
                    act.wait_ge(zero_out, 16 * (NBLK - NBMIN))
                nc.scalar.activation(vaug[:, 5 * h:5 * h + 2, j, 0:HD],
                                     psum[:, 4, 0:2 * P].rearrange("p (t e) -> p t e", e=HD), ACT.Copy).then_inc(v_ok, 1)
                nc.scalar.activation(vaug[:, 5 * h + 2:5 * h + 5, j, 0:HD],
                                     psum[:, 5, 0:3 * P].rearrange("p (t e) -> p t e", e=HD), ACT.Copy).then_inc(v_ok, 1)

            for j in range(NH):
                n = n0 + V0 + j
                if h == 0:
                    store_sample(HTILES + j)
                act.wait_ge(cm_ps, n + 1)
                if j == 0:
                    act.wait_ge(hT_ok, 2 * KD * (h + 1))
                if j >= 2:
                    act.wait_ge(vtr_ps, h * NH + j - 1)
                nc.scalar.activation(fbuf[:, j % 2].rearrange("p (g t) -> p g t", g=2),
                                     psum[:, 2 * (n % 2):2 * (n % 2) + 2, 0:GW], ACT.Copy).then_inc(cm_ev, 1)
                if j >= 1:
                    v_tokens(j - 1)
            v_tokens(NH - 1)
            if h == 0:
                store_sample(NT - 1)
            if h == 1:
                act.wait_ge(conv, CONV_ALL)
            with act.Fori(0, 2) as i:
                for j in range(2):
                    evac_chunk(i * 2 + (n0 + O0 + 1 + j), 2 * ((n0 + O0 + j) % 2), slot_ap(h, i * 2 + (OO + j)))
                    if h == 1:
                        ada_row(2, i * (2 * P) + j * P, j, i * 2 + (ADA_FIRST + 28 + j + 1))

        act.wait_ge(cm_ev, 2 * NCH)
        for h in range(2):
            nc.scalar.activation(PT[:, h, OO:OO + 4], PT[:, h, OO:OO + 4], ACT.Sigmoid).then_inc(so_ok, 1)
        for t in range(NT):
            act.wait_ge(ab_ps, t + 1)
            nc.scalar.activation(AB[:, t].rearrange("p v (j c) -> p j v c", j=2),
                                 psum[:, t % 4, :].rearrange("p (j v c) -> p j v c", j=2, v=2), ACT.Copy).then_inc(ab_ok, 1)
        def squares(h):
            act.wait_ge(cen_ok, 2 * (h + 1))
            if h == 1:
                act.wait_ge(scl_ok, 1)
            for j in range(2):
                nc.scalar.activation(sq[:, j], PT[:, h, CA + j], ACT.Square).then_inc(sq_ok, 1)

        def conv_silu(h):
            act.wait_ge(var_ok, h + 1)
            nc.scalar.activation(sq[:, 0], sq[:, 0], ACT.Ln).then_inc(rst_ok, 1)
            act.wait_ge(rst_ok, 2 * h + 1)
            nc.scalar.activation(sq[:, 1], sq[:, 0], ACT.Exp, scale=-0.5).then_inc(rst_ok, 1)
            act.wait_ge(scl_ok, h + 1)
            for j in range(2):
                nc.scalar.activation(PT[:, h, CA + j], PT[:, h, CA + j], ACT.Silu, scale=colv[:, C_LNG + j:C_LNG + j + 1],
                                     bias=colv[:, C_LNB + j:C_LNB + j + 1]).then_inc(z_ok, 1)

        squares(0)
        act.wait_ge(gstep, 10)
        nc.scalar.activation(rowC, rowC, ACT.Exp, scale=-1.0).then_inc(gact, 1)
        act.wait_ge(gact, 1)
        nc.scalar.activation(rowC, rowC, ACT.Ln, bias=1.0).then_inc(gact, 1)
        act.wait_ge(yt_ps, 1)
        nc.scalar.activation(YT[:, :, 0:TP], psum[:, 4:6, 0:TP], ACT.Copy).then_inc(yt_ok, 1)
        conv_silu(0)
        squares(1)
        for q in range(4):
            act.wait_ge(gtr_ps, q + 1)
            src = psum[:, GBANK[q], 0:NT * ROWG].rearrange("p (t r) -> p t r", r=ROWG)
            for d in range(2):
                nc.scalar.activation(gcol[:, q, :, d, :], src[:, :, 32 * d:32 * d + NH], ACT.Copy if q == 0 else ACT.Exp)\
                    .then_inc(gcol_ok, 1)
        act.wait_ge(dec_in, 16)
        nc.scalar.activation(dec[:, :, :, :], dec[:, :, :, :], ACT.Exp).then_inc(dec_ok, 1)
        conv_silu(1)
        act.wait_ge(ct_used, TS // P)
        nc.scalar.activation(YT[:, :, TP:TP + 512], psum[:, 6:8, :], ACT.Copy).then_inc(yt_ok, 1)
        act.wait_ge(yt_ps, 2)
        nc.scalar.activation(YT[:, :, TP + 512:NK], psum[:, 4, 0:2].unsqueeze(2), ACT.Copy).then_inc(yt_ok, 1)
        for h in range(2):
            act.wait_ge(pw_ps, h + 1)
            for j in range(2):
                nc.scalar.activation(PT[:, h, CA + j].rearrange("p (g t) -> p g t", g=2), psum[:, 2 * j:2 * j + 2, 0:GW], ACT.Copy)\
                    .then_inc(pw_ok, 1)
        for q, (bank, n, dst) in enumerate(FN):
            act.wait_ge(fn_ps, q + 1)
            for (c0, c1, h, col) in dst:
                nc.scalar.activation(PT[:, h, XA + q % 2, col:col + c1 - c0], psum[:, bank, c0:c1], ACT.Copy).then_inc(fn_ok, 1)
        act.wait_ge(wcol_ok, 1)
        def decays(n):
            act.wait_ge(e_ok, NH * (n + 1))
            nc.scalar.activation(Dm[:, n % 2], Dm[:, n % 2], ACT.Exp).then_inc(exp_ok, 1)

        decays(0)
        decays(1)
        for n, (c, d, t) in enumerate(UNITS):
            act.wait_ge(kt_ps, n + 1)
            if n >= 2:
                act.wait_ge(u_ps, n - 1)
            for hd in range(NH):
                nc.scalar.activation(kw[:, n % 2, hd], psum[:, 1, hd * P:(hd + 1) * P], ACT.Copy,
                                     scale=gcol[:, 2, t, d, hd:hd + 1]).then_inc(kw_ok, 1)
            act.wait_ge(inter_ps, n + 1)
            if n >= 2:
                act.wait_ge(num_ok, n - 1)
            for hd in range(NH):
                nc.scalar.activation(t1b[:, n % 2, hd], psum[:, 4 + hd // 2, (hd % 2) * E1:(hd % 2 + 1) * E1], ACT.Copy,
                                     scale=gcol[:, 1, t, d, hd:hd + 1]).then_inc(t1_ok, 1)
            if n + 2 < NU:
                decays(n + 2)
            for q in due(n, 1):
                ft = DONE[q][1]
                act.wait_ge(hsum_ok, q + 1)
                for hd in range(NH):
                    nc.scalar.activation(Hd[:, 1, ft, hd * HD:(hd + 1) * HD], Hd[:, 0, ft, hd * HD:(hd + 1) * HD], ACT.Square,
                                         accum_out=hss[:, 0, ft, hd:hd + 1]).then_inc(hsq_ok, 1)
        for t in range(NT):
            act.wait_ge(x1_ok, 2 * (t + 1))
            if t >= 2:
                act.wait_ge(h2_out[t % 2], 16 * (t // 2))
            nc.scalar.activation(h2[:, t % 2], x1[:, t], ACT.Square, accum_out=ss[:, 0, t:t + 1]).then_inc(sq2_ok, 1)
            if t == NT - 2:
                act.wait_ge(lg_ps, BATCH)
                nc.scalar.activation(score[:, 0:BATCH * NE], psum[:, 6, 0:BATCH * NE], ACT.Sigmoid).then_inc(sig_ok, 1)
            h2_transposed(t)
        act.wait_ge(lg_ps, NT)
        nc.scalar.activation(score[:, BATCH * NE:], psum[:, 7, BATCH * NE:NTE], ACT.Sigmoid).then_inc(sig_ok, 1)

        act.wait_ge(route_ok, 3)
        pairs = act.value_load(trip[0:1, 0:1], min_val=1, max_val=NBLK // 2 - 1)

        def x_chan(r, n):
            act.wait_ge(xt_ps, n)
            nc.scalar.activation(xT[:, r].rearrange("p (b k) t -> p b (k t)", b=2), psum[:, 4:6, :], ACT.Copy).then_inc(xt_ok, 1)

        def gate_silu(r, n):
            act.wait_ge(gu_ps, n)
            nc.scalar.activation(act_g[:, r], psum[:, r, 0:FE], ACT.Silu).then_inc(sg_ok, 1)

        def out_rows(r, n, free, row):
            act.wait_ge(dn_ps, n + 1)
            act.wait_ge(y_out[r], free)
            nc.scalar.activation(yb[:, r].rearrange("p (b c) -> p b c", b=2), psum[:, 2:4, :], ACT.Copy).then_inc(yb_ok, 1)
            act.wait_ge(yb_ok, n + 1)
            act.dma_start(row, yb[:, r]).then_inc(y_out[r], 16)

        x_chan(0, 1)
        x_chan(1, 2)
        gate_silu(0, 1)
        with act.Fori(0, pairs) as i:
            for j in range(2):
                r = 1 - j
                x_chan(j, i * 2 + (3 + j))
                gate_silu(r, i * 2 + (2 + j))
                out_rows(j, i * 2 + (1 + j), i * 16 + 16, y_dram[bass.ds(i * 256 + j * P, P)])
        out_rows(0, pairs * 2 + 1, pairs * 16 + 16, y_dram[bass.ds(pairs * 256, P)])

        for t in range(NT):
            final_square(t)

    @block.tensor
    def _(pe):
        pe.wait_ge(ident_ok, 2)
        pe.wait_ge(rows_in, 32)
        nc.tensor.transpose(psum[:, 7, 0:NROWS1], rows1[:, :], ident[0:NROWS1, 0:NROWS1])
        nc.tensor.transpose(psum[:, 7, NROWS1:NROWS1 + ADA_FIRST], rows2[:, :], ident[0:ADA_FIRST, 0:ADA_FIRST]).then_inc(cols_ps, 1)

        def ada(out, r):
            for k in range(KD):
                last = nc.tensor.matmul(out, silc[:, k, :], raw[:, r, k], start=(k == 0), stop=(k == KD - 1))
            last.then_inc(ada_used, 1)

        def positions(s0, s1):
            for s in range(s0, s1):
                if s >= 2:
                    pe.wait_ge(x_pos, 2 * (s - 1))
                nc.tensor.matmul(psum[:, 4 + s % 2], possel[:, s, :], postab[:, :], start=True, stop=True)\
                    .then_inc(posr_ps, 1)

        def first_ada(i):
            for r in range(4):
                pe.wait_ge(raw_full[r], (i + 1) * 16)
                ada(psum[0:2, bass.ds(i, 1), r * P:(r + 1) * P].rearrange("p a n -> p (a n)"), r)

        pe.wait_ge(silc_ok, 1)
        first_ada(0)
        pe.wait_ge(pos_in, 64)
        positions(0, HTILES - PT_TILES)
        first_ada(1)
        positions(HTILES - PT_TILES, NT - PT_TILES)
        with pe.Fori(2, ADA_FIRST // 4) as i:
            first_ada(i)
        pe.wait_ge(ada_ev, 4)
        for m in range(ADA_FIRST):
            last = nc.tensor.transpose(psum[:, 7, 2 * m:2 * m + 2], row1[:, m * P:(m + 1) * P], ident[0:2, 0:2])
        last.then_inc(cols_ps, 1)

        for h in range(2):
            n0 = h * NCH
            def input_transposes(k):
                g = h * KD + k
                if k == 0:
                    pe.wait_ge(xn_ok, HTILES * (h + 1))
                    pe.wait_ge(x_pos, 2 * (NT - PT_TILES)) if h == 0 else pe.wait_ge(v_ok, 2 * NH)
                if k == 1:
                    pe.wait_ge(mod_ok, 1) if h == 0 else pe.wait_ge(ada_ev, 4 + 14)
                if k >= 2:
                    pe.wait_ge(f_ok, 2 * (g - 1))
                for i in range(HTILES):
                    bank, col = (4, i) if i < 2 else (5, i - 2)
                    last = nc.tensor.transpose(psum[:, 2 * (k % 2) + bank, col * P:(col + 1) * P],
                                               xntile(h * HTILES + i)[:, k * P:(k + 1) * P], ident[:, :])
                last.then_inc(tr_ps, 1)

            def chunk(r, full_split, ev, first=False):
                pe.wait_ge(wsplit, full_split)
                if ev is not None:
                    pe.wait_ge(cm_ev, ev)
                for k in range(KD):
                    if first:
                        if k + 2 < KD:
                            input_transposes(k + 2)
                        pe.wait_ge(hT_ok, 2 * (KD * h + k + 1))
                    for wv, xv in ((0, 0), (0, 1), (1, 0)):
                        for g in range(2):
                            last = nc.tensor.matmul(psum[:, 2 * r + g, 0:GW], spl[:, r, wv, k],
                                                    hT[:, xv, k, g * GW:(g + 1) * GW],
                                                    start=(k == 0 and wv == 0 and xv == 0),
                                                    stop=(k == KD - 1 and wv == 1))
                last.then_inc(cm_ps, 1)

            input_transposes(0)
            input_transposes(1)
            chunk(n0 % 2, 2 * (n0 + 1), n0 - 1 if h else None, True)
            with pe.Fori(0, 7) as i:
                for j in range(2):
                    n = n0 + 1 + j
                    chunk(n % 2, i * 4 + 2 * (n + 1), i * 2 + (n - 1) if n > 1 else i * 2)
                    pe.wait_ge(raw_full[2 + j], i * 16 + 16 * (4 + 7 * h + 1))
                    pe.wait_ge(ada_ev, i * 2 + (14 * h + j + 3))
                    ada(psum[0:2, 6 + j, 0:P], 2 + j)

            def v_transposes(j):
                pe.wait_ge(cm_ev, n0 + V0 + j + 1)
                g = h * NH + j
                if g >= 1:
                    pe.wait_ge(v_ok, 2 * g)
                for i in range(HTILES):
                    bank, col = (4, i) if i < 2 else (5, i - 2)
                    last = nc.tensor.transpose(psum[:, bank, col * P:(col + 1) * P],
                                               fbuf[:, j % 2, i * P:(i + 1) * P], ident[:, :])
                last.then_inc(vtr_ps, 1)

            for j in range(NH):
                n = n0 + V0 + j
                chunk(n % 2, 2 * (n + 1), n - 1)
                if j >= 1:
                    v_transposes(j - 1)
            v_transposes(NH - 1)
            with pe.Fori(0, 2) as i:
                for j in range(2):
                    n = n0 + O0 + j
                    chunk(n % 2, i * 4 + 2 * (n + 1), i * 2 + (n - 1))
                    if h == 1:
                        pe.wait_ge(raw_full[2 + j], i * 16 + 16 * (4 + 14 + 1))
                        pe.wait_ge(ada_ev, i * 2 + (28 + j + 3))
                        ada(psum[0:2, 6 + j, 0:P], 2 + j)

        def mm(out, lhsT, rhs, start=True, stop=True, **kw_):
            return nc.tensor.matmul(out, lhsT, rhs, start=start, stop=stop, **kw_)

        pe.wait_ge(v_ok, 4 * NH)
        pe.wait_ge(ada_ev, 4 + NADA - ADA_FIRST)
        pe.wait_ge(const_ok, 1)
        for h in range(2):
            for g in range(2):
                for j in range(2):
                    last = mm(psum[:, 4 + 2 * h + g, 0:GW], onesd[:, :], PT[:, h, CA + j, g * GW:(g + 1) * GW], j == 0, j == 1)
            last.then_inc(mean_ps, 1)
        pe.wait_ge(misc_in, 80)
        pe.wait_ge(cm_ev, 2 * NCH)
        for t in range(NT):
            if t >= 4:
                pe.wait_ge(ab_ok, t - 3)
            h, cols = tile_cols(t)
            for j in range(2):
                last = mm(psum[:, t % 4, j * 256:(j + 1) * 256], PT[:, h, XA + j, cols], bdcs)
            last.then_inc(ab_ps, 1)
        pe.wait_ge(ab_ok, NT)

        def variance(h):
            pe.wait_ge(sq_ok, 2 * (h + 1))
            for g in range(2):
                for j in range(2):
                    last = mm(psum[:, 2 * h + g, 0:GW], onesd[:, :], sq[:, j, g * GW:(g + 1) * GW], j == 0, j == 1)
            last.then_inc(var_ps, 1)

        def gate_columns():
            pe.wait_ge(gout, GOUT_ALL)
            pe.wait_ge(yt_ok, 1)
            pe.wait_ge(var_ok, 1)
            for q, row in enumerate((LF, rowC, rowD, LI)):
                for t in range(NT):
                    last = nc.tensor.transpose(psum[:, GBANK[q], t * ROWG:(t + 1) * ROWG], row[:, t * P:(t + 1) * P],
                                               ident[0:ROWG, 0:ROWG])
                last.then_inc(gtr_ps, 1)

        variance(0)
        pe.wait_ge(cen_ok, 4)
        for j in range(2):
            for t in range(PT_TILES):
                for v in range(2):
                    last = mm(psum[:, 4 + j, 0:TP], AB[:, t, v, j * P:(j + 1) * P], ctp[:, t, v, :], t + v == 0, t + v == 2)
        last.then_inc(yt_ps, 1)
        for i in range(TS // P):
            if i == 6:
                gate_columns()
                variance(1)
            pe.wait_ge(ct_full[i % 4], 16 * (i // 4 + 1))
            for j in range(2):
                for v in range(2):
                    last = mm(psum[:, 6 + j, :], AB[:, PT_TILES + i, v, j * P:(j + 1) * P], cts[:, i % 4, v, :],
                              i + v == 0, i + v == TS // P)
            last.then_inc(ct_used, 1)
        pe.wait_ge(gcol_ok, 8)
        for j in range(2):
            for i in range(TS // P):
                last = mm(psum[:, 4, j:j + 1], AB[:, PT_TILES + i, 0, j * P:(j + 1) * P], alt[:, :], i == 0, i == TS // P - 1)
        last.then_inc(yt_ps, 1)

        def pointwise(h):
            pe.wait_ge(z_ok, 2 * (h + 1))
            if h == 1:
                pe.wait_ge(pw_ok, 2)
            for jo in range(2):
                for g in range(2):
                    for j in range(2):
                        last = mm(psum[:, 2 * jo + g, 0:GW], wpw[:, j, jo * P:(jo + 1) * P], PT[:, h, CA + j, g * GW:(g + 1) * GW],
                                  j == 0, j == 1)
            last.then_inc(pw_ps, 1)

        pe.wait_ge(var_ok, 2)
        pointwise(0)
        pointwise(1)
        pe.wait_ge(yt_ok, 3)
        pe.wait_ge(pw_ok, 4)
        for q, (bank, n, dst) in enumerate(FN):
            jo = q % 2
            kind = q // 2
            if q >= 4:
                pe.wait_ge(fn_ok, FN_DONE[q - 4])
            for j in range(2):
                rhs = (YT[:, j, 0:TP], YT[:, j, TP:TP + 512], YT[:, j, TP + 512:NK], YT[:, j, TP + 1:TP + 512][:, ::-1])[kind]
                last = mm(psum[:, bank, 0:n], wf[:, 1 if kind == 3 else 0, j, jo * P:(jo + 1) * P], rhs, j == 0, j == 1)
            last.then_inc(fn_ps, 1)
        pe.wait_ge(fn_ok, FN_DONE[-1])
        pe.wait_ge(ones_ok, 1)

        def scores(n):
            c, d, t = UNITS[n]
            h, cols = tile_cols(t)
            if n >= 1:
                pe.wait_ge(st_ok, n)
            for hd in range(NH):
                last = mm(psum[:, 0, hd * P:(hd + 1) * P], PT[:, h, KK + hd, cols], PT[:, h, QQ + hd, cols])
            last.then_inc(s_ps, 1)
            if n >= 1:
                pe.wait_ge(kw_ok, NH * n)
            for hd in range(NH):
                last = nc.tensor.transpose(psum[:, 1, hd * P:(hd + 1) * P], PT[:, h, KK + hd, cols], ident[:, :])
            last.then_inc(kt_ps, 1)

        scores(0)
        for n, (c, d, t) in enumerate(UNITS):
            h, cols = tile_cols(t)
            m = before(n)
            if m is None:
                pe.wait_ge(st_in, 64)
                pe.wait_ge(st_zero, 1)
            else:
                pe.wait_ge(c_ok, NH * (m + 1))
            if n >= 1:
                pe.wait_ge(t1_ok, NH * n)
            for hd in range(NH):
                last = mm(psum[:, 4 + hd // 2, (hd % 2) * E1:(hd % 2 + 1) * E1], PT[:, h, QQ + hd, cols], Cst[:, c, hd])
            last.then_inc(inter_ps, 1)
            if n + 1 < NU:
                scores(n + 1)
            pe.wait_ge(st_ok, n + 1)
            if n >= 1:
                pe.wait_ge(num_ok, n)
            for hd in range(NH):
                last = mm(psum[:, 2 + hd // 2, (hd % 2) * E1:(hd % 2 + 1) * E1], St[:, n % 2, hd], vaug[:, t, hd])
            last.then_inc(intra_ps, 1)
            pe.wait_ge(kw_ok, NH * (n + 1))
            if n >= 1:
                pe.wait_ge(c_ok, NH * n)
            for hd in range(NH):
                last = mm(psum[:, 6 + hd // 2, (hd % 2) * E1:(hd % 2 + 1) * E1], kw[:, n % 2, hd], vaug[:, t, hd])
            last.then_inc(u_ps, 1)
        def heads_back(t):
            pe.wait_ge(hn_ok, TILE_Q[t] + 1)
            if t >= 1:
                pe.wait_ge(mix_ok, NH * t)
            for hd in range(NH):
                last = nc.tensor.transpose(psum[:, 7, hd * P:(hd + 1) * P], Hd[:, 1, t, hd * HD:(hd + 1) * HD], ident[:, :])
            last.then_inc(htr_ps, 1)

        def route(t):
            pe.wait_ge(h2_ok, 2 * (t + 1))
            if t >= 1:
                pe.wait_ge(h2T_ok, t)
            for k in range(KD):
                last = nc.tensor.transpose(psum[:, 4 + k // 4, (k % 4) * P:(k % 4 + 1) * P], h2[:, t % 2, k * P:(k + 1) * P],
                                           ident[:, :])
            last.then_inc(h2tr_ps, 1)

        def logits(t):
            pe.wait_ge(h2T_ok, t + 1)
            for k in range(KD):
                last = mm(psum[:, 6 if t < BATCH else 7, t * NE:(t + 1) * NE], h2T[t % 2][:, k], wr[:, k], k == 0, k == KD - 1)
            last.then_inc(lg_ps, 1)

        MIX = (0, 1, 2, 3, QQ, QQ + 1, QQ + 2, QQ + 3)
        pe.wait_ge(c_ok, NH * NU)
        pe.wait_ge(wo_in, 16 * 4)
        for t in range(NT):
            h, cols = tile_cols(t)
            if t >= 2:
                pe.wait_ge(x1_ok, 2 * t - 3)
            for k in range(KD):
                if k == 4 and t == 0:
                    heads_back(0)
                    heads_back(1)
                    pe.wait_ge(wo_in, 16 * KD)
                    pe.wait_ge(tab_in, 48)
                if k == 4:
                    pe.wait_ge(mix_ok, NH * (t + 1))
                for g in range(2):
                    last = mm(psum[:, 2 * (t % 2) + g, :], PT[:, h, MIX[k], cols], wout(k)[:, g * 512:(g + 1) * 512],
                              k == 0, k == KD - 1)
            last.then_inc(o_ps, 1)
            if t + 2 < NT:
                heads_back(t + 2)
            if t >= 1:
                route(t - 1)
            if t >= 2:
                logits(t - 2)
        route(NT - 1)
        logits(NT - 2)
        logits(NT - 1)

        pe.wait_ge(onehot, 1)
        pe.wait_ge(const_ok, 6)
        pe.wait_ge(tab_ok, 2)
        mm(psum[:, 0, 0:NTE], upper, taken, True, False)
        mm(psum[:, 0, 0:NTE], onesd[:, :], cum, False, True)
        mm(psum[:, 1, 0:NE], onesd[:, :], total).then_inc(pos_ps, 1)
        pe.wait_ge(onehot, 2)
        for q in range(2 * NT):
            last = mm(psum[:, 2, 0:2 * NBLK], offhot[:, q], blkhot[:, q], q == 0, q == 2 * NT - 1)
        last.then_inc(tok_ps, 1)

        pe.wait_ge(route_ok, 3)
        pairs = pe.value_load(trip[0:1, 0:1], min_val=1, max_val=NBLK // 2 - 1)

        def x_trans(r, full, read):
            pe.wait_ge(xg_full[r], full)
            if read is not None:
                pe.wait_ge(xt_ok, read)
            for k in range(KD):
                last = nc.tensor.transpose(psum[:, 4 + k // 4, (k % 4) * P:(k % 4 + 1) * P], xg[:, r, k * P:(k + 1) * P], ident[:, :])
            last.then_inc(xt_ps, 1)

        def gate_up(r, blk, have):
            need = pe.value_load(eidI[0:1, blk], min_val=16 * WPART, max_val=16 * WPART * NE)
            off = pe.value_load(offI[0:1, blk], min_val=0, max_val=2 * WE)
            pe.wait_ge(w_full, need)
            pe.wait_ge(xt_ok, have)
            for k in range(KD):
                last = mm(psum[:, r, :], xT[:, r, k], wexp[:, bass.ds(off + k * 2 * FE, 2 * FE)], k == 0, k == KD - 1)
            last.then_inc(gu_ps, 1)
            return off

        def a_trans(r, n):
            pe.wait_ge(a_ok, n)
            for j in range(2):
                last = nc.tensor.transpose(psum[:, 6, j * P:(j + 1) * P], act_a[:, r, j * P:(j + 1) * P], ident[:, :])
            last.then_inc(at_ps, 1)

        def down(r, n, off):
            pe.wait_ge(at_ok, n)
            pe.wait_ge(yb_ok, n)
            for g in range(2):
                for j in range(2):
                    last = mm(psum[:, 2 + g, :], aT[:, r, j], wexp[:, bass.ds(off + (KD * 2 * FE + j * D + g * 512), 512)],
                              j == 0, j == 1)
            last.then_inc(dn_ps, 1)

        x_trans(0, 16, None)
        x_trans(1, 16, 1)
        gate_up(0, slice(0, 1), 1)
        with pe.Fori(0, pairs) as i:
            for j in range(2):
                prev = bass.ds(i * 2 + j, 1)
                a_trans(j, i * 2 + (1 + j))
                x_trans(j, i * 16 + 32, i * 2 + (2 + j))
                gate_up(1 - j, bass.ds(i * 2 + (1 + j), 1), i * 2 + (2 + j))
                off = pe.value_load(offI[0:1, prev], min_val=0, max_val=2 * WE)
                down(j, i * 2 + (1 + j), off)
        a_trans(0, pairs * 2 + 1)
        off = pe.value_load(offI[0:1, bass.ds(pairs * 2, 1)], min_val=0, max_val=2 * WE)
        down(0, pairs * 2 + 1, off)

        pe.wait_ge(diag_ok, 1)
        pe.wait_ge(yb_ok, pairs * 2 + 2)
        for t in range(NT):
            pe.wait_ge(y_in[t % NY], 32 * (t // NY + 1))
            if t >= 2:
                pe.wait_ge(fstep, t - 1)
            for g in range(2):
                for j in range(2):
                    last = mm(psum[:, 2 * (t % 2) + g, :], diag[:, j, t], y12[:, t % NY, j, g * 512:(g + 1) * 512], j == 0, j == 1)
            last.then_inc(comb_ps, 1)

    @block.vector
    def _(dve):
        dve.wait_ge(cols_ps, 1)
        nc.vector.tensor_copy(colv[:, :], psum[:, 7, 0:NROWS1]).then_inc(cols_ok, 1)
        nc.vector.tensor_copy(bada[:, :], psum[:, 7, NROWS1:NROWS1 + ADA_FIRST]).then_inc(cols_ok, 1)
        dve.wait_ge(pos_in, 64)

        def add_pos(t):
            s = t - PT_TILES
            dve.wait_ge(x_in[t], 16)
            dve.wait_ge(posr_ps, s + 1)
            x = xtile(t)
            nc.vector.tensor_tensor(x[:, 0:512], x[:, 0:512], psum[:, 4 + s % 2], ALU.add).then_inc(x_pos, 1)
            nc.vector.tensor_tensor(x[:, 512:D], x[:, 512:D], poscol[:, :], ALU.add).then_inc(x_pos, 1)

        def norm(t):
            dve.wait_ge(rstd_ok, 2 * (t + 1))
            nc.vector.tensor_scalar(xntile(t), xtile(t), ss[:, 2, t:t + 1], None, ALU.mult).then_inc(xn_ok, 1)

        for t in range(PT_TILES, HTILES):
            add_pos(t)
        for t in range(HTILES):
            norm(t)
        for t in range(HTILES, NT):
            add_pos(t)
        for t in range(HTILES, NT):
            norm(t)
        dve.wait_ge(cols_ps, 2)
        dve.wait_ge(cols_ok, 2)
        bb = bada[:, :].unsqueeze(1).broadcast_to([P, 2, ADA_FIRST])
        nc.vector.tensor_tensor(mod[:, :, :], psum[:, 7, 0:2 * ADA_FIRST].rearrange("p (m s) -> p s m", s=2), bb, ALU.add).then_inc(mod_ok, 1)
        dve.wait_ge(mod_ok, 1)
        g1 = colv[:, C_G1:C_G1 + KD].unsqueeze(1).broadcast_to([P, 2, KD])
        nc.vector.tensor_scalar(sc1[:, :, :], mod[:, :, KD:2 * KD], 1.0, None, ALU.add).then_inc(mod_ok, 1)
        dve.wait_ge(mod_ok, 2)
        nc.vector.tensor_tensor(sc1[:, :, :], sc1[:, :, :], g1, ALU.mult).then_inc(mod_ok, 1)

        def split_input(h):
            for k in range(KD):
                g = h * KD + k
                dve.wait_ge(f_ok, 2 * (g + 1))
                if h == 1 and k == 0:
                    dve.wait_ge(cm_ps, NCH)
                nc.vector.tensor_copy(hT[:, 0, k], fbuf[:, k % 2]).then_inc(hT_ok, 1)
                dve.wait_ge(hT_ok, 2 * g + 1)
                nc.vector.tensor_tensor(hT[:, 1, k], fbuf[:, k % 2], hT[:, 0, k].bitcast(F32), ALU.subtract)\
                    .then_inc(hT_ok, 1)

        def taps(wcol, pieces, base):
            m = len(pieces)
            for q, (j, u, out, n) in enumerate(pieces):
                nc.vector.tensor_scalar(out, u[:, 0:n], colv[:, C_WDW + j:C_WDW + j + 1], colv[:, C_BDW + j:C_BDW + j + 1],
                                        ALU.mult, ALU.add).then_inc(conv, 1)
            with dve.Fori(1, TAPS) as i:
                for q, (j, u, out, n) in enumerate(pieces):
                    dve.wait_ge(conv, i * m + (base + q + 1 - m))
                    nc.vector.scalar_tensor_tensor(out, u[:, bass.ds(i, n)], colv[:, bass.ds(i * 2 + (C_WDW + j), 1)], out,
                                                   ALU.mult, ALU.add).then_inc(conv, 1)

        def mix_tile(t):
            h, cols = tile_cols(t)
            dve.wait_ge(htr_ps, t + 1)
            for hd in range(NH):
                nc.vector.scalar_tensor_tensor(PT[:, h, QQ + hd, cols], psum[:, 7, hd * P:(hd + 1) * P],
                                               colv[:, C_GMH + hd:C_GMH + hd + 1], PT[:, h, OO + hd, cols],
                                               ALU.mult, ALU.mult).then_inc(mix_ok, 1)

        split_input(0)
        dve.wait_ge(gt_sig, 1)
        dve.wait_ge(upad_ok, 1)
        nc.vector.tensor_tensor(uprompt[:, :, PAD:PAD + TP], PT[:, 0, CA:CA + 2, 0:TP], PT[:, 0, GT:GT + 2, 0:TP],
                                ALU.mult).then_inc(u_ok, 1)
        dve.wait_ge(u_ok, 1)
        taps(0, [(j, uprompt[:, j], PT[:, 0, CA + j, 0:TP], TP) for j in range(2)], 0)
        split_input(1)
        dve.wait_ge(gt_sig, 2)
        n1 = HT - TP
        nc.vector.memset(usample[:, :, 0:PAD], 0.0).then_inc(u_ok, 1)
        nc.vector.memset(usample[:, :, PAD + TS:], 0.0).then_inc(u_ok, 1)
        nc.vector.tensor_tensor(usample[:, :, PAD:PAD + n1], PT[:, 0, CA:CA + 2, TP:HT], PT[:, 0, GT:GT + 2, TP:HT],
                                ALU.mult).then_inc(u_ok, 1)
        nc.vector.tensor_tensor(usample[:, :, PAD + n1:PAD + TS], PT[:, 1, CA:CA + 2], PT[:, 1, GT:GT + 2],
                                ALU.mult).then_inc(u_ok, 1)
        dve.wait_ge(u_ok, 5)
        taps(0, [p for j in range(2) for p in ((j, usample[:, j], PT[:, 0, CA + j, TP:HT], n1),
                                               (j, usample[:, j, n1:], PT[:, 1, CA + j], HT))], 2 * TAPS)

        for h in range(2):
            dve.wait_ge(mean_ps, h + 1)
            if h == 0:
                dve.wait_ge(conv, CONV_ALL)
            for j in range(2):
                x = PT[:, h, CA + j].rearrange("p (g t) -> p g t", g=2)
                nc.vector.tensor_tensor(x, x, psum[:, 4 + 2 * h:6 + 2 * h, 0:GW], ALU.subtract).then_inc(cen_ok, 1)

        steps = [0]

        def link(ins):
            steps[0] += 1
            ins.then_inc(gstep, 1)
            dve.wait_ge(gstep, steps[0])

        SEQ = ((0, TP), (TP, T))

        dve.wait_ge(cm_ev, NCH + 1)
        dve.wait_ge(gates_ev, 2)
        dve.wait_ge(conv, CONV_ALL)
        link(nc.vector.memset(rowD, 0.0))
        link(nc.vector.memset(rowE, 0.0))
        link(nc.vector.tensor_copy(rowE[0:NH, :], LI[0:NH, :]))
        link(nc.vector.tensor_scalar(rowD[0:NH, :], LF[0:NH, :], gvec[0:NH, 1:2], None, ALU.add))
        bk = slice(32, 32 + NH)
        for c0, c1 in SEQ:
            link(nc.vector.tensor_copy(rowE[bk, c0:c1][:, ::-1], LI[bk, c0:c1]))
            link(nc.vector.tensor_scalar(rowD[bk, c0:c1][:, ::-1], LF[bk, c0:c1], gvec[bk, 1:2], None, ALU.add))
        dve.wait_ge(vtr_ps, 2 * NH)
        link(nc.vector.memset(rowC, 0.0))
        link(nc.vector.scalar_tensor_tensor(rowC, rowD, -1.0, rowD, ALU.mult, ALU.max))
        dve.wait_ge(cm_ps, 2 * NCH)
        link(nc.vector.memset(rowF, 1.0))
        link(nc.vector.memset(rowF[:, 0:T:P], 0.0))
        dve.wait_ge(gact, 2)
        link(nc.vector.scalar_tensor_tensor(rowD, rowD, 0.0, rowC, ALU.min, ALU.subtract))
        link(nc.vector.tensor_tensor_scan(rowC, rowF, rowD, 0.0, ALU.mult, ALU.add))
        link(nc.vector.tensor_tensor_scan(rowG[:, 0:TP], rowD[:, 0:TP], rowE[:, 0:TP], 0.0, ALU.add, ALU.max))
        link(nc.vector.tensor_tensor_scan(rowG[:, TP:T], rowD[:, TP:T], rowE[:, TP:T], gvec[:, 2:3], ALU.add, ALU.max))
        link(nc.vector.tensor_tensor(rowF, rowG, rowC, ALU.subtract))
        link(nc.vector.tensor_tensor(rowE, rowE, rowC, ALU.subtract))
        mprev, mlast, decs, deco = (small[:, i, :] for i in range(4))
        link(nc.vector.memset(mprev[:, 0:1], 0.0))
        link(nc.vector.tensor_copy(mprev[:, 1:2], rowG[:, P - 1:P]))
        link(nc.vector.tensor_copy(mprev[:, PT_TILES:PT_TILES + 1], gvec[:, 2:3]))
        link(nc.vector.tensor_copy(mprev[:, PT_TILES + 1:NT], rowG[:, TP + P - 1:T - 1:P]))
        link(nc.vector.tensor_copy(mlast, rowF[:, P - 1:T:P]))
        link(nc.vector.tensor_tensor(decs, mprev, mlast, ALU.subtract))
        fw = slice(0, NH)
        nc.vector.tensor_scalar(LI[fw, :], rowG[fw, :], -1.0, None, ALU.mult).then_inc(gout, 1)
        nc.vector.tensor_copy(LF[fw, :], rowE[fw, :]).then_inc(gout, 1)
        ch = lambda ap: ap.rearrange("p (c t) -> p c t", t=P)
        per = lambda ap, r, c0, c1: ap[r, c0 // P:c1 // P].unsqueeze(2).broadcast_to([NH, (c1 - c0) // P, P])
        nc.vector.tensor_tensor(ch(rowC[fw, :]), per(mprev, fw, 0, T), ch(rowF[fw, :]), ALU.subtract).then_inc(gout, 1)
        nc.vector.tensor_tensor(ch(rowD[fw, :]), ch(rowE[fw, :]), per(mlast, fw, 0, T), ALU.subtract).then_inc(gout, 1)
        for c0, c1 in SEQ:
            rev = lambda ap: ap[bk, c0:c1][:, ::-1]
            nc.vector.tensor_scalar(rev(LI), rowG[bk, c0:c1], -1.0, None, ALU.mult).then_inc(gout, 1)
            nc.vector.tensor_copy(rev(LF), rowE[bk, c0:c1]).then_inc(gout, 1)
            nc.vector.tensor_tensor(ch(rev(rowC)), per(mprev, bk, c0, c1), ch(rowF[bk, c0:c1]), ALU.subtract).then_inc(gout, 1)
            nc.vector.tensor_tensor(ch(rev(rowD)), ch(rowE[bk, c0:c1]), per(mlast, bk, c0, c1), ALU.subtract).then_inc(gout, 1)
        nc.vector.tensor_copy(deco[fw, :], decs[fw, :]).then_inc(gout, 1)
        nc.vector.tensor_copy(deco[bk, 0:PT_TILES][:, ::-1], decs[bk, 0:PT_TILES]).then_inc(gout, 1)
        nc.vector.tensor_copy(deco[bk, PT_TILES:][:, ::-1], decs[bk, PT_TILES:]).then_inc(gout, 1)
        dve.wait_ge(gout, 15)
        nc.vector.tensor_copy(decs[:, 0:1], rowG[:, TP - 1:TP]).then_inc(gout, 1)
        dve.wait_ge(gout, 16)
        nc.vector.tensor_scalar(rowG[fw, :], rowF[fw, :], -1.0, None, ALU.mult).then_inc(gout, 1)
        for c0, c1 in SEQ:
            nc.vector.tensor_scalar(rowG[bk, c0:c1][:, ::-1], rowF[bk, c0:c1], -1.0, None, ALU.mult).then_inc(gout, 1)

        for h in range(2):
            dve.wait_ge(var_ps, h + 1)
            nc.vector.tensor_scalar(sq[:, 0].rearrange("p (g t) -> p g t", g=2), psum[:, 2 * h:2 * h + 2, 0:GW], EPS, None,
                                    ALU.add).then_inc(var_ok, 1)
            dve.wait_ge(rst_ok, 2 * (h + 1))
            x = PT[:, h, CA:CA + 2]
            nc.vector.tensor_tensor(x, x, sq[:, 1].unsqueeze(1).broadcast_to([P, 2, HT]), ALU.mult).then_inc(scl_ok, 1)

        dve.wait_ge(gcol_ok, 8)
        nc.vector.tensor_scalar(gcol[:, 2], gcol[:, 2], SCALE, None, ALU.mult).then_inc(wcol_ok, 1)

        def decay_logs(n):
            c, d, t = UNITS[n]
            dve.wait_ge(nmb_in[n % 2], 16 * (n // 2 + 1))
            if n >= 2:
                dve.wait_ge(st_ok, n - 1)
            for hd in range(NH):
                nc.vector.scalar_tensor_tensor(Dm[:, n % 2, hd], nmb[:, n % 2, hd], gcol[:, 0, t, d, hd:hd + 1],
                                               (maskf if d == 0 else maskb)[:, :], ALU.add, ALU.min).then_inc(e_ok, 1)

        dve.wait_ge(const_ok, 5)
        dve.wait_ge(ada_used, NADA)
        dve.wait_ge(ct_used, TS // P)
        def decayed_scores(n):
            dve.wait_ge(exp_ok, n + 1)
            dve.wait_ge(s_ps, n + 1)
            if n >= 2:
                dve.wait_ge(intra_ps, n - 1)
            nc.vector.scalar_tensor_tensor(St[:, n % 2], psum[:, 0, :].rearrange("p (h t) -> p h t", h=NH), SCALE, Dm[:, n % 2],
                                           ALU.mult, ALU.mult).then_inc(st_ok, 1)

        decay_logs(0)
        decay_logs(1)
        decayed_scores(0)
        for n, (c, d, t) in enumerate(UNITS):
            if n + 1 < NU:
                decayed_scores(n + 1)
            if n + 2 < NU:
                decay_logs(n + 2)
            dve.wait_ge(u_ps, n + 1)
            if n == 0:
                dve.wait_ge(dec_ok, 1)
            for hd in range(NH):
                nc.vector.scalar_tensor_tensor(Cst[:, c, hd], Cst[:, c, hd], dec[:, d, hd, t:t + 1],
                                               psum[:, 6 + hd // 2, (hd % 2) * E1:(hd % 2 + 1) * E1],
                                               ALU.mult, ALU.add).then_inc(c_ok, 1)
            dve.wait_ge(intra_ps, n + 1)
            dve.wait_ge(t1_ok, NH * (n + 1))
            if n >= 1:
                dve.wait_ge(h_ok, n)
            nc.vector.tensor_tensor(numb[:, :, :].rearrange("p (b h) e -> p b h e", b=2),
                                    t1b[:, n % 2].rearrange("p (b h) e -> p b h e", b=2),
                                    psum[:, 2:4, 0:2 * E1].rearrange("p b (h e) -> p b h e", h=2), ALU.add).then_inc(num_ok, 1)
            dve.wait_ge(num_ok, n + 1)
            den = numb[:, :, HD]
            nc.vector.scalar_tensor_tensor(dens[:, 0], den, -1.0, den, ALU.mult, ALU.max).then_inc(den_ok, 1)
            dve.wait_ge(den_ok, 3 * n + 1)
            nc.vector.tensor_tensor(dens[:, 1], dens[:, 0], gcol[:, 3, t, d], ALU.max).then_inc(den_ok, 1)
            dve.wait_ge(den_ok, 3 * n + 2)
            nc.vector.reciprocal(dens[:, 2], dens[:, 1]).then_inc(den_ok, 1)
            for q in due(n, 3):
                ft = DONE[q][1]
                dve.wait_ge(hrs_ok, 2 * (q + 1))
                nc.vector.tensor_tensor(Hd[:, 1, ft].rearrange("p (h e) -> p h e", h=NH),
                                        Hd[:, 0, ft].rearrange("p (h e) -> p h e", h=NH),
                                        hss[:, 2, ft].unsqueeze(2).broadcast_to([P, NH, HD]), ALU.mult).then_inc(hn_ok, 1)

        dve.wait_ge(so_ok, 2)
        mix_tile(0)
        mix_tile(1)

        rsteps = [0]

        def then(ins):
            rsteps[0] += 1
            ins.then_inc(rstep, 1)
            dve.wait_ge(rstep, rsteps[0])

        te = lambda ap: ap.rearrange("p (t e) -> p t e", e=NE)
        four = lambda w: w.rearrange("p (n i j) -> p n i j", i=EPG, j=EPG)
        grp = lambda ap: ap.rearrange("p (n j) -> p n j", j=EPG)

        def ranks(dst, vals, gt, eq):
            n = vals.shape[1] // EPG
            gt, eq = gt[:, 0:n * EPG * EPG], eq[:, 0:n * EPG * EPG]
            other = grp(vals).unsqueeze(2).broadcast_to([P, n, EPG, EPG])
            self_ = vals.rearrange("p (n i) -> p n i", i=EPG).unsqueeze(3).broadcast_to([P, n, EPG, EPG])
            then(nc.vector.tensor_tensor(four(gt), other, self_, ALU.is_gt))
            then(nc.vector.tensor_tensor(four(eq), other, self_, ALU.is_equal))
            then(nc.vector.tensor_tensor(four(eq), four(eq), ties.unsqueeze(1).broadcast_to([P, n, EPG, EPG]), ALU.mult))
            then(nc.vector.tensor_tensor(four(gt), four(gt), four(eq), ALU.add))
            then(nc.vector.tensor_reduce(dst, grp(gt), AX.X, ALU.add))

        def choose(t0, t1, gt, eq):
            n, e, g = t1 - t0, slice(t0 * NE, t1 * NE), slice(t0 * NGRP, t1 * NGRP)
            then(nc.vector.tensor_tensor(te(selv[:, e]), te(score[:, e]), brow.unsqueeze(1).broadcast_to([P, n, NE]), ALU.add))
            ranks(rank[:, e], selv[:, e], gt, eq)
            then(nc.vector.scalar_tensor_tensor(hot2[:, e], rank[:, e], 2.0, selv[:, e], ALU.is_lt, ALU.mult))
            then(nc.vector.tensor_reduce(gsum[:, g], grp(hot2[:, e]), AX.X, ALU.add))
            ranks(grank[:, g], gsum[:, g], gt, eq)
            then(nc.vector.tensor_scalar(gbest[:, g], grank[:, g], 0.0, None, ALU.is_equal))
            gb4 = gbest[:, g].unsqueeze(2).broadcast_to([P, n * NGRP, EPG])
            for hot, r in ((hot1, 0.0), (hot2, 1.0)):
                then(nc.vector.scalar_tensor_tensor(grp(hot[:, e]), grp(rank[:, e]), r, gb4, ALU.is_equal, ALU.mult))
            then(nc.vector.tensor_tensor(taken[:, e], hot1[:, e], hot2[:, e], ALU.add))
            for t in range(max(t0, 1), t1):
                then(nc.vector.tensor_tensor(cum[:, t * NE:(t + 1) * NE], cum[:, (t - 1) * NE:t * NE],
                                             taken[:, (t - 1) * NE:t * NE], ALU.add))

        dve.wait_ge(conv, 2 * TAPS)
        then(nc.vector.memset(ties, 0.0))
        for i in range(1, EPG):
            then(nc.vector.memset(ties[:, i, 0:i], 1.0))
        dve.wait_ge(c_ok, NH * NU)
        dve.wait_ge(h_ok, NU)
        then(nc.vector.memset(cum[:, 0:NE], 0.0))
        dve.wait_ge(tab_in, 48)

        dve.wait_ge(rows_b, 16 * 7)
        for q in range(2):
            nc.vector.scalar_tensor_tensor(A2[:, q], A2[:, q], 1.0, g2row, ALU.add, ALU.mult).then_inc(ab2_ok, 1)

        def normed(t):
            q = 0 if t < PT_TILES else 1
            dve.wait_ge(rs2_ok, 2 * (t + 1))
            if t == 0:
                dve.wait_ge(ab2_ok, 2)
            if t >= 2:
                dve.wait_ge(h2tr_ps, t - 1)
            nc.vector.scalar_tensor_tensor(h2[:, t % 2], x1[:, t], ss[:, 2, t:t + 1], A2[:, q], ALU.mult, ALU.mult).then_inc(h2_ok, 1)
            dve.wait_ge(h2_ok, 2 * t + 1)
            nc.vector.tensor_tensor(h2[:, t % 2], h2[:, t % 2], B2[:, q], ALU.add).then_inc(h2_ok, 1)

        for t in range(NT):
            q = 0 if t < PT_TILES else 1
            dve.wait_ge(o_ps, t + 1)
            if t == 0:
                dve.wait_ge(hn_ok, NT)
            nc.vector.tensor_tensor(x1[:, t].rearrange("p (b c) -> p b c", b=2), psum[:, 2 * (t % 2):2 * (t % 2) + 2, :],
                                    ga1[:, q].rearrange("p (b c) -> p b c", b=2), ALU.mult).then_inc(x1_ok, 1)
            dve.wait_ge(x1_ok, 2 * t + 1)
            dve.wait_ge(x_in[t], 32)
            nc.vector.tensor_tensor(x1[:, t], x1[:, t], xr[:, t % NX], ALU.add).then_inc(x1_ok, 1)
            normed(t)
            if t + 2 < NT:
                mix_tile(t + 2)
            if t == NT - 2:
                dve.wait_ge(sig_ok, 1)
                choose(0, BATCH, *pairs_a)

        dve.wait_ge(sig_ok, 2)
        choose(BATCH, NT, *pairs_b)
        nc.vector.tensor_tensor(total, cum[:, NTE - NE:NTE], taken[:, NTE - NE:NTE], ALU.add).then_inc(onehot, 1)
        for j, hot in enumerate((hot1, hot2)):
            then(nc.vector.tensor_tensor(tmp16, hot, score, ALU.mult))
            then(nc.vector.tensor_reduce(wtok[:, j], te(tmp16), AX.X, ALU.add))
        then(nc.vector.tensor_tensor(wsum, wtok[:, 0], wtok[:, 1], ALU.add))
        then(nc.vector.reciprocal(wsum, wsum))
        then(nc.vector.tensor_tensor(wtok[:, :, :], wtok[:, :, :], wsum.unsqueeze(1).broadcast_to([P, 2, NT]), ALU.mult))
        dve.wait_ge(pos_ps, 1)
        then(nc.vector.tensor_copy(counts, psum[:, 1, 0:NE]))
        eb = big[:, 0:NE * NT].rearrange("p (e b) -> p e b", b=NT)
        then(nc.vector.tensor_tensor(eb, counts.unsqueeze(2).broadcast_to([P, NE, NT]),
                                     b128[:, 0:NT].unsqueeze(1).broadcast_to([P, NE, NT]), ALU.is_gt))
        then(nc.vector.tensor_reduce(nblk, eb, AX.X, ALU.add))
        then(nc.vector.memset(counts, 1.0))
        then(nc.vector.tensor_tensor_scan(ends, counts, nblk, 0.0, ALU.mult, ALU.add))
        then(nc.vector.tensor_tensor(counts, ends, nblk, ALU.subtract))
        then(nc.vector.tensor_scalar(counts, counts, float(P), None, ALU.mult))
        then(nc.vector.tensor_tensor(te(tmp16), te(psum[:, 0, 0:NT * NE]), counts.unsqueeze(1).broadcast_to([P, NT, NE]), ALU.add))
        for j, hot in enumerate((hot1, hot2)):
            then(nc.vector.tensor_tensor(hot, hot, tmp16, ALU.mult))
            then(nc.vector.tensor_reduce(slotf[:, j * NT:(j + 1) * NT], te(hot), AX.X, ALU.add))
        then(nc.vector.tensor_copy(slotU[:, :, :].rearrange("p j t -> p (j t)"), slotf))
        N2 = 2 * NT
        ge37 = big[:, 0:N2 * 37].rearrange("p (n b) -> p n b", b=37)
        then(nc.vector.tensor_tensor(ge37, slotf.unsqueeze(2).broadcast_to([P, N2, 37]), b128.unsqueeze(1).broadcast_to([P, N2, 37]),
                                     ALU.is_ge))
        then(nc.vector.tensor_reduce(blkf, ge37, AX.X, ALU.add))
        then(nc.vector.tensor_tensor(diff, ge37[:, :, 0:36], ge37[:, :, 1:37], ALU.subtract))
        then(nc.vector.tensor_scalar(blkf, blkf, -float(P), float(P), ALU.mult, ALU.add))
        then(nc.vector.tensor_tensor(slotf, slotf, blkf, ALU.add))
        then(nc.vector.tensor_scalar(blkhot[:, :, 0], diff, tokid[:, 0:1], None, ALU.mult))
        for j in range(2):
            sl = slice(j * NT, (j + 1) * NT)
            then(nc.vector.tensor_tensor(blkhot[:, sl, 1], diff[:, sl], iota[:, 0:NT].unsqueeze(2).broadcast_to([P, NT, NBLK]),
                                         ALU.mult))
        nc.vector.tensor_tensor(offhot, slotf.unsqueeze(2).broadcast_to([P, N2, P]), iota.unsqueeze(1).broadcast_to([P, N2, P]),
                                ALU.is_equal).then_inc(onehot, 1)
        ee = big[:, 0:NBLK * 15].rearrange("p (b e) -> p b e", e=15)
        then(nc.vector.tensor_tensor(ee, ends[:, 0:15].unsqueeze(1).broadcast_to([P, NBLK, 15]),
                                     iota[:, 0:NBLK].unsqueeze(2).broadcast_to([P, NBLK, 15]), ALU.is_le))
        then(nc.vector.tensor_reduce(eidf, ee, AX.X, ALU.add))
        then(nc.vector.tensor_scalar(eidI[:, :], eidf, 16.0 * WPART, 16.0 * WPART, ALU.mult, ALU.add))
        dve.wait_ge(tok_ps, 1)
        then(nc.vector.tensor_copy(eidf, psum[:, 2, 0:NBLK]))
        nc.vector.memset(idxU[:, NBLK:NBLK + 1], 0).then_inc(route_ok, 1)
        nc.vector.scalar_tensor_tensor(idxU[:, 0:NBLK], psum[:, 2, NBLK:2 * NBLK], float(P), eidf, ALU.mult, ALU.add).then_inc(route_ok, 1)
        then(nc.vector.tensor_tensor(ee, ee, mod3[:, 0:15].unsqueeze(1).broadcast_to([P, NBLK, 15]), ALU.mult))
        then(nc.vector.tensor_reduce(eidf, ee, AX.X, ALU.add))
        then(nc.vector.tensor_scalar(offI[:, :], eidf, float(WE), None, ALU.mult))
        then(nc.vector.tensor_scalar(endI[:, :], ends, 1.0, None, ALU.add))
        then(nc.vector.tensor_scalar(eidf[:, 0:17], iota[:, 1:35:2], ends[:, 15:16], None, ALU.is_lt))
        then(nc.vector.tensor_reduce(gsum[:, 0:1], eidf[:, 0:17], AX.X, ALU.add))
        then(nc.vector.tensor_copy(trip[:, :], gsum[:, 0:1]))
        nc.vector.memset(eidf[:, 0:1], 0.0).then_inc(dn_ps, 1)
        nc.vector.memset(wsum, 0.0).then_inc(yb_ok, 1)
        nc.vector.memset(counts, 0.0).then_inc(y_out[0], 16)
        nc.vector.memset(nblk, 0.0).then_inc(y_out[1], 16)
        nc.vector.nop().then_inc(route_ok, 1)

        nc.vector.tensor_tensor(diag.rearrange("p j t q -> p (j t) q"), ident[:, :].unsqueeze(1).broadcast_to([P, 2 * NT, P]),
                                wtok[:, :, :].rearrange("p j t -> p (j t)").unsqueeze(2).broadcast_to([P, 2 * NT, P]),
                                ALU.mult).then_inc(diag_ok, 1)

        pairs = dve.value_load(trip[0:1, 0:1], min_val=1, max_val=NBLK // 2 - 1)

        def product(r, n):
            dve.wait_ge(sg_ok, n)
            nc.vector.tensor_tensor(act_a[:, r], act_g[:, r], psum[:, r, FE:2 * FE], ALU.mult).then_inc(a_ok, 1)

        def a_chan(r, n):
            dve.wait_ge(at_ps, n)
            nc.vector.tensor_copy(aT[:, r].rearrange("p j t -> p (j t)"), psum[:, 6, 0:2 * P]).then_inc(at_ok, 1)

        product(0, 1)
        with dve.Fori(0, pairs) as i:
            for j in range(2):
                a_chan(j, i * 2 + (1 + j))
                product(1 - j, i * 2 + (2 + j))
        a_chan(0, pairs * 2 + 1)

        dve.wait_ge(y_out[0], pairs * 16 + 32)
        dve.wait_ge(y_out[1], pairs * 16 + 16)
        nc.vector.memset(wsum, 0.0).then_inc(y_all, 1)
        dve.wait_ge(rows_c, 48)

        def out_norm(t):
            dve.wait_ge(rs3_ok, 2 * (t + 1))
            if t >= 3:
                dve.wait_ge(ob_out[t % 3], 16 * (t // 3))
            nc.vector.scalar_tensor_tensor(outb[:, t % 3], x2[:, t % 2], ss[:, 2, t:t + 1], fg, ALU.mult, ALU.mult).then_inc(o_ok, 1)

        for t in range(NT):
            q = 0 if t < PT_TILES else 1
            dve.wait_ge(comb_ps, t + 1)
            if t >= 2:
                dve.wait_ge(o_ok, t - 1)
                dve.wait_ge(sq3_ok, t - 1)
            nc.vector.tensor_tensor(x2[:, t % 2].rearrange("p (b c) -> p b c", b=2), psum[:, 2 * (t % 2):2 * (t % 2) + 2, :],
                                    ga2[:, q].rearrange("p (b c) -> p b c", b=2), ALU.mult).then_inc(fstep, 1)
            dve.wait_ge(fstep, t + 1)
            nc.vector.tensor_tensor(x2[:, t % 2], x2[:, t % 2], x1[:, t], ALU.add).then_inc(x2_ok, 1)
            if t >= 1:
                out_norm(t - 1)
        out_norm(NT - 1)

    ctx.close()


def host_arrays(x):
    f = np.float32
    cut = np.ascontiguousarray
    w_in = np.asarray(x["w_in"])[0]
    w_ada = np.asarray(x["w_ada"])[0]

    def chunked(w):
        return cut(w.reshape(KD, P, -1, P).transpose(2, 1, 0, 3))

    gates = np.zeros((D, P), f)
    gb = np.zeros((ROWG, 3), f)
    b_gate = np.asarray(x["b_gate"])[0]
    for d in range(2):
        for kind in range(2):
            src = 2816 + d * 8 + kind * 4
            gates[:, 64 * kind + 32 * d:64 * kind + 32 * d + 4] = w_in[:, src:src + 4]
            gb[32 * d:32 * d + 4, kind] = b_gate[d * 8 + kind * 4:d * 8 + kind * 4 + 4]
        gb[32 * d:32 * d + 4, 2] = np.asarray(x["state_m"])[0, 0, d]
    arrays = {
        "w_ada": chunked(w_ada),
        "w_in": chunked(np.concatenate([gates, w_in[:, :2816]], axis=1)),
        "gvec": gb,
        "rows1": cut(np.concatenate([
            np.asarray(x[n]).reshape(-1, P) for n in
            ("c_ctx", "c", "norm1_g", "b_dw", "conv_ln_g", "conv_ln_b", "g_mh", "w_dw")])),
        "rows2": cut(np.asarray(x["b_ada"]).reshape(-1, P)[:ADA_FIRST]),
        "x_prompt": np.asarray(x["x_prompt"])[0],
        "x_sample": np.asarray(x["x_sample"])[0],
    }
    rest = np.asarray(x["b_ada"]).reshape(-1, P)[ADA_FIRST:]
    arrays["b_ada64"] = cut(np.concatenate([rest[0:14], rest[28:32]]).reshape(-1))
    arrays["b_ada96"] = cut(rest[14:28].reshape(-1))
    quarter = D // 4
    omega = (1.0 / (f(10000.0) ** (np.arange(quarter, dtype=f) / f(quarter)))).astype(f)

    def enc(n):
        ang = (np.arange(n, dtype=f)[:, None] * omega[None, :]).astype(f)
        return np.concatenate([np.sin(ang), np.cos(ang)], axis=-1).astype(f)

    arrays["postab"] = enc(TS // GRID_W)
    arrays["poscol"] = cut(np.tile(enc(GRID_W), (P // GRID_W, 1)))
    def angles(n, rows, cols):
        return 2 * np.pi * ((rows[:, None] * cols[None, :]) % n) / n

    ch = angles(64, np.arange(64), np.arange(64))
    bd = np.zeros((P, 2, P), f)
    for i in range(2):
        bd[64 * i:64 * i + 64, 0, 64 * i:64 * i + 64] = np.cos(ch) / 8
        bd[64 * i:64 * i + 64, 1, 64 * i:64 * i + 64] = np.sin(ch) / 8
    arrays["bdcs"] = bd.reshape(P, 2 * P)
    an = angles(TP, np.arange(TP), np.arange(TP))
    arrays["ctp"] = cut(np.stack([np.cos(an), -np.sin(an)], 1).astype(f).reshape(2, P, 2, TP).transpose(1, 0, 2, 3) / f(16))
    an = angles(TS, np.arange(TS), np.arange(TS // 2))
    arrays["cts"] = cut(np.stack([np.cos(an), -np.sin(an)], 1).astype(f).reshape(TS // P, P, 2, TS // 2) / f(32))
    arrays["alt"] = (((-1.0) ** np.arange(P)) / 32).astype(f)[:, None]
    wfn = np.asarray(x["w_fnet"])[0]
    neg = np.array([(c // 64) * 64 + (-c) % 64 for c in range(256)])
    arrays["wf"] = cut(np.stack([wfn, wfn[neg]]).reshape(2, 2, P, 256).transpose(2, 0, 1, 3))
    arrays["wpw"] = cut(np.asarray(x["w_pw"])[0].reshape(2, P, 256).transpose(1, 0, 2))
    arrays["state_C"] = np.asarray(x["state_C"])[0, 0]
    arrays["state_n"] = np.asarray(x["state_n"])[0, 0]
    sel = np.zeros((16, TS // P, P), f)
    for i in range(TS // P):
        for p in range(P):
            sel[i * 2 + p // GRID_W, i, p] = 1.0
    arrays["possel"] = sel
    arrays["w_out"] = np.asarray(x["w_out"])[0].reshape(KD, P, D)
    arrays["norm2_g"] = np.asarray(x["norm2_g"])[0]
    arrays["final_g"] = np.asarray(x["final_g"])
    arrays["w_router"] = cut(np.asarray(x["w_router"]).reshape(KD, P, NE).transpose(1, 0, 2))
    arrays["tables"] = np.concatenate([[-1.0], np.arange(1, 37) * 128.0, np.where(np.arange(NE) % 3 == 2, -2.0, 1.0), np.asarray(x["b_router"]),
                                       np.arange(P)]).astype(f)
    arrays["tokid"] = cut(np.arange(T, dtype=f).reshape(NT, P).T)
    wg, wu, wd = (np.asarray(x[n])[0] for n in ("w_exp_gate", "w_exp_up", "w_exp_down"))
    gu = np.concatenate([wg, wu], axis=2).reshape(NE, KD, P, 2 * FE).transpose(0, 2, 1, 3).reshape(NE, P, -1)
    arrays["w_exp"] = cut(np.concatenate([gu, wd.reshape(NE, 2, P, D).transpose(0, 2, 1, 3).reshape(NE, P, -1)], axis=2))
    return {f"in_{n}": v for n, v in arrays.items()}


OUTS = [((1, TP, D), "float32"), ((1, TS, D), "float32"), ((1, 1, 2, NH, HD, HD), "float32"),
        ((1, 1, 2, NH, HD), "float32"), ((1, 1, 2, NH), "float32")]


def kernel(**inputs):
    from concourse import bacc
    from concourse.bass_utils import run_bass_kernel_spmd

    nc = bacc.Bacc("TRN2", target_bir_lowering=False, num_devices=1)
    arrays = host_arrays(inputs)
    a = {n[3:]: nc.dram_tensor(n, v.shape, mybir.dt.from_np(v.dtype), kind="ExternalInput").ap() for n, v in arrays.items()}
    o = [nc.dram_tensor(f"out_{i}", s, mybir.dt.from_np(np.dtype(d)), kind="ExternalOutput").ap()
         for i, (s, d) in enumerate(OUTS)]
    program(nc, a, o)
    r = run_bass_kernel_spmd(nc, [arrays], core_ids=[0])
    return tuple(r.results[0][f"out_{i}"] for i in range(len(OUTS)))
```
